# Optimizing a Trainium2 kernel written in Bass

```python
import jax, jax.numpy as jnp
from jax import lax
import numpy as np

D_MODEL = 1024
BATCH = 1
SEQ = 1024
DEPTH = 1
DEC_BATCH = 8
DEC_SEQ = 8
PAST_LEN = 2048
PAGE_SIZE = 128

HEAD_DIM = 64
MIX_WIDTH = D_MODEL
RET_HEADS = MIX_WIDTH // 2 // HEAD_DIM
SWA_HEADS = MIX_WIDTH // 2 // HEAD_DIM
SWA_KV_HEADS = 2
SWA_GROUP = SWA_HEADS // SWA_KV_HEADS
WINDOW = 128
SWA_BLOCK = WINDOW
RET_CHUNK = 128
D_FF = ((8 * D_MODEL // 3 + 127) // 128) * 128
RET_W = RET_HEADS * HEAD_DIM
SWA_W = SWA_HEADS * HEAD_DIM
KV_W = SWA_KV_HEADS * HEAD_DIM
IN_COLS = 4 * RET_W + SWA_W + 2 * KV_W
LN_EPS = 1e-5
GN_EPS = 1e-5
DN_ALPHA = (2.0 * DEPTH) ** 0.25
DN_BETA = (8.0 * DEPTH) ** -0.25

kernel_name = "hymba_retention_swa_sink_macaron_deepnorm_step"

def _layer_norm(x, g, b):
    xf = x.astype(jnp.float32)
    mu = jnp.mean(xf, axis=-1, keepdims=True)
    var = jnp.mean(jnp.square(xf - mu), axis=-1, keepdims=True)
    return ((xf - mu) * lax.rsqrt(var + LN_EPS) * g.astype(jnp.float32) + b.astype(jnp.float32)).astype(x.dtype)

def _swiglu(x, w_gate, w_up, w_down):
    return (jax.nn.silu(x @ w_gate) * (x @ w_up)) @ w_down

def _project_in(h, w_in):
    B, S = h.shape[:2]
    proj = h @ w_in
    cuts = [RET_W, 2 * RET_W, 3 * RET_W, 4 * RET_W, 4 * RET_W + SWA_W, 4 * RET_W + SWA_W + KV_W]
    rq, rk, rv, rg, sq, sk, sv = jnp.split(proj, cuts, axis=-1)
    heads = lambda t, n: t.reshape(B, S, n, HEAD_DIM)
    return (heads(rq, RET_HEADS), heads(rk, RET_HEADS), heads(rv, RET_HEADS), rg,
            heads(sq, SWA_HEADS), heads(sk, SWA_KV_HEADS), heads(sv, SWA_KV_HEADS))

def _retention(q, k, v, s0, chunk):
    B, S = q.shape[:2]
    nc = S // chunk
    shp = (B, nc, chunk, RET_HEADS, HEAD_DIM)
    qf = q.astype(jnp.float32).reshape(shp)
    kf = (k.astype(jnp.float32) * HEAD_DIM ** -0.5).reshape(shp)
    vf = v.astype(jnp.float32).reshape(shp)
    log_g = jnp.log1p(-jnp.exp2(-5.0 - jnp.arange(RET_HEADS, dtype=jnp.float32)))
    idx = jnp.arange(chunk, dtype=jnp.float32)
    diff = idx[:, None] - idx[None, :]
    causal = diff >= 0
    dmask = jnp.where(causal[None], jnp.exp(jnp.where(causal, diff, 0.0)[None] * log_g[:, None, None]), 0.0)
    scores = jnp.einsum('bnihd,bnjhd->bnhij', qf, kf) * dmask
    intra = jnp.einsum('bnhij,bnjhe->bnihe', scores, vf)
    k_w = jnp.exp((chunk - 1.0 - idx)[:, None] * log_g[None, :])
    kv = jnp.einsum('bnjhd,bnjhe->nbhde', kf * k_w[:, :, None], vf)
    g_c = jnp.exp(chunk * log_g)[None, :, None, None]

    def step(s, kv_n):
        return g_c * s + kv_n, s

    s_final, s_start = lax.scan(step, s0, kv)
    q_w = jnp.exp((idx + 1.0)[:, None] * log_g[None, :])
    inter = jnp.einsum('bnihd,nbhde->bnihe', qf * q_w[:, :, None], s_start)
    return (intra + inter).reshape(B, S, RET_HEADS, HEAD_DIM), s_final

def _head_group_norm(o, gain):
    mu = jnp.mean(o, axis=-1, keepdims=True)
    var = jnp.mean(jnp.square(o - mu), axis=-1, keepdims=True)
    y = (o - mu) * lax.rsqrt(var + GN_EPS)
    return y.reshape(o.shape[:2] + (RET_W,)) * gain.astype(jnp.float32)

def _sink_attention(q, k, v, dist, valid, sinks):
    qg = q.astype(jnp.float32).reshape(q.shape[:-2] + (SWA_KV_HEADS, SWA_GROUP, HEAD_DIM))
    s = jnp.einsum('...qngd,...knd->...ngqk', qg, k.astype(jnp.float32)) * HEAD_DIM ** -0.5
    slopes = jnp.exp2(-8.0 / SWA_HEADS * jnp.arange(1, SWA_HEADS + 1, dtype=jnp.float32))
    s = s - slopes.reshape(SWA_KV_HEADS, SWA_GROUP, 1, 1) * dist
    s = jnp.where(valid, s, -jnp.inf)
    sink = sinks.astype(jnp.float32).reshape(SWA_KV_HEADS, SWA_GROUP, 1)
    m = jnp.maximum(jnp.max(s, axis=-1), sink)
    p = jnp.exp(s - m[..., None])
    denom = jnp.sum(p, axis=-1) + jnp.exp(sink - m)
    o = jnp.einsum('...ngqk,...knd->...qngd', p / denom[..., None], v.astype(jnp.float32))
    return o.reshape(q.shape[:-2] + (SWA_HEADS, HEAD_DIM))

def _swa_prompt(q, k, v, sinks):
    B, S = q.shape[:2]
    nb = S // SWA_BLOCK
    qb = q.reshape(B, nb, SWA_BLOCK, SWA_HEADS, HEAD_DIM)
    kb = k.reshape(B, nb, SWA_BLOCK, SWA_KV_HEADS, HEAD_DIM)
    vb = v.reshape(B, nb, SWA_BLOCK, SWA_KV_HEADS, HEAD_DIM)
    shift = lambda t: jnp.concatenate([jnp.zeros_like(t[:, :1]), t[:, :-1]], axis=1)
    kk = jnp.concatenate([shift(kb), kb], axis=2)
    vv = jnp.concatenate([shift(vb), vb], axis=2)
    i = jnp.arange(SWA_BLOCK)
    j = jnp.arange(2 * SWA_BLOCK)
    dist = i[:, None] + SWA_BLOCK - j[None, :]
    within = (dist >= 0) & (dist <= WINDOW)
    has_prev = jnp.arange(nb) > 0
    valid = within[None] & (has_prev[:, None, None] | (j >= SWA_BLOCK)[None, None, :])
    o = _sink_attention(qb, kk, vv, dist.astype(jnp.float32), valid[:, None, None], sinks)
    return o.reshape(B, S, SWA_HEADS, HEAD_DIM)

def _swa_sample(q, k, v, k_buf, v_buf, sinks):
    T = q.shape[1]
    kk = jnp.concatenate([k_buf.astype(k.dtype), k], axis=1)
    vv = jnp.concatenate([v_buf.astype(v.dtype), v], axis=1)
    i = jnp.arange(T)
    j = jnp.arange(WINDOW + T)
    dist = i[:, None] + WINDOW - j[None, :]
    valid = (dist >= 0) & (dist <= WINDOW)
    o = _sink_attention(q, kk, vv, dist.astype(jnp.float32), valid, sinks)
    return o, kk[:, T:], vv[:, T:]

def _mixer(h, w_in, w_out, gn_w, sinks, ret_state=None, k_buf=None, v_buf=None):
    B, S = h.shape[:2]
    rq, rk, rv, rg, sq, sk, sv = _project_in(h, w_in)
    if ret_state is None:
        s0 = jnp.zeros((B, RET_HEADS, HEAD_DIM, HEAD_DIM), jnp.float32)
        o_ret, s_new = _retention(rq, rk, rv, s0, RET_CHUNK)
        o_swa = _swa_prompt(sq, sk, sv, sinks)
        new_k, new_v = sk[:, -WINDOW:], sv[:, -WINDOW:]
    else:
        o_ret, s_new = _retention(rq, rk, rv, ret_state.astype(jnp.float32), S)
        o_swa, new_k, new_v = _swa_sample(sq, sk, sv, k_buf, v_buf, sinks)
    y_ret = jax.nn.silu(rg.astype(jnp.float32)) * _head_group_norm(o_ret, gn_w)
    merged = jnp.concatenate([y_ret, o_swa.reshape(B, S, SWA_W)], axis=-1).astype(h.dtype)
    return merged @ w_out, s_new.astype(h.dtype), new_k, new_v

def _decoder_layer(x, ln_g, ln_b, w_in, gn_w, sinks, w_out, f1g, f1u, f1d, f2g, f2u, f2d,
                   ret_state=None, k_buf=None, v_buf=None):
    x = _layer_norm(DN_ALPHA * x + 0.5 * _swiglu(x, f1g, f1u, f1d), ln_g[0], ln_b[0])
    m, s_new, new_k, new_v = _mixer(x, w_in, w_out, gn_w, sinks, ret_state, k_buf, v_buf)
    x = _layer_norm(DN_ALPHA * x + m, ln_g[1], ln_b[1])
    x = _layer_norm(DN_ALPHA * x + 0.5 * _swiglu(x, f2g, f2u, f2d), ln_g[2], ln_b[2])
    return x, s_new, new_k, new_v

def setup_inputs(seed: int = 0) -> dict:
    key = jax.random.key(seed)
    ks = jax.random.split(key, 18)
    n = lambda i, shape: jax.random.normal(ks[i], shape, jnp.float32)
    return {
        "x_prompt": n(0, (BATCH, SEQ, D_MODEL)),
        "x_sample": n(1, (DEC_BATCH, DEC_SEQ, D_MODEL)),
        "state_ret": 0.5 * n(2, (DEPTH, DEC_BATCH, RET_HEADS, HEAD_DIM, HEAD_DIM)),
        "cache_swa_k": n(3, (DEPTH, DEC_BATCH, WINDOW, SWA_KV_HEADS, HEAD_DIM)),
        "cache_swa_v": n(4, (DEPTH, DEC_BATCH, WINDOW, SWA_KV_HEADS, HEAD_DIM)),
        "ln_gain": 1.0 + 0.02 * n(5, (DEPTH, 3, D_MODEL)),
        "ln_bias": 0.02 * n(6, (DEPTH, 3, D_MODEL)),
        "w_in": n(7, (DEPTH, D_MODEL, IN_COLS)) * D_MODEL ** -0.5,
        "ret_gn_w": 1.0 + 0.02 * n(8, (DEPTH, RET_W)),
        "swa_sinks": 0.5 * n(9, (DEPTH, SWA_HEADS)),
        "w_out": n(10, (DEPTH, MIX_WIDTH, D_MODEL)) * (MIX_WIDTH ** -0.5 * DN_BETA),
        "ffn1_gate": n(11, (DEPTH, D_MODEL, D_FF)) * D_MODEL ** -0.5,
        "ffn1_up": n(12, (DEPTH, D_MODEL, D_FF)) * D_MODEL ** -0.5,
        "ffn1_down": n(13, (DEPTH, D_FF, D_MODEL)) * (D_FF ** -0.5 * DN_BETA),
        "ffn2_gate": n(14, (DEPTH, D_MODEL, D_FF)) * D_MODEL ** -0.5,
        "ffn2_up": n(15, (DEPTH, D_MODEL, D_FF)) * D_MODEL ** -0.5,
        "ffn2_down": n(16, (DEPTH, D_FF, D_MODEL)) * (D_FF ** -0.5 * DN_BETA),
    }

def reference(x_prompt, x_sample, state_ret, cache_swa_k, cache_swa_v, ln_gain, ln_bias, w_in,
              ret_gn_w, swa_sinks, w_out, ffn1_gate, ffn1_up, ffn1_down, ffn2_gate, ffn2_up, ffn2_down):
    yp, ys = x_prompt, x_sample
    sp_list, kp_list, vp_list, ss_list, ks_list, vs_list = [], [], [], [], [], []
    for l in range(DEPTH):
        params = (ln_gain[l], ln_bias[l], w_in[l], ret_gn_w[l], swa_sinks[l], w_out[l],
                  ffn1_gate[l], ffn1_up[l], ffn1_down[l], ffn2_gate[l], ffn2_up[l], ffn2_down[l])
        yp, sp, kp, vp = _decoder_layer(yp, *params)
        ys, s_s, k_s, v_s = _decoder_layer(ys, *params, ret_state=state_ret[l],
                                           k_buf=cache_swa_k[l], v_buf=cache_swa_v[l])
        sp_list.append(sp); kp_list.append(kp); vp_list.append(vp)
        ss_list.append(s_s); ks_list.append(k_s); vs_list.append(v_s)
    state_ret_prompt = jnp.stack(sp_list, axis=0)
    cache_swa_k_prompt = jnp.stack(kp_list, axis=0)
    cache_swa_v_prompt = jnp.stack(vp_list, axis=0)
    state_ret_sample = jnp.stack(ss_list, axis=0)
    cache_swa_k_sample = jnp.stack(ks_list, axis=0)
    cache_swa_v_sample = jnp.stack(vs_list, axis=0)
    return (yp, ys, state_ret_prompt, cache_swa_k_prompt, cache_swa_v_prompt,
            state_ret_sample, cache_swa_k_sample, cache_swa_v_sample)


_drawn_inputs = setup_inputs


def setup_inputs(seed=0):
    import zlib

    import numpy as np

    out = dict(_drawn_inputs(seed))
    spreads = {}
    factors = {'ret_gn_w': 8.0, 'swa_sinks': 7.676}
    for name, (base, spread) in spreads.items():
        noise = np.random.default_rng([zlib.crc32(name.encode()), seed]).standard_normal(out[name].shape)
        drawn = base * np.exp(spread * noise) if base else spread * noise
        out[name] = __import__('jax').numpy.asarray(drawn.astype(out[name].dtype))
    for name, factor in factors.items():
        out[name] = (out[name] * factor).astype(out[name].dtype)
    return out
```

```python
import math
from contextlib import ExitStack

import numpy as np

import concourse.bass as bass
from concourse import mybir

F32 = mybir.dt.float32
F32R = mybir.dt.float32r
ACT = mybir.ActivationFunctionType
ALU = mybir.AluOpType
AX = mybir.AxisListType

P = 128
D_MODEL = 1024
D_FF = 2816
KT = D_MODEL // P
FT = D_FF // P
SEQ = 1024
DEC_BATCH, DEC_SEQ = 8, 8
DEC = DEC_BATCH * DEC_SEQ
TOK = SEQ + DEC
HEADS, HD = 8, 64
PAIRS = HEADS // 2
KVH = 2
GROUP = HEADS // KVH
WINDOW = 128
BLOCKS = SEQ // P
EPS = 1e-5
ALPHA = 2.0 ** 0.25
QSCALE = HD ** -0.5
MASKED = -1e30

CHUNKS = [(0, 362), (362, 726), (726, TOK)]
CW = max(b - a for a, b in CHUNKS)

RET, SWA = 0, 1


class Layout:

    def __init__(self, nc, at):
        self.nc, self.at = nc, at

    def put(self, name, shape, dtype=F32):
        t = self.nc.alloc_sbuf_tensor_at(name, shape, dtype, offset=self.at)
        self.at += -(-int(np.prod(shape[1:])) * 4 // 32) * 32
        return t


def three_passes(pe, out, weights, moving, first, last):
    (wh, wl), (xh, xl) = weights, moving
    pe.matmul(out, wh, xh, start=first, stop=False)
    pe.matmul(out, wh, xl, start=False, stop=False)
    return pe.matmul(out, wl, xh, start=False, stop=last)


def load_phase(nc, x_in, small_in, small, ones_mean, ones_head, eps, acc, xh, xl):
    with ExitStack() as ctx:
        sem = lambda n: ctx.enter_context(nc.semaphore("load_" + n))
        x_loaded = [sem(f"x_loaded{h}") for h in range(2)]
        small_loaded, hi_done, lo_done, scaled, filled = map(
            sem, ("small_loaded", "hi_done", "lo_done", "scaled", "filled"))
        halves = [slice(0, KT // 2), slice(KT // 2, KT)]
        with nc.Block() as block:

            @block.sync
            def _(sp):
                sp.dma_start(acc[:, halves[0], :], x_in[:, halves[0], :]).then_inc(x_loaded[0], 16)
                sp.dma_start(acc[:, halves[1], :], x_in[:, halves[1], :]).then_inc(x_loaded[1], 16)
                sp.dma_start(small[:, :], small_in).then_inc(small_loaded, 16)
                sp.wait_ge(small_loaded, 16)

            @block.gpsimd
            def _(pool):
                pool.memset(ones_mean[:, :], 1.0 / D_MODEL).then_inc(filled, 1)
                pool.memset(ones_head[:, :], 0.0).then_inc(filled, 1)
                pool.memset(eps[:, :], EPS).then_inc(filled, 1)
                pool.wait_ge(filled, 3)
                for h in range(2):
                    d = slice(HD * h, HD * h + HD)
                    pool.memset(ones_head[d, d], 1.0 / HD).then_inc(filled, 1)

            @block.scalar
            def _(act):
                for h in range(2):
                    act.wait_ge(x_loaded[h], 16)
                    act.activation(xh[:, halves[h], :], acc[:, halves[h], :], ACT.Copy).then_inc(hi_done, 1)

            @block.vector
            def _(dve):
                for h in range(2):
                    dve.wait_ge(hi_done, h + 1)
                    dve.tensor_tensor(xl[:, halves[h], :], acc[:, halves[h], :],
                                      xh[:, halves[h], :].bitcast(F32), ALU.subtract).then_inc(lo_done, 1)
                    dve.wait_ge(lo_done, h + 1)
                    dve.tensor_scalar(acc[:, halves[h], :], acc[:, halves[h], :], 2 * ALPHA, None,
                                      ALU.mult).then_inc(scaled, 1)


def ffn_phase(nc, tag, at, w_in, acc, xh, xl):
    m = Layout(nc, at)
    stage = m.put(tag + "stage", [P, 3, D_MODEL])
    w_hi = [[m.put(f"{tag}w_hi{s}{j}", [P, KT, P], F32R) for j in range(3)] for s in range(2)]
    w_lo = [[m.put(f"{tag}w_lo{s}{j}", [P, KT, P], F32R) for j in range(3)] for s in range(2)]
    h_hi = [m.put(f"{tag}h_hi{s}", [P, TOK], F32R) for s in range(2)]
    h_lo = [m.put(f"{tag}h_lo{s}", [P, TOK], F32R) for s in range(2)]
    silu = m.put(tag + "silu", [P, 3, CW])
    h_full = m.put(tag + "h_full", [P, 3, CW])
    GATE, UP, DOWN = range(3)
    NC_ = len(CHUNKS)
    DOWNS = KT * NC_
    with ExitStack() as ctx:
        sem = lambda n: ctx.enter_context(nc.semaphore(tag + n))
        bank = lambda n: ctx.enter_context(nc.psum_tensor(tag + n, [P, 512], F32))
        gate_ps = [bank(f"gate_ps{i}") for i in range(2)]
        up_ps = [bank(f"up_ps{i}") for i in range(2)]
        down_ps = [bank(f"down_ps{i}") for i in range(4)]
        staged = [sem(f"staged{j}") for j in range(3)]
        hi_done = sem("hi_done")
        gu_split = sem("gu_split")
        down_split = sem("down_split")
        gate_done, up_done = sem("gate_done"), sem("up_done")
        silu_done = sem("silu_done")
        pair_free = sem("pair_free")
        h_hi_done, h_lo_done = sem("h_hi_done"), sem("h_lo_done")
        down_done = sem("down_done")
        down_free = sem("down_free")

        def tiles(eng, step):
            with eng.Fori(0, (FT - 2) // 2) as i:
                step(2 * i + 1, 1)
                step(2 * i + 2, 0)
            step(FT - 1, 1)

        def pair_of(s, c):
            return (3 * s + c) % 2

        with nc.Block() as block:

            @block.sync
            def _(sp):
                def load(f, j):
                    sp.dma_start(stage[:, j, :], w_in[f, :, j, :]).then_inc(staged[j], 16)

                for j in range(3):
                    load(0, j)
                with sp.Fori(1, FT) as f:
                    for j in (GATE, UP):
                        sp.wait_ge(gu_split, 2 * f - 1 + j)
                        sp.dma_start(stage[:, j, :], w_in[bass.ds(f, 1), :, j, :].rearrange("a p n -> (a p) n")).then_inc(staged[j], 16)
                    sp.wait_ge(down_split, f)
                    sp.dma_start(stage[:, DOWN, :], w_in[bass.ds(f, 1), :, DOWN, :].rearrange("a p n -> (a p) n")).then_inc(staged[DOWN], 16)

            @block.scalar
            def _(act):
                def round_part(f, s, j):
                    act.wait_ge(staged[j], 16 * f + 16)
                    act.activation(w_hi[s][j][:, :, :].rearrange("p k n -> p (k n)"), stage[:, j, :],
                                   ACT.Copy).then_inc(hi_done, 1)

                def silu_chunk(f, s, c):
                    a, b = CHUNKS[c]
                    act.wait_ge(gate_done, 3 * f + c + 1)
                    act.activation(silu[:, c, 0:b - a], gate_ps[pair_of(s, c)][:, 0:b - a],
                                   ACT.Silu).then_inc(silu_done, 1)

                def round_h(f, s, c):
                    a, b = CHUNKS[c]
                    act.wait_ge(pair_free, 2 + 3 * f + c + 1)
                    act.activation(h_hi[s][:, a:b], h_full[:, c, 0:b - a], ACT.Copy).then_inc(h_hi_done, 1)

                def step(f, s, more=True):
                    if more:
                        if not (isinstance(f, int) and f == 0):
                            act.wait_ge(up_done, 3 * f)
                        round_part(f + 1, 1 - s, GATE)
                        round_part(f + 1, 1 - s, UP)
                    silu_chunk(f, s, 0)
                    silu_chunk(f, s, 1)
                    round_h(f, s, 0)
                    silu_chunk(f, s, 2)
                    round_h(f, s, 1)
                    round_h(f, s, 2)
                    if more:
                        if not (isinstance(f, int) and f == 0):
                            act.wait_ge(down_done, DOWNS * f)
                        round_part(f + 1, 1 - s, DOWN)

                for j in range(3):
                    round_part(0, 0, j)
                step(0, 0)
                with act.Fori(0, (FT - 2) // 2) as i:
                    step(2 * i + 1, 1)
                    step(2 * i + 2, 0)
                step(FT - 1, 1, more=False)

            @block.gpsimd
            def _(pool):
                def split(f, s):
                    for j, done in ((GATE, gu_split), (UP, gu_split), (DOWN, down_split)):
                        pool.wait_ge(hi_done, 3 * f + j + 1)
                        pool.tensor_tensor(w_lo[s][j][:, :, :].rearrange("p k n -> p (k n)"), stage[:, j, :],
                                           w_hi[s][j][:, :, :].rearrange("p k n -> p (k n)").bitcast(F32),
                                           ALU.subtract).then_inc(done, 1)

                split(0, 0)
                with pool.Fori(0, (FT - 2) // 2) as i:
                    split(2 * i + 1, 1)
                    split(2 * i + 2, 0)
                split(FT - 1, 1)

            @block.tensor
            def _(pe):
                def gate_up(f, s):
                    for c, (a, b) in enumerate(CHUNKS):
                        pair = pair_of(s, c)
                        pe.wait_ge(pair_free, 3 * f + c + 1)
                        for j, ps, done in ((GATE, gate_ps, gate_done), (UP, up_ps, up_done)):
                            if c == 0:
                                pe.wait_ge(gu_split, 2 * f + j + 1)
                            for k in range(KT):
                                mm = three_passes(pe, ps[pair][:, 0:b - a],
                                                  (w_hi[s][j][:, k, :], w_lo[s][j][:, k, :]),
                                                  (xh[:, k, a:b], xl[:, k, a:b]), k == 0, k == KT - 1)
                            mm.then_inc(done, 1)

                def down(f, s):
                    pe.wait_ge(down_split, f + 1)
                    n = 0
                    for d in range(KT):
                        for c, (a, b) in enumerate(CHUNKS):
                            if d == 0:
                                pe.wait_ge(h_lo_done, 3 * f + c + 1)
                            pe.wait_ge(down_free, DOWNS * f + n + 1 + DOWNS - 4)
                            three_passes(pe, down_ps[n % 4][:, 0:b - a],
                                         (w_hi[s][DOWN][:, d, :], w_lo[s][DOWN][:, d, :]),
                                         (h_hi[s][:, a:b], h_lo[s][:, a:b]), True, True).then_inc(down_done, 1)
                            n += 1

                def step(f, s):
                    gate_up(f, s)
                    down(f - 1, 1 - s)

                gate_up(0, 0)
                tiles(pe, step)
                down(FT - 1, 1)

            @block.vector
            def _(dve):
                dve.sem_inc(pair_free, 2)
                dve.sem_inc(down_free, DOWNS)

                def h_chunk(f, s, c):
                    a, b = CHUNKS[c]
                    if not (isinstance(f, int) and f == 0):
                        dve.wait_ge(h_lo_done, 3 * f + c - 2)
                    dve.wait_ge(silu_done, 3 * f + c + 1)
                    dve.wait_ge(up_done, 3 * f + c + 1)
                    dve.tensor_tensor(h_full[:, c, 0:b - a], up_ps[pair_of(s, c)][:, 0:b - a],
                                      silu[:, c, 0:b - a], ALU.mult).then_inc(pair_free, 1)

                def split_h(f, s, c):
                    a, b = CHUNKS[c]
                    dve.wait_ge(h_hi_done, 3 * f + c + 1)
                    dve.tensor_tensor(h_lo[s][:, a:b], h_full[:, c, 0:b - a],
                                      h_hi[s][:, a:b].bitcast(F32), ALU.subtract).then_inc(h_lo_done, 1)

                def h_tile(f, s):
                    h_chunk(f, s, 0)
                    h_chunk(f, s, 1)
                    split_h(f, s, 0)
                    h_chunk(f, s, 2)
                    split_h(f, s, 1)
                    split_h(f, s, 2)

                def add_down(f):
                    n = 0
                    for d in range(KT):
                        for a, b in CHUNKS:
                            dve.wait_ge(down_free, DOWNS * f + n + 1)
                            dve.wait_ge(down_done, DOWNS * f + n + 1)
                            dve.tensor_tensor(acc[:, d, a:b], down_ps[n % 4][:, 0:b - a], acc[:, d, a:b],
                                              ALU.add).then_inc(down_free, 1)
                            n += 1

                def step(f, s):
                    h_tile(f, s)
                    add_down(f - 1)

                h_tile(0, 0)
                tiles(dve, step)
                add_down(FT - 1)


def norm_phase(nc, tag, at, scale, acc, gain, bias, ones_mean, eps, xh=None, xl=None, rescale=None,
               y_out=None):
    m = Layout(nc, at)
    squares = [m.put(f"{tag}squares{i}", [P, KT, CW]) for i in range(2)]
    rstd = [m.put(f"{tag}rstd{i}", [P, CW]) for i in range(2)]
    with ExitStack() as ctx:
        sem = lambda n: ctx.enter_context(nc.semaphore(tag + n))
        bank = lambda n: ctx.enter_context(nc.psum_tensor(tag + n, [P, 512], F32))
        mean_ps = [bank(f"mean_ps{i}") for i in range(3)]
        var_ps = [bank(f"var_ps{i}") for i in range(3)]
        mean_done, centred, squared, var_done, std_done, rstd_done, scaled, affine, hi_done, \
            lo_done, rescaled, stored = map(sem, ("mean_done", "centred", "squared", "var_done",
                                                  "std_done", "rstd_done", "scaled", "affine",
                                                  "hi_done", "lo_done", "rescaled", "stored"))
        N = len(CHUNKS)
        with nc.Block() as block:

            @block.tensor
            def _(pe):
                def mean(c):
                    a, b = CHUNKS[c]
                    for k in range(KT):
                        mm = pe.matmul(mean_ps[c][:, 0:b - a], ones_mean[:, :], acc[:, k, a:b],
                                       start=k == 0, stop=k == KT - 1)
                    mm.then_inc(mean_done, 1)

                def variance(c):
                    a, b = CHUNKS[c]
                    pe.wait_ge(squared, c + 1)
                    for k in range(KT):
                        mm = pe.matmul(var_ps[c][:, 0:b - a], ones_mean[:, :], squares[c % 2][:, k, 0:b - a],
                                       start=k == 0, stop=k == KT - 1)
                    mm.then_inc(var_done, 1)

                mean(0)
                mean(1)
                variance(0)
                mean(2)
                variance(1)
                variance(2)

            @block.vector
            def _(dve):
                def centre(c):
                    a, b = CHUNKS[c]
                    dve.wait_ge(mean_done, c + 1)
                    for k in range(KT):
                        i = dve.tensor_tensor(acc[:, k, a:b], acc[:, k, a:b], mean_ps[c][:, 0:b - a],
                                              ALU.subtract)
                    i.then_inc(centred, 1)

                def normalise(c):
                    a, b = CHUNKS[c]
                    dve.wait_ge(std_done, c + 1)
                    dve.reciprocal(rstd[c % 2][:, 0:b - a], rstd[c % 2][:, 0:b - a]).then_inc(rstd_done, 1)
                    dve.wait_ge(rstd_done, c + 1)
                    dve.wait_ge(centred, c + 1)
                    for k in range(KT):
                        i = dve.scalar_tensor_tensor(acc[:, k, a:b], acc[:, k, a:b], scale,
                                                     rstd[c % 2][:, 0:b - a], ALU.mult, ALU.mult)
                    i.then_inc(scaled, 1)

                def finish(c):
                    if rescale is None:
                        return
                    a, b = CHUNKS[c]
                    dve.wait_ge(lo_done, c + 1)
                    dve.tensor_scalar(acc[:, :, a:b], acc[:, :, a:b], rescale, None, ALU.mult).then_inc(rescaled, 1)

                centre(0)
                centre(1)
                normalise(0)
                centre(2)
                normalise(1)
                finish(0)
                normalise(2)
                finish(1)
                finish(2)

            @block.scalar
            def _(act):
                def square(c):
                    a, b = CHUNKS[c]
                    act.wait_ge(centred, c + 1)
                    if c >= 2:
                        act.wait_ge(var_done, c - 1)
                    act.activation(squares[c % 2][:, :, 0:b - a], acc[:, :, a:b], ACT.Square,
                                   scale=scale).then_inc(squared, 1)

                def deviation(c):
                    a, b = CHUNKS[c]
                    act.wait_ge(var_done, c + 1)
                    if c >= 2:
                        act.wait_ge(scaled, c - 1)
                    act.activation(rstd[c % 2][:, 0:b - a], var_ps[c][:, 0:b - a], ACT.Sqrt,
                                   bias=eps[:, 0:1]).then_inc(std_done, 1)

                def affine_and_round(c):
                    a, b = CHUNKS[c]
                    act.wait_ge(scaled, c + 1)
                    for k in range(KT):
                        i = act.activation(acc[:, k, a:b], acc[:, k, a:b], ACT.Identity,
                                           scale=gain[:, k:k + 1], bias=bias[:, k:k + 1])
                    i.then_inc(affine, 1)
                    if xh is not None:
                        act.wait_ge(affine, c + 1)
                        act.activation(xh[:, :, a:b], acc[:, :, a:b], ACT.Copy).then_inc(hi_done, 1)

                square(0)
                square(1)
                deviation(0)
                square(2)
                deviation(1)
                affine_and_round(0)
                deviation(2)
                affine_and_round(1)
                affine_and_round(2)

            @block.gpsimd
            def _(pool):
                for c, (a, b) in enumerate(CHUNKS):
                    if xl is not None:
                        pool.wait_ge(hi_done, c + 1)
                        pool.tensor_tensor(xl[:, :, a:b], acc[:, :, a:b], xh[:, :, a:b].bitcast(F32),
                                           ALU.subtract).then_inc(lo_done, 1)

            @block.sync
            def _(sp):
                if y_out is not None:
                    for c, (a, b) in enumerate(CHUNKS):
                        sp.wait_ge(affine, c + 1)
                        sp.dma_start(y_out[:, :, a:b], acc[:, :, a:b]).then_inc(stored, 16)
                    sp.wait_ge(stored, 16 * N)


def weight_buffers(m, tag):
    stage = m.put(tag + "stage", [P, 2, D_MODEL])
    w_hi = [m.put(f"{tag}w_hi{s}", [P, D_MODEL], F32R) for s in range(2)]
    w_lo = [m.put(f"{tag}w_lo{s}", [P, D_MODEL], F32R) for s in range(2)]
    return stage, w_hi, w_lo


def project_tile(pe, out, w_hi, w_lo, xh, xl, a, b):
    for k in range(KT):
        d = slice(P * k, P * k + P)
        mm = three_passes(pe, out[:, 0:b - a], (w_hi[:, d], w_lo[:, d]), (xh[:, k, a:b], xl[:, k, a:b]),
                          k == 0, k == KT - 1)
    return mm


TOKEN_TILES = BLOCKS + 1
TURN_BATCHES = [(0, 3), (3, 6), (6, 9)]


def tile_tokens(n):
    return (P * n, P * n + P) if n < BLOCKS else (SEQ, TOK)


def retention_projection_phase(nc, at, w_in, w_small, xh, xl, ident, q_t, k_t, gate_t, k_tok, v_tok):
    k_decay, k_decay_dec = w_small
    tag = "rp_"
    m = Layout(nc, at)
    stage, w_hi, w_lo = weight_buffers(m, tag)
    k_turn = m.put(tag + "k_turn", [P, TOK])
    v_turn = m.put(tag + "v_turn", [P, TOK])
    Q, K, V, GATE = range(4)
    TILES = 4 * PAIRS
    with ExitStack() as ctx:
        sem = lambda n: ctx.enter_context(nc.semaphore(tag + n))
        bank = lambda n: ctx.enter_context(nc.psum_tensor(tag + n, [P, 512], F32))
        proj_ps = [bank(f"proj_ps{i}") for i in range(4)]
        turn_ps = [bank(f"turn_ps{i}") for i in range(3)]
        staged = [sem(f"staged{s}") for s in range(2)]
        hi_done, lo_done = sem("hi_done"), sem("lo_done")
        proj_done = sem("proj_done")
        proj_free = sem("proj_free")
        turned = sem("turned")
        turn_free = sem("turn_free")
        k_copied = sem("k_copied")
        zeroed = sem("zeroed")
        with nc.Block() as block:

            @block.sync
            def _(sp):
                for s in range(2):
                    sp.dma_start(stage[:, s, :], w_in[s]).then_inc(staged[s], 16)
                with sp.Fori(1, TILES // 2) as i:
                    for s in range(2):
                        sp.wait_ge(lo_done, 2 * i + s - 1)
                        sp.dma_start(stage[:, s, :], w_in[bass.ds(2 * i + s, 1), :, :].rearrange("a p n -> (a p) n")).then_inc(staged[s], 16)

            @block.scalar
            def _(act):
                act.sem_inc(proj_free, 4)

                def round_tile(t, j):
                    act.wait_ge(staged[j % 2], 32 * t + 16 * (j // 2) + 16)
                    act.activation(w_hi[j % 2][:, :], stage[:, j % 2, :], ACT.Copy).then_inc(hi_done, 1)

                def evacuate(t, j):
                    if j == K:
                        act.wait_ge(turned, 6 * t + 3)
                        act.wait_ge(k_copied, 3 + 3 * t)
                    if j == V:
                        act.wait_ge(turned, 6 * t + 6)
                    for c, (a, b) in enumerate(CHUNKS):
                        act.wait_ge(proj_done, 3 + 12 * t + 3 * j + c + 1)
                        ps = proj_ps[(3 * j + c) % 4][:, 0:b - a]
                        if j == Q:
                            out, func = q_t[:, bass.ds(t, 1), a:b].rearrange("p o n -> p (o n)"), ACT.Copy
                        elif j == K:
                            out, func = k_turn[:, a:b], ACT.Copy
                        elif j == V:
                            out, func = v_turn[:, a:b], ACT.Copy
                        else:
                            out, func = gate_t[:, bass.ds(t, 1), a:b].rearrange("p o n -> p (o n)"), ACT.Silu
                        act.activation(out, ps, func).then_inc(proj_free, 1)

                def step(t, last):
                    for j in range(4):
                        if not (last and j == GATE):
                            act.wait_ge(proj_done, 3 + 12 * t + 3 * j)
                            round_tile(t + (j + 1) // 4, (j + 1) % 4)
                        evacuate(t, j)

                round_tile(0, 0)
                with act.Fori(0, PAIRS - 1) as t:
                    step(t, False)
                step(PAIRS - 1, True)

            @block.gpsimd
            def _(pool):
                pool.sem_inc(k_copied, 3)
                pool.memset(k_tok[:, BLOCKS, :], 0.0).then_inc(zeroed, 1)
                pool.memset(v_tok[:, BLOCKS, :], 0.0).then_inc(zeroed, 1)

                def split(t, j):
                    pool.wait_ge(hi_done, 4 * t + j + 1)
                    pool.tensor_tensor(w_lo[j % 2][:, :], stage[:, j % 2, :], w_hi[j % 2][:, :].bitcast(F32),
                                       ALU.subtract).then_inc(lo_done, 1)

                def step(t, last):
                    for j in range(4):
                        if not (last and j == GATE):
                            split(t + (j + 1) // 4, (j + 1) % 4)
                        if j == K:
                            for c, (a, b) in enumerate(CHUNKS):
                                pool.wait_ge(proj_free, 4 + 12 * t + 3 * K + c + 1)
                                pool.tensor_copy(k_t[:, bass.ds(t, 1), a:b].rearrange("p o n -> p (o n)"),
                                                 k_turn[:, a:b]).then_inc(k_copied, 1)

                split(0, 0)
                with pool.Fori(0, PAIRS - 1) as t:
                    step(t, False)
                step(PAIRS - 1, True)

            @block.tensor
            def _(pe):
                pe.sem_inc(turned, 6)
                pe.sem_inc(proj_done, 3)

                def project(t, j):
                    pe.wait_ge(lo_done, 4 * t + j + 1)
                    for c, (a, b) in enumerate(CHUNKS):
                        pe.wait_ge(proj_free, 12 * t + 3 * j + c + 1)
                        project_tile(pe, proj_ps[(3 * j + c) % 4], w_hi[j % 2], w_lo[j % 2], xh, xl, a, b)\
                            .then_inc(proj_done, 1)

                def turn(t, src, j):
                    pe.wait_ge(proj_free, 4 + 12 * t + 3 * j + 3)
                    for n, (u0, u1) in enumerate(TURN_BATCHES):
                        pe.wait_ge(turn_free, 6 * t + 3 * (j - K) + n + 1)
                        for u in range(u0, u1):
                            a, b = tile_tokens(u)
                            mm = pe.transpose(turn_ps[n][0:b - a, P * (u - u0):P * (u - u0) + P],
                                              src[:, a:b], ident[:, :])
                        mm.then_inc(turned, 1)

                def step(t):
                    project(t, Q)
                    project(t, K)
                    project(t, V)
                    turn(t, k_turn, K)
                    project(t, GATE)
                    turn(t, v_turn, V)

                with pe.Fori(0, PAIRS) as t:
                    step(t)

            @block.vector
            def _(dve):
                dve.sem_inc(turn_free, 3)
                dve.wait_ge(zeroed, 2)

                def step(t):
                    for j in (K, V):
                        for n, (u0, u1) in enumerate(TURN_BATCHES):
                            dve.wait_ge(turned, 6 + 6 * t + 3 * (j - K) + n + 1)
                            heads = bass.ds(t * P, P)
                            for u in range(u0, u1):
                                rows = P if u < BLOCKS else DEC
                                ps = turn_ps[n][0:rows, P * (u - u0):P * (u - u0) + P]
                                if j == V:
                                    i = dve.tensor_copy(v_tok[0:rows, u, heads], ps)
                                else:
                                    decay = (k_decay if u < BLOCKS else k_decay_dec)[0:rows, bass.ds(2 * t, 2)]
                                    i = dve.tensor_tensor(
                                        k_tok[0:rows, u, heads].rearrange("p (h n) -> p h n", h=2),
                                        ps.rearrange("p (h n) -> p h n", h=2),
                                        decay.unsqueeze(2).to_broadcast([rows, 2, HD]), ALU.mult)
                            i.then_inc(turn_free, 1)

                with dve.Fori(0, PAIRS) as t:
                    step(t)


def retention_phase(nc, at, tables, g_chunk, g_dec, state_in, q_t, k_t, k_tok, v_tok, state_out,
                    state_dec_out):
    tag = "rt_"
    m = Layout(nc, at)
    mask = m.put(tag + "mask", [P, 2, PAIRS, P])
    q_decay = m.put(tag + "q_decay", [P, PAIRS, P])
    mask_dec = m.put(tag + "mask_dec", [P, 2, PAIRS, DEC])
    q_decay_dec = m.put(tag + "q_decay_dec", [P, PAIRS, DEC])
    own = m.put(tag + "own", [P, DEC_BATCH])
    state_dec = m.put(tag + "state_dec", [P, PAIRS, DEC_BATCH, HD])
    v_own = m.put(tag + "v_own", [DEC, HEADS, DEC_BATCH, HD])
    q_dec = [m.put(f"{tag}q_dec{i}", [P, PAIRS, P]) for i in range(2)]
    probs = [m.put(f"{tag}probs{i}", [P, 2, PAIRS * P]) for i in range(2)]
    state = [m.put(f"{tag}state{i}", [P, PAIRS, HD]) for i in range(2)]
    LAST = BLOCKS
    with ExitStack() as ctx:
        sem = lambda n: ctx.enter_context(nc.semaphore(tag + n))
        bank = lambda n: ctx.enter_context(nc.psum_tensor(tag + n, [P, 512], F32))
        score_ps = [[bank(f"score_ps{i}{h}") for h in range(2)] for i in range(2)]
        out_ps = [bank(f"out_ps{h}") for h in range(2)]
        kv_ps = [bank(f"kv_ps{i}") for i in range(2)]
        tables_in, dec_in = sem("tables_in"), sem("dec_in")
        scored, masked, q_ready, kv_done, state_done, out_done, out_read, owned, stored, dec_state_done, \
            zeroed = map(sem, ("scored", "masked", "q_ready", "kv_done", "state_done", "out_done",
                               "out_read", "owned", "stored", "dec_state_done", "zeroed"))

        def tokens(n):
            a, b = tile_tokens(n)
            return a, b, b - a

        def head(t, h):
            return slice(HD * (2 * t + h), HD * (2 * t + h) + HD)

        with nc.Block() as block:

            @block.sync
            def _(sp):
                for buf, src in ((mask, tables["mask"]), (q_decay, tables["q_decay"]),
                                 (mask_dec, tables["mask_dec"]), (q_decay_dec, tables["q_decay_dec"]),
                                 (own, tables["own"])):
                    sp.dma_start(buf[tuple(slice(None) for _ in buf.shape)], src).then_inc(tables_in, 16)
                sp.dma_start(state_dec[:, :, :, :], state_in).then_inc(dec_in, 16)
                sp.wait_ge(state_done, PAIRS * BLOCKS)
                sp.dma_start(state_out, state[(BLOCKS - 1) % 2][:, :, :]).then_inc(stored, 16)
                sp.wait_ge(dec_state_done, PAIRS)
                sp.dma_start(state_dec_out, state_dec[:, :, :, :]).then_inc(stored, 16)
                sp.wait_ge(stored, 32)

            @block.gpsimd
            def _(pool):
                pool.wait_ge(tables_in, 80)
                for n in range(LAST + 1):
                    a, b, w = tokens(n)
                    if n >= 2:
                        pool.wait_ge(out_done, n - 1)
                    decay = q_decay if n < LAST else q_decay_dec
                    pool.tensor_tensor(q_dec[n % 2][:, :, 0:w], q_t[:, :, a:b], decay[:, :, :],
                                       ALU.mult).then_inc(q_ready, 1)
                    if n == 0:
                        for hd in range(HEADS):
                            pool.tensor_tensor(
                                v_own[:, hd, :, :],
                                v_tok[0:DEC, LAST, HD * hd:HD * hd + HD].unsqueeze(1).to_broadcast([DEC, DEC_BATCH, HD]),
                                own[0:DEC, :].unsqueeze(2).to_broadcast([DEC, DEC_BATCH, HD]),
                                ALU.mult).then_inc(owned, 1)

            @block.tensor
            def _(pe):
                def scores(n):
                    a, b, w = tokens(n)
                    if n >= 2:
                        pe.wait_ge(masked, 2 * (n - 1))
                    for h in range(2):
                        d = slice(HD * h, HD * h + HD)
                        for t in range(PAIRS):
                            mm = pe.matmul(score_ps[n % 2][h][0:w, w * t:w * t + w], k_t[d, t, a:b], q_t[d, t, a:b],
                                           start=True, stop=True)
                        mm.then_inc(scored, 1)

                def key_values(n):
                    if n >= 2:
                        pe.wait_ge(state_done, PAIRS * (n - 1))
                    for t in range(PAIRS):
                        for h in range(2):
                            mm = pe.matmul(kv_ps[n % 2][HD * h:HD * h + HD, HD * t:HD * t + HD],
                                           k_tok[:, n, head(t, h)], v_tok[:, n, head(t, h)], start=True, stop=True)
                    mm.then_inc(kv_done, 1)

                def output(n):
                    a, b, w = tokens(n)
                    pe.wait_ge(masked, 2 * n + 2)
                    if n == LAST:
                        pe.wait_ge(zeroed, 1)
                    if n >= 1:
                        pe.wait_ge(out_read, 2 * n)
                    if 1 <= n < LAST:
                        pe.wait_ge(state_done, PAIRS * n)
                    pe.wait_ge(q_ready, n + 1)
                    if n == LAST:
                        pe.wait_ge(dec_in, 16)
                    for h in range(2):
                        d = slice(HD * h, HD * h + HD)
                        for t in range(PAIRS):
                            mm = pe.matmul(out_ps[h][d, w * t:w * t + w], v_tok[:, n, head(t, h)],
                                           probs[n % 2][:, h, w * t:w * t + w], start=True, stop=n == 0)
                            if n == LAST:
                                for s in range(DEC_BATCH):
                                    i = slice(DEC_SEQ * s, DEC_SEQ * s + DEC_SEQ)
                                    mm = pe.matmul(out_ps[h][d, w * t + i.start:w * t + i.stop],
                                                   state_dec[d, t, s, :], q_dec[n % 2][d, t, i],
                                                   start=False, stop=s == DEC_BATCH - 1)
                            elif n >= 1:
                                mm = pe.matmul(out_ps[h][d, w * t:w * t + w], state[(n - 1) % 2][d, t, :],
                                               q_dec[n % 2][d, t, 0:w], start=False, stop=True)
                    mm.then_inc(out_done, 1)

                pe.wait_ge(tables_in, 80)
                scores(0)
                for n in range(LAST + 1):
                    if n < LAST:
                        scores(n + 1)
                        key_values(n)
                    output(n)
                for t in range(PAIRS):
                    if t < 2:
                        pe.wait_ge(state_done, PAIRS * BLOCKS)
                    else:
                        pe.wait_ge(dec_state_done, t - 1)
                    pe.wait_ge(owned, 2 * t + 2)
                    for h in range(2):
                        mm = pe.matmul(kv_ps[t % 2][HD * h:HD * h + HD, :], k_tok[0:DEC, LAST, head(t, h)],
                                       v_own[:, 2 * t + h, :, :].rearrange("p b e -> p (b e)"), start=True, stop=True)
                    mm.then_inc(kv_done, 1)

            @block.vector
            def _(dve):
                dve.wait_ge(tables_in, 80)
                for n in range(LAST + 1):
                    a, b, w = tokens(n)
                    if n == LAST:
                        dve.wait_ge(out_done, n - 1)
                        dve.memset(probs[n % 2][DEC:P, :, :], 0.0).then_inc(zeroed, 1)
                    for h in range(2):
                        dve.wait_ge(scored, 2 * n + h + 1)
                        if n >= 2:
                            dve.wait_ge(out_done, n - 1)
                        table = (mask if n < LAST else mask_dec)[0:w, h, :, :].rearrange("p t i -> p (t i)")
                        dve.tensor_tensor(probs[n % 2][0:w, h, 0:w * PAIRS], score_ps[n % 2][h][0:w, 0:w * PAIRS],
                                          table, ALU.mult).then_inc(masked, 1)
                    if n == LAST:
                        break
                    dve.wait_ge(kv_done, n + 1)
                    if n >= 2:
                        dve.wait_ge(out_done, n)
                    for t in range(PAIRS):
                        kv = kv_ps[n % 2][:, HD * t:HD * t + HD]
                        if n == 0:
                            dve.tensor_copy(state[0][:, t, :], kv).then_inc(state_done, 1)
                        else:
                            dve.wait_ge(state_done, PAIRS * (n - 1) + t + 1)
                            dve.scalar_tensor_tensor(state[n % 2][:, t, :], state[(n - 1) % 2][:, t, :],
                                                     g_chunk[:, t:t + 1], kv, ALU.mult, ALU.add).then_inc(state_done, 1)
                dve.wait_ge(out_done, LAST + 1)
                for t in range(PAIRS):
                    dve.wait_ge(kv_done, BLOCKS + t + 1)
                    s = state_dec[:, t, :, :].rearrange("p b e -> p (b e)")
                    dve.scalar_tensor_tensor(s, s, g_dec[:, t:t + 1], kv_ps[t % 2][:, :], ALU.mult, ALU.add)\
                       .then_inc(dec_state_done, 1)

            @block.scalar
            def _(act):
                for n in range(LAST + 1):
                    a, b, w = tokens(n)
                    act.wait_ge(out_done, n + 1)
                    act.wait_ge(q_ready, n + 1)
                    for h in range(2):
                        d = slice(HD * h, HD * h + HD)
                        act.activation(q_t[d, :, a:b], out_ps[h][d, 0:w * PAIRS].rearrange("p (t i) -> p t i", i=w),
                                       ACT.Copy).then_inc(out_read, 1)


def group_norm_phase(nc, at, gn_sum, gn_spread, ones_head, eps, gn_w, o_t, gate_t, mix_hi, mix_lo):
    tag = "gn_"
    m = Layout(nc, at)
    sum_w = m.put(tag + "sum_w", [P, PAIRS, HEADS])
    spread_w = m.put(tag + "spread_w", [HEADS, PAIRS, P])
    squares = [m.put(f"{tag}squares{i}", [P, PAIRS, CW]) for i in range(2)]
    rstd = [m.put(f"{tag}rstd{i}", [HEADS, CW]) for i in range(2)]
    with ExitStack() as ctx:
        sem = lambda n: ctx.enter_context(nc.semaphore(tag + n))
        bank = lambda n: ctx.enter_context(nc.psum_tensor(tag + n, [P, 512], F32))
        mean_ps = [bank(f"mean_ps{i}") for i in range(2)]
        var_ps = [bank(f"var_ps{i}") for i in range(2)]
        spread_ps = [bank(f"spread_ps{i}") for i in range(4)]
        tables_in, mean_done, centred, squared, var_done, std_done, rstd_done, spread_done, scaled, \
            gated, hi_done, lo_done = map(sem, (
                "tables_in", "mean_done", "centred", "squared", "var_done", "std_done", "rstd_done",
                "spread_done", "scaled", "gated", "hi_done", "lo_done"))
        N = len(CHUNKS)
        with nc.Block() as block:

            @block.sync
            def _(sp):
                sp.dma_start(sum_w[:, :, :], gn_sum).then_inc(tables_in, 16)
                sp.dma_start(spread_w[:, :, :], gn_spread).then_inc(tables_in, 16)
                sp.wait_ge(tables_in, 32)

            @block.tensor
            def _(pe):
                def means(c):
                    a, b = CHUNKS[c]
                    for t in range(PAIRS):
                        u = PAIRS * c + t
                        if u >= 2:
                            pe.wait_ge(centred, u - 1)
                        pe.matmul(mean_ps[u % 2][:, 0:b - a], ones_head[:, :], o_t[:, t, a:b],
                                  start=True, stop=True).then_inc(mean_done, 1)

                def variance(c):
                    a, b = CHUNKS[c]
                    pe.wait_ge(squared, c + 1)
                    if c >= 2:
                        pe.wait_ge(std_done, c - 1)
                    for t in range(PAIRS):
                        mm = pe.matmul(var_ps[c % 2][0:HEADS, 0:b - a], sum_w[:, t, :], squares[c % 2][:, t, 0:b - a],
                                       start=t == 0, stop=t == PAIRS - 1)
                    mm.then_inc(var_done, 1)

                def spread(c):
                    a, b = CHUNKS[c]
                    pe.wait_ge(rstd_done, c + 1)
                    for t in range(PAIRS):
                        if c:
                            pe.wait_ge(scaled, PAIRS * (c - 1) + t + 1)
                        pe.matmul(spread_ps[t][:, 0:b - a], spread_w[:, t, :], rstd[c % 2][:, 0:b - a],
                                  start=True, stop=True).then_inc(spread_done, 1)

                pe.wait_ge(tables_in, 32)
                means(0)
                for c in range(N):
                    if c + 1 < N:
                        means(c + 1)
                    variance(c)
                    spread(c)

            @block.vector
            def _(dve):
                def centre(c):
                    a, b = CHUNKS[c]
                    for t in range(PAIRS):
                        dve.wait_ge(mean_done, PAIRS * c + t + 1)
                        dve.tensor_tensor(o_t[:, t, a:b], o_t[:, t, a:b], mean_ps[(PAIRS * c + t) % 2][:, 0:b - a],
                                          ALU.subtract).then_inc(centred, 1)

                def invert(c):
                    a, b = CHUNKS[c]
                    dve.wait_ge(std_done, c + 1)
                    r = rstd[c % 2][:, 0:b - a]
                    dve.reciprocal(r, r).then_inc(rstd_done, 1)

                def gate(c):
                    a, b = CHUNKS[c]
                    for t in range(PAIRS):
                        dve.wait_ge(spread_done, PAIRS * c + t + 1)
                        dve.wait_ge(centred, PAIRS * c + t + 1)
                        dve.wait_ge(squared, c + 1)
                        dve.scalar_tensor_tensor(o_t[:, t, a:b], o_t[:, t, a:b], gn_w[:, t:t + 1],
                                                 spread_ps[t][:, 0:b - a], ALU.mult, ALU.mult).then_inc(scaled, 1)
                    for t in range(PAIRS):
                        dve.wait_ge(scaled, PAIRS * c + t + 1)
                        dve.tensor_tensor(o_t[:, t, a:b], o_t[:, t, a:b], gate_t[:, t, a:b],
                                          ALU.mult).then_inc(gated, 1)

                centre(0)
                for c in range(N):
                    if c + 1 < N:
                        centre(c + 1)
                    invert(c)
                    gate(c)

            @block.scalar
            def _(act):
                def square(c):
                    a, b = CHUNKS[c]
                    act.wait_ge(centred, PAIRS * c + PAIRS)
                    if c >= 2:
                        act.wait_ge(var_done, c - 1)
                    act.activation(squares[c % 2][:, :, 0:b - a], o_t[:, :, a:b], ACT.Square).then_inc(squared, 1)

                def deviation(c):
                    a, b = CHUNKS[c]
                    act.wait_ge(var_done, c + 1)
                    if c >= 2:
                        act.wait_ge(spread_done, PAIRS * (c - 1))
                    act.activation(rstd[c % 2][:, 0:b - a], var_ps[c % 2][0:HEADS, 0:b - a], ACT.Sqrt,
                                   bias=eps[0:HEADS, 0:1]).then_inc(std_done, 1)

                def round_mix(c):
                    a, b = CHUNKS[c]
                    act.wait_ge(gated, PAIRS * c + PAIRS)
                    act.activation(mix_hi[:, 0:PAIRS, a:b], o_t[:, :, a:b], ACT.Copy).then_inc(hi_done, 1)

                square(0)
                for c in range(N):
                    deviation(c)
                    if c + 1 < N:
                        square(c + 1)
                    round_mix(c)

            @block.gpsimd
            def _(pool):
                for c, (a, b) in enumerate(CHUNKS):
                    pool.wait_ge(hi_done, c + 1)
                    pool.tensor_tensor(mix_lo[:, 0:PAIRS, a:b], o_t[:, :, a:b], mix_hi[:, 0:PAIRS, a:b].bitcast(F32),
                                       ALU.subtract).then_inc(lo_done, 1)



def attention_projection_phase(nc, at, w_in, xh, xl, ident, q_t, k_t, v_tok):
    tag = "ap_"
    m = Layout(nc, at)
    stage, w_hi, w_lo = weight_buffers(m, tag)
    v_turn = m.put(tag + "v_turn", [P, TOK])
    K, V = PAIRS, PAIRS + 1
    TILES = PAIRS + 2
    with ExitStack() as ctx:
        sem = lambda n: ctx.enter_context(nc.semaphore(tag + n))
        bank = lambda n: ctx.enter_context(nc.psum_tensor(tag + n, [P, 512], F32))
        ps = [bank(f"ps{i}") for i in range(6)]
        turn_ps = [bank(f"turn_ps{i}") for i in range(2)]
        staged = [sem(f"staged{s}") for s in range(2)]
        hi_done, lo_done = sem("hi_done"), sem("lo_done")
        proj_done = sem("proj_done")
        proj_free = sem("proj_free")
        turned, turn_free, zeroed = sem("turned"), sem("turn_free"), sem("zeroed")
        with nc.Block() as block:

            @block.sync
            def _(sp):
                for s in range(2):
                    sp.dma_start(stage[:, s, :], w_in[s]).then_inc(staged[s], 16)
                with sp.Fori(1, TILES // 2) as i:
                    for s in range(2):
                        sp.wait_ge(lo_done, 2 * i + s - 1)
                        sp.dma_start(stage[:, s, :], w_in[bass.ds(2 * i + s, 1), :, :].rearrange("a p n -> (a p) n")).then_inc(staged[s], 16)

            @block.scalar
            def _(act):
                act.sem_inc(proj_free, 6)

                def round_tile(i, s):
                    act.wait_ge(staged[s], 16 * i + 16)
                    act.activation(w_hi[s][:, :], stage[:, s, :], ACT.Copy).then_inc(hi_done, 1)

                def evacuate(tile, s, out):
                    for c, (a, b) in enumerate(CHUNKS):
                        act.wait_ge(proj_done, 3 + 3 * tile + c + 1)
                        act.activation(out(a, b), ps[3 * s + c][:, 0:b - a], ACT.Copy).then_inc(proj_free, 1)

                round_tile(0, 0)
                with act.Fori(0, PAIRS // 2) as i:
                    for s in range(2):
                        act.wait_ge(proj_done, 3 + 6 * i + 3 * s)
                        round_tile(i + s, 1 - s)
                        evacuate(2 * i + s, s,
                                 lambda a, b: q_t[:, bass.ds(2 * i + s, 1), a:b].rearrange("p o n -> p (o n)"))
                act.wait_ge(proj_done, 3 + 3 * K)
                round_tile(PAIRS // 2, 1)
                evacuate(K, 0, lambda a, b: k_t[:, a:b])
                evacuate(V, 1, lambda a, b: v_turn[:, a:b])

            @block.gpsimd
            def _(pool):
                pool.memset(v_tok[:, BLOCKS, :], 0.0).then_inc(zeroed, 1)
                with pool.Fori(0, TILES // 2) as i:
                    for s in range(2):
                        pool.wait_ge(hi_done, 2 * i + s + 1)
                        pool.tensor_tensor(w_lo[s][:, :], stage[:, s, :], w_hi[s][:, :].bitcast(F32),
                                           ALU.subtract).then_inc(lo_done, 1)

            @block.tensor
            def _(pe):
                pe.sem_inc(proj_done, 3)
                with pe.Fori(0, TILES // 2) as i:
                    for s in range(2):
                        pe.wait_ge(lo_done, 2 * i + s + 1)
                        for c, (a, b) in enumerate(CHUNKS):
                            pe.wait_ge(proj_free, 6 * i + 3 * s + c + 1)
                            project_tile(pe, ps[3 * s + c], w_hi[s], w_lo[s], xh, xl, a, b).then_inc(proj_done, 1)
                pe.wait_ge(proj_free, 6 + 3 * TILES)
                for n, (u0, u1) in enumerate(TURN_BATCHES):
                    if n == 2:
                        pe.wait_ge(turn_free, 1)
                    for u in range(u0, u1):
                        a, b = tile_tokens(u)
                        mm = pe.transpose(turn_ps[n % 2][0:b - a, P * (u - u0):P * (u - u0) + P], v_turn[:, a:b],
                                          ident[:, :])
                    mm.then_inc(turned, 1)

            @block.vector
            def _(dve):
                dve.wait_ge(zeroed, 1)
                for n, (u0, u1) in enumerate(TURN_BATCHES):
                    dve.wait_ge(turned, n + 1)
                    for u in range(u0, u1):
                        rows = P if u < BLOCKS else DEC
                        i = dve.tensor_copy(v_tok[0:rows, u, :], turn_ps[n % 2][0:rows, P * (u - u0):P * (u - u0) + P])
                    i.then_inc(turn_free, 1)


def attention_phase(nc, at, at_caches, tables, sinks, sinks_dec, caches, q_t, k_t, v_tok, ident,
                    mix_hi, mix_lo, outs):
    tag = "at_"
    m = Layout(nc, at)
    bias = m.put(tag + "bias", [P, KVH, GROUP, 2 * P])
    bias_dec = m.put(tag + "bias_dec", [P, KVH, 2, P + DEC])
    SLOTS = 3
    scores = [m.put(f"{tag}scores{i}", [P, GROUP * 2 * P]) for i in range(SLOTS)]
    turned = [m.put(f"{tag}turned{i}", [P, GROUP * P]) for i in range(2)]
    stats = [m.put(f"{tag}stats{i}", [P, 6, GROUP]) for i in range(SLOTS)]
    q_rows = m.put(tag + "q_rows", [P, DEC_BATCH, GROUP, DEC_SEQ])
    TOP, NEG, SUM, SINK, DEN, INV = range(6)
    mc = Layout(nc, at_caches)
    k_cache = mc.put(tag + "k_cache", [P, DEC_BATCH, WINDOW])
    v_cache = mc.put(tag + "v_cache", [P, DEC_BATCH, P])
    ITEMS = [(n, h) for n in range(BLOCKS + 1) for h in range(KVH)]
    LAST = len(ITEMS)
    KEYS = P + DEC
    with ExitStack() as ctx:
        sem = lambda n: ctx.enter_context(nc.semaphore(tag + n))
        bank = lambda n: ctx.enter_context(nc.psum_tensor(tag + n, [P, 512], F32))
        score_ps = [[bank(f"score_ps{i}{j}") for j in range(2)] for i in range(2)]
        turn_ps = [bank(f"turn_ps{i}") for i in range(2)]
        out_ps = [bank(f"out_ps{i}") for i in range(KVH)]
        tables_in, dec_in, scored, biased, maxed, topped, negated, sunk, exped, sink_exped, summed, inverted, \
            normed, turn_done, turn_read, out_done, hi_done, lo_done, stored, cached, q_ordered = map(sem, (
                "tables_in", "dec_in", "scored", "biased", "maxed", "topped", "negated", "sunk",
                "exped", "sink_exped", "summed", "inverted", "normed", "turn_done", "turn_read",
                "out_done", "hi_done", "lo_done", "stored", "cached", "q_ordered"))

        def shape(i):
            n, h = ITEMS[i]
            if n == BLOCKS:
                return 2, 0, KEYS
            return GROUP, (P if n == 0 else 0), 2 * P

        def scores_of(i):
            n, h = ITEMS[i]
            groups, k0, k1 = shape(i)
            width = KEYS if n == BLOCKS else 2 * P
            return scores[i % SLOTS][:, 0:groups * width].rearrange("p (g k) -> p g k", g=groups)[:, :, k0:k1]

        def per_group(i, what):
            return stats[i % SLOTS][:, what, 0:shape(i)[0]]

        def sinks_of(i):
            n, h = ITEMS[i]
            if n == BLOCKS:
                return sinks_dec[:, h:h + 1].to_broadcast([P, 2])
            return sinks[:, GROUP * h:GROUP * h + GROUP]

        with nc.Block() as block:

            @block.sync
            def _(sp):
                sp.dma_start(bias[:, :, :, :], tables["bias"]).then_inc(tables_in, 16)
                sp.dma_start(bias_dec[:, :, :, :], tables["bias_dec"]).then_inc(tables_in, 16)
                sp.dma_start(k_cache[:, :, :], caches["k"]).then_inc(dec_in, 16)
                sp.dma_start(v_cache[:, :, :], caches["v"]).then_inc(dec_in, 16)
                sp.dma_start(outs["k_prompt"], k_t[:, SEQ - WINDOW:SEQ]).then_inc(stored, 16)
                sp.dma_start(outs["v_prompt"], v_tok[:, BLOCKS - 1, :]).then_inc(stored, 16)
                sp.dma_start(outs["k_dec"][:, :, WINDOW - DEC_SEQ:WINDOW],
                             k_t[:, SEQ:TOK].rearrange("p (b i) -> p b i", i=DEC_SEQ)).then_inc(stored, 16)
                for s in range(DEC_BATCH):
                    sp.dma_start(outs["v_dec"][s, WINDOW - DEC_SEQ:WINDOW, :],
                                 v_tok[DEC_SEQ * s:DEC_SEQ * s + DEC_SEQ, BLOCKS, :]).then_inc(stored, 16)
                sp.wait_ge(dec_in, 32)
                sp.dma_start(outs["k_dec"][:, :, 0:WINDOW - DEC_SEQ], k_cache[:, :, DEC_SEQ:WINDOW]).then_inc(stored, 16)
                sp.dma_start(outs["v_dec"][:, 0:WINDOW - DEC_SEQ, :].rearrange("b k n -> k b n"),
                             v_cache[DEC_SEQ:WINDOW, :, :]).then_inc(stored, 16)
                sp.wait_ge(stored, 16 * (5 + DEC_BATCH))

            @block.tensor
            def _(pe):
                def score(i):
                    n, h = ITEMS[i]
                    d = slice(HD * h, HD * h + HD)
                    if i >= 2:
                        pe.wait_ge(biased, i - 1)
                    if n == BLOCKS:
                        pe.wait_ge(dec_in, 32)
                        pe.wait_ge(q_ordered, GROUP)
                        for s in range(DEC_BATCH):
                            rows = slice(32 * (s % 4), 32 * (s % 4) + 32)
                            half = KEYS * (s // 4)
                            q = q_rows[d, s, :, :].rearrange("p t i -> p (t i)")
                            pe.matmul(score_ps[i % 2][0][rows, half:half + P], q, k_cache[d, s, :], start=True, stop=True)
                            mm = pe.matmul(score_ps[i % 2][0][rows, half + P:half + KEYS], q, k_t[d, SEQ:TOK],
                                           start=True, stop=True)
                    else:
                        k0 = P if n == 0 else 0
                        for t in range(GROUP):
                            col = 2 * P * (t % 2)
                            mm = pe.matmul(score_ps[i % 2][t // 2][:, col + k0:col + 2 * P],
                                           q_t[d, t, P * n:P * n + P], k_t[d, P * (n - 1) + k0:P * (n + 1)],
                                           start=True, stop=True)
                    mm.then_inc(scored, 1)

                def transposes(i):
                    n, h = ITEMS[i]
                    pe.wait_ge(normed, i + 1)
                    if i:
                        pe.wait_ge(turn_read, 2 * i)
                    p = scores[i % SLOTS]
                    if n == BLOCKS:
                        for half in range(2):
                            pe.transpose(turn_ps[0][:, P * half:P * half + P], p[:, KEYS * half:KEYS * half + P], ident[:, :])
                        for half in range(2):
                            mm = pe.transpose(turn_ps[1][0:DEC, P * half:P * half + P],
                                              p[:, KEYS * half + P:KEYS * half + KEYS], ident[:, :])
                    else:
                        for kb in range(1 if n == 0 else 0, 2):
                            for t in range(GROUP):
                                mm = pe.transpose(turn_ps[kb][:, P * t:P * t + P],
                                                  p[:, P * (2 * t + kb):P * (2 * t + kb) + P], ident[:, :])
                    mm.then_inc(turn_done, 1)

                def output(i):
                    n, h = ITEMS[i]
                    d = slice(HD * h, HD * h + HD)
                    pe.wait_ge(turn_read, 2 * i + 2)
                    if i >= 2:
                        pe.wait_ge(lo_done, i - 1)
                    if n == BLOCKS:
                        for half in range(2):
                            mm = pe.matmul(out_ps[h][d, P * half:P * half + P], v_tok[:, BLOCKS, d],
                                           turned[1][:, P * half:P * half + P], start=True, stop=False)
                            for s in range(4 * half, 4 * half + 4):
                                col = slice(32 * s, 32 * s + 32)
                                mm = pe.matmul(out_ps[h][d, col], v_cache[:, s, d], turned[0][:, col],
                                               start=False, stop=s % 4 == 3)
                    else:
                        first = 1 if n == 0 else 0
                        for kb in range(first, 2):
                            mm = pe.matmul(out_ps[h][d, :], v_tok[:, n - 1 + kb, d], turned[kb][:, :],
                                           start=kb == first, stop=kb == 1)
                    mm.then_inc(out_done, 1)

                score(0)
                score(1)
                for i in range(LAST):
                    transposes(i)
                    if i + 2 < LAST:
                        score(i + 2)
                    output(i)

            @block.vector
            def _(dve):
                dve.wait_ge(tables_in, 32)

                def add_bias(i):
                    n, h = ITEMS[i]
                    groups, k0, k1 = shape(i)
                    dve.wait_ge(scored, i + 1)
                    if i >= SLOTS:
                        dve.wait_ge(turn_done, i - SLOTS + 1)
                    out = scores_of(i)
                    if n == BLOCKS:
                        ps = score_ps[i % 2][0][:, 0:2 * KEYS].rearrange("p (g k) -> p g k", g=2)
                        dve.scalar_tensor_tensor(out, ps, QSCALE, bias_dec[:, h, :, :], ALU.mult, ALU.add)\
                           .then_inc(biased, 1)
                    else:
                        for j in range(2):
                            ps = score_ps[i % 2][j][:, :].rearrange("p (g k) -> p g k", g=2)[:, :, k0:k1]
                            x = dve.scalar_tensor_tensor(out[:, 2 * j:2 * j + 2, :], ps, QSCALE,
                                                         bias[:, h, 2 * j:2 * j + 2, k0:k1], ALU.mult, ALU.add)
                        x.then_inc(biased, 1)

                def top(i):
                    dve.wait_ge(biased, i + 1)
                    if i >= SLOTS:
                        dve.wait_ge(normed, i - SLOTS + 1)
                    dve.tensor_reduce(per_group(i, TOP), scores_of(i), AX.X, ALU.max).then_inc(maxed, 1)
                    dve.wait_ge(maxed, i + 1)
                    dve.tensor_tensor(per_group(i, TOP), per_group(i, TOP), sinks_of(i), ALU.max).then_inc(topped, 1)
                    dve.wait_ge(topped, i + 1)
                    dve.tensor_tensor(per_group(i, SINK), sinks_of(i), per_group(i, TOP), ALU.subtract).then_inc(sunk, 1)
                    dve.tensor_scalar(per_group(i, NEG), per_group(i, TOP), -1.0, None, ALU.mult).then_inc(negated, 1)

                def denominator(i):
                    dve.wait_ge(sink_exped, i + 1)
                    dve.tensor_tensor(per_group(i, DEN), per_group(i, SUM), per_group(i, SINK), ALU.add).then_inc(summed, 1)
                    dve.wait_ge(summed, i + 1)
                    dve.reciprocal(per_group(i, INV), per_group(i, DEN)).then_inc(inverted, 1)

                def low_part(i):
                    n, h = ITEMS[i]
                    d = slice(HD * h, HD * h + HD)
                    dve.wait_ge(hi_done, i + 1)
                    if n == BLOCKS:
                        for t in range(GROUP):
                            x = dve.tensor_tensor(
                                mix_lo[d, PAIRS + t, SEQ:TOK].rearrange("p (b i) -> p b i", i=DEC_SEQ),
                                out_ps[h][d, 0:2 * P].rearrange("p (b t i) -> p b t i", t=GROUP, i=DEC_SEQ)[:, :, t, :],
                                mix_hi[d, PAIRS + t, SEQ:TOK].rearrange("p (b i) -> p b i", i=DEC_SEQ).bitcast(F32),
                                ALU.subtract)
                        x.then_inc(lo_done, 1)
                    else:
                        dve.tensor_tensor(mix_lo[d, PAIRS:2 * PAIRS, P * n:P * n + P],
                                          out_ps[h][d, :].rearrange("p (t q) -> p t q", t=GROUP),
                                          mix_hi[d, PAIRS:2 * PAIRS, P * n:P * n + P].bitcast(F32),
                                          ALU.subtract).then_inc(lo_done, 1)

                for i in range(LAST + 3):
                    if i < LAST:
                        add_bias(i)
                        top(i)
                    if 1 <= i <= LAST:
                        denominator(i - 1)
                    if i >= 3:
                        low_part(i - 3)

            @block.scalar
            def _(act):
                def exponentials(i):
                    n, h = ITEMS[i]
                    act.wait_ge(negated, i + 1)
                    s = scores_of(i)
                    for g in range(shape(i)[0]):
                        act.activation(s[:, g, :], s[:, g, :], ACT.Exp, bias=stats[i % SLOTS][:, NEG, g:g + 1],
                                       accum_out=stats[i % SLOTS][:, SUM, g:g + 1]).then_inc(exped, 1)
                    act.activation(per_group(i, SINK), per_group(i, SINK), ACT.Exp).then_inc(sink_exped, 1)

                def read_turned(i):
                    n, h = ITEMS[i]
                    act.wait_ge(turn_done, i + 1)
                    if i:
                        act.wait_ge(out_done, i)
                    for kb in range(2):
                        if n == 0 and kb == 0:
                            act.sem_inc(turn_read, 1)
                            continue
                        rows = DEC if n == BLOCKS and kb == 1 else P
                        cols = 2 * P if n == BLOCKS else GROUP * P
                        if rows < P and h == 0:
                            act.wait_ge(cached, 1)
                        act.activation(turned[kb][0:rows, 0:cols], turn_ps[kb][0:rows, 0:cols], ACT.Copy)\
                           .then_inc(turn_read, 1)

                def high_part(i):
                    n, h = ITEMS[i]
                    d = slice(HD * h, HD * h + HD)
                    act.wait_ge(out_done, i + 1)
                    if n == BLOCKS:
                        for t in range(GROUP):
                            x = act.activation(
                                mix_hi[d, PAIRS + t, SEQ:TOK].rearrange("p (b i) -> p b i", i=DEC_SEQ),
                                out_ps[h][d, 0:2 * P].rearrange("p (b t i) -> p b t i", t=GROUP, i=DEC_SEQ)[:, :, t, :],
                                ACT.Copy)
                        x.then_inc(hi_done, 1)
                    else:
                        act.activation(mix_hi[d, PAIRS:2 * PAIRS, P * n:P * n + P],
                                       out_ps[h][d, :].rearrange("p (t q) -> p t q", t=GROUP), ACT.Copy).then_inc(hi_done, 1)

                exponentials(0)
                for i in range(LAST):
                    if i + 1 < LAST:
                        exponentials(i + 1)
                    read_turned(i)
                    high_part(i)

            @block.gpsimd
            def _(pool):
                for t in range(GROUP):
                    pool.tensor_copy(q_rows[:, :, t, :], q_t[:, t, SEQ:TOK].rearrange("p (b i) -> p b i", i=DEC_SEQ))\
                        .then_inc(q_ordered, 1)
                for i in range(LAST):
                    n, h = ITEMS[i]
                    groups, k0, k1 = shape(i)
                    if i == LAST - 2:
                        pool.wait_ge(out_done, i)
                        pool.memset(turned[1][:, :], 0.0).then_inc(cached, 1)
                    pool.wait_ge(inverted, i + 1)
                    s = scores_of(i)
                    pool.tensor_tensor(s, s, per_group(i, INV).unsqueeze(2).to_broadcast([P, groups, k1 - k0]),
                                       ALU.mult).then_inc(normed, 1)


def output_projection_phase(nc, at, w_out, mix_hi, mix_lo, xh, xl, acc):
    tag = "op_"
    m = Layout(nc, at)
    stage, w_hi, w_lo = weight_buffers(m, tag)
    with ExitStack() as ctx:
        sem = lambda n: ctx.enter_context(nc.semaphore(tag + n))
        ps = [ctx.enter_context(nc.psum_tensor(f"{tag}ps{i}", [P, 512], F32)) for i in range(6)]
        staged = [sem(f"staged{s}") for s in range(2)]
        hi_done, lo_done = sem("hi_done"), sem("lo_done")
        proj_done = sem("proj_done")
        proj_free = sem("proj_free")
        summed = sem("summed")
        with nc.Block() as block:

            @block.sync
            def _(sp):
                for s in range(2):
                    sp.dma_start(stage[:, s, :], w_out[s]).then_inc(staged[s], 16)
                with sp.Fori(1, KT // 2) as i:
                    for s in range(2):
                        sp.wait_ge(lo_done, 2 * i + s - 1)
                        sp.dma_start(stage[:, s, :], w_out[bass.ds(2 * i + s, 1), :, :].rearrange("a p n -> (a p) n")).then_inc(staged[s], 16)

            @block.scalar
            def _(act):
                act.wait_ge(staged[0], 16)
                act.activation(w_hi[0][:, :], stage[:, 0, :], ACT.Copy).then_inc(hi_done, 1)
                act.wait_ge(staged[1], 16)
                act.activation(w_hi[1][:, :], stage[:, 1, :], ACT.Copy).then_inc(hi_done, 1)
                with act.Fori(1, KT // 2) as i:
                    for s in range(2):
                        act.wait_ge(staged[s], 16 * i + 16)
                        act.wait_ge(proj_done, 6 * i + 3 * s - 3)
                        act.activation(w_hi[s][:, :], stage[:, s, :], ACT.Copy).then_inc(hi_done, 1)

            @block.gpsimd
            def _(pool):
                with pool.Fori(0, KT // 2) as i:
                    for s in range(2):
                        pool.wait_ge(hi_done, 2 * i + s + 1)
                        pool.tensor_tensor(w_lo[s][:, :], stage[:, s, :], w_hi[s][:, :].bitcast(F32),
                                           ALU.subtract).then_inc(lo_done, 1)

            @block.tensor
            def _(pe):
                with pe.Fori(0, KT // 2) as i:
                    for s in range(2):
                        pe.wait_ge(lo_done, 2 * i + s + 1)
                        for c, (a, b) in enumerate(CHUNKS):
                            pe.wait_ge(proj_free, 6 * i + 3 * s + c + 1)
                            project_tile(pe, ps[3 * s + c], w_hi[s], w_lo[s], mix_hi, mix_lo, a, b).then_inc(proj_done, 1)

            @block.vector
            def _(dve):
                dve.sem_inc(proj_free, 6)
                with dve.Fori(0, KT // 2) as i:
                    for s in range(2):
                        for c, (a, b) in enumerate(CHUNKS):
                            u = 6 * i + 3 * s + c
                            one = lambda t: t[:, bass.ds(2 * i + s, 1), a:b].rearrange("p o n -> p (o n)")
                            dve.wait_ge(proj_done, u + 1)
                            dve.scalar_tensor_tensor(one(acc), one(xh).bitcast(F32), ALPHA, ps[3 * s + c][:, 0:b - a],
                                                     ALU.mult, ALU.add).then_inc(proj_free, 1)
                            dve.wait_ge(proj_free, 6 + u + 1)
                            dve.scalar_tensor_tensor(one(acc), one(xl).bitcast(F32), ALPHA, one(acc),
                                                     ALU.mult, ALU.add).then_inc(summed, 1)


SMALL = {}
for _name, _width in (("ln_gain", 3 * KT), ("ln_bias", 3 * KT), ("gn_w", PAIRS), ("g_chunk", PAIRS),
                      ("g_dec", PAIRS), ("sinks", HEADS), ("sinks_dec", KVH), ("k_decay", HEADS),
                      ("k_decay_dec", HEADS), ("ident", P)):
    _at = sum(s.stop - s.start for s in SMALL.values())
    SMALL[_name] = slice(_at, _at + _width)
SMALL_W = SMALL["ident"].stop


def decoder_layer_kernel(nc, i, o):
    base = Layout(nc, -(-nc.sbuf_base // 32) * 32)
    xh = base.put("x_hi", [P, KT, TOK], F32R)
    xl = base.put("x_lo", [P, KT, TOK], F32R)
    small = base.put("small", [P, SMALL_W])
    ones_mean = base.put("ones_mean", [P, P])
    ones_head = base.put("ones_head", [P, P])
    eps = base.put("eps", [P, 1])
    part = lambda name: small[:, SMALL[name]]
    ident = part("ident")
    mixer_at = base.at
    acc = base.put("acc", [P, KT, TOK])
    free = base.at

    gain = lambda n: small[:, SMALL["ln_gain"].start + KT * n:SMALL["ln_gain"].start + KT * n + KT]
    shift = lambda n: small[:, SMALL["ln_bias"].start + KT * n:SMALL["ln_bias"].start + KT * n + KT]

    load_phase(nc, i["x"], i["small"], small, ones_mean, ones_head, eps, acc, xh, xl)
    ffn_phase(nc, "f1_", free, i["ffn1"], acc, xh, xl)
    norm_phase(nc, "n1_", free, 0.5, acc, gain(0), shift(0), ones_mean, eps, xh, xl)

    m = Layout(nc, mixer_at)
    q_t = m.put("ret_q", [P, PAIRS, TOK])
    gate_t = m.put("ret_gate", [P, PAIRS, TOK])
    m = Layout(nc, free)
    k_t = m.put("ret_k", [P, PAIRS, TOK])
    k_tok = m.put("ret_k_tok", [P, TOKEN_TILES, HEADS * HD])
    v_tok = m.put("ret_v_tok", [P, TOKEN_TILES, HEADS * HD])
    retention_projection_phase(nc, m.at, i["w_ret"], (part("k_decay"), part("k_decay_dec")), xh, xl, ident,
                               q_t, k_t, gate_t, k_tok, v_tok)
    retention_phase(nc, m.at, i, part("g_chunk"), part("g_dec"), i["state"], q_t, k_t, k_tok, v_tok,
                    o["state_prompt"], o["state_dec"])
    m = Layout(nc, free)
    mix_hi = m.put("mix_hi", [P, KT, TOK], F32R)
    mix_lo = m.put("mix_lo", [P, KT, TOK], F32R)
    behind = m.at
    group_norm_phase(nc, behind, i["gn_sum"], i["gn_spread"], ones_head, eps, part("gn_w"), q_t, gate_t,
                     mix_hi, mix_lo)

    m = Layout(nc, mixer_at)
    q_t = m.put("att_q", [P, PAIRS, TOK])
    k_t = m.put("att_k", [P, TOK])
    v_tok = m.put("att_v_tok", [P, TOKEN_TILES, P])
    attention_projection_phase(nc, behind, i["w_att"], xh, xl, ident, q_t, k_t, v_tok)
    attention_phase(nc, behind, m.at, i, part("sinks"), part("sinks_dec"), {"k": i["k_cache"], "v": i["v_cache"]},
                    q_t, k_t, v_tok, ident, mix_hi, mix_lo, o)
    output_projection_phase(nc, behind, i["w_out"], mix_hi, mix_lo, xh, xl, acc)
    norm_phase(nc, "n2_", free, 1.0, acc, gain(1), shift(1), ones_mean, eps, xh, xl, rescale=2 * ALPHA)

    ffn_phase(nc, "f2_", free, i["ffn2"], acc, xh, xl)
    norm_phase(nc, "n3_", free, 0.5, acc, gain(2), shift(2), ones_mean, eps, y_out=o["y"])


def shape_constants():
    head = np.arange(HEADS, dtype=np.float64)
    log_g = np.log1p(-np.exp2(-5.0 - head))
    halves = lambda t: np.repeat(t.reshape(PAIRS, 2).T, HD, axis=0)
    idx = np.arange(P)
    tok = np.arange(DEC)
    seq, pos = tok // DEC_SEQ, tok % DEC_SEQ

    def decay_mask(dist, valid):
        e = np.where(valid[None], np.exp(np.where(valid, dist, 0)[None] * log_g[:, None, None]), 0.0) * QSCALE
        return e.reshape(PAIRS, 2, *dist.shape).transpose(2, 1, 0, 3)

    def rows(a):
        out = np.zeros((P, *a.shape[1:]))
        out[:a.shape[0]] = a
        return out

    dist = idx[None, :] - idx[:, None]
    dist_dec = pos[None, :] - pos[:, None]
    same = seq[None, :] == seq[:, None]
    slopes = np.exp2(-8.0 / HEADS * np.arange(1, HEADS + 1))
    back = idx[:, None] + P - np.arange(2 * P)[None, :]
    bias = np.where((back >= 0) & (back <= WINDOW), -slopes.reshape(KVH, GROUP, 1, 1) * back, MASKED)
    s4, t4, i8 = (v.reshape(-1) for v in np.meshgrid(np.arange(4), np.arange(GROUP), np.arange(DEC_SEQ), indexing="ij"))
    cached = i8[:, None] + WINDOW - np.arange(WINDOW)[None, :]
    bias_dec = np.empty((P, KVH, 2, P + DEC))
    for h in range(KVH):
        for half in range(2):
            sl = slopes[GROUP * h + t4][:, None]
            new = i8[:, None] - pos[None, :]
            mine = (4 * half + s4)[:, None] == seq[None, :]
            bias_dec[:, h, half, :WINDOW] = np.where(cached <= WINDOW, -sl * cached, MASKED)
            bias_dec[:, h, half, WINDOW:] = np.where(mine & (new >= 0), -sl * new, MASKED)
    gn_sum = np.zeros((P, PAIRS, HEADS))
    gn_spread = np.zeros((HEADS, PAIRS, P))
    for t in range(PAIRS):
        for h in range(2):
            gn_sum[HD * h:HD * h + HD, t, 2 * t + h] = 1.0 / HD
            gn_spread[2 * t + h, t, HD * h:HD * h + HD] = 1.0
    small = {
        "g_chunk": halves(np.exp(P * log_g)),
        "g_dec": halves(np.exp(DEC_SEQ * log_g)),
        "k_decay": np.exp((P - 1.0 - idx)[:, None] * log_g) * QSCALE,
        "k_decay_dec": rows(np.exp((DEC_SEQ - 1.0 - pos)[:, None] * log_g) * QSCALE),
        "ident": np.eye(P),
    }
    q_exp = lambda p: np.exp((p + 1.0)[None, :] * log_g[:, None])
    q_tab = lambda p: np.repeat(q_exp(p).reshape(PAIRS, 2, -1).transpose(1, 0, 2), HD, axis=0)
    tables = {
        "mask": decay_mask(dist, dist >= 0),
        "mask_dec": rows(decay_mask(dist_dec, same & (dist_dec >= 0))),
        "q_decay": q_tab(idx),
        "q_decay_dec": q_tab(pos),
        "own": rows((seq[:, None] == np.arange(DEC_BATCH)[None, :]).astype(np.float64)),
        "bias": bias.transpose(2, 0, 1, 3),
        "bias_dec": bias_dec,
        "gn_sum": gn_sum,
        "gn_spread": gn_spread,
    }
    f = lambda d: {k: np.ascontiguousarray(v, dtype=np.float32) for k, v in d.items()}
    return f(small), f(tables)


def kernel(x_prompt, x_sample, state_ret, cache_swa_k, cache_swa_v, ln_gain, ln_bias, w_in, ret_gn_w,
           swa_sinks, w_out, ffn1_gate, ffn1_up, ffn1_down, ffn2_gate, ffn2_up, ffn2_down):
    import concourse.bacc as bacc
    from concourse.bass_utils import run_bass_kernel_spmd

    arr = np.asarray
    small_c, tables = shape_constants()

    def by_feature(v):
        return arr(v).reshape(-1, P).T

    def lhs_tiles(w):
        w = arr(w)
        return w.reshape(KT, P, -1, P).transpose(2, 1, 0, 3).reshape(-1, P, D_MODEL)

    def ffn(gate, up, down):
        return np.stack([lhs_tiles(gate[0]), lhs_tiles(up[0]), arr(down[0]).reshape(FT, P, D_MODEL)], axis=2)

    x = np.concatenate([arr(x_prompt)[0], arr(x_sample).reshape(DEC, D_MODEL)], axis=0)
    w = arr(w_in)[0]
    R = HEADS * HD
    ret = lhs_tiles(w[:, :4 * R]).reshape(4, PAIRS, P, D_MODEL).transpose(1, 0, 2, 3).reshape(4 * PAIRS, P, D_MODEL)
    att_q = w[:, 4 * R:5 * R].reshape(D_MODEL, KVH, GROUP, HD).transpose(0, 2, 1, 3).reshape(D_MODEL, R)
    att = np.concatenate([lhs_tiles(att_q), lhs_tiles(w[:, 5 * R:])], axis=0)
    wo = arr(w_out)[0]
    wo_att = wo[R:].reshape(KVH, GROUP, HD, D_MODEL).transpose(1, 0, 2, 3).reshape(R, D_MODEL)
    sinks = arr(swa_sinks)[0]
    sinks_dec = np.broadcast_to(sinks.reshape(KVH, 1, GROUP, 1), (KVH, 4, GROUP, DEC_SEQ)).reshape(KVH, P).T
    small = {
        **small_c,
        "ln_gain": by_feature(arr(ln_gain)[0]), "ln_bias": by_feature(arr(ln_bias)[0]),
        "gn_w": by_feature(arr(ret_gn_w)[0]),
        "sinks": np.broadcast_to(sinks, (P, HEADS)), "sinks_dec": sinks_dec,
    }
    ins = {
        "x": x.T.reshape(KT, P, TOK).transpose(1, 0, 2),
        "small": np.concatenate([small[n] for n in SMALL], axis=1),
        "ffn1": ffn(ffn1_gate, ffn1_up, ffn1_down),
        "ffn2": ffn(ffn2_gate, ffn2_up, ffn2_down),
        "w_ret": ret,
        "w_att": att,
        "w_out": lhs_tiles(np.concatenate([wo[:R], wo_att], axis=0)),
        "state": arr(state_ret)[0].reshape(DEC_BATCH, PAIRS, 2, HD, HD).transpose(2, 3, 1, 0, 4)
                 .reshape(P, PAIRS, DEC_BATCH, HD),
        "k_cache": arr(cache_swa_k)[0].transpose(2, 3, 0, 1).reshape(P, DEC_BATCH, WINDOW),
        "v_cache": arr(cache_swa_v)[0].transpose(1, 0, 2, 3).reshape(WINDOW, DEC_BATCH, P),
        **tables,
    }
    outs = {
        "y": (P, KT, TOK),
        "state_prompt": (P, PAIRS, HD),
        "state_dec": (P, PAIRS, DEC_BATCH, HD),
        "k_prompt": (P, WINDOW), "v_prompt": (WINDOW, P),
        "k_dec": (P, DEC_BATCH, WINDOW), "v_dec": (DEC_BATCH, WINDOW, P),
    }
    nc = bacc.Bacc("TRN2", target_bir_lowering=False, num_devices=1)
    i = {n: nc.dram_tensor(n + "_in", a.shape, F32, kind="ExternalInput").ap() for n, a in ins.items()}
    o = {n: nc.dram_tensor(n + "_out", s, F32, kind="ExternalOutput").ap() for n, s in outs.items()}
    decoder_layer_kernel(nc, i, o)
    got = run_bass_kernel_spmd(nc, [{n + "_in": np.ascontiguousarray(a) for n, a in ins.items()}],
                               core_ids=[0]).results[0]
    got = {n: got[n + "_out"] for n in outs}

    y = got["y"].transpose(2, 1, 0).reshape(TOK, D_MODEL)
    state_p = got["state_prompt"].reshape(2, HD, PAIRS, HD).transpose(2, 0, 1, 3)
    state_d = got["state_dec"].reshape(2, HD, PAIRS, DEC_BATCH, HD).transpose(3, 2, 0, 1, 4)
    k_p = got["k_prompt"].reshape(KVH, HD, WINDOW).transpose(2, 0, 1)
    k_d = got["k_dec"].reshape(KVH, HD, DEC_BATCH, WINDOW).transpose(2, 3, 0, 1)
    return (
        y[:SEQ].reshape(1, SEQ, D_MODEL), y[SEQ:].reshape(DEC_BATCH, DEC_SEQ, D_MODEL),
        state_p.reshape(1, 1, HEADS, HD, HD), k_p.reshape(1, 1, WINDOW, KVH, HD),
        got["v_prompt"].reshape(1, 1, WINDOW, KVH, HD),
        state_d.reshape(1, DEC_BATCH, HEADS, HD, HD), k_d.reshape(1, DEC_BATCH, WINDOW, KVH, HD),
        got["v_dec"].reshape(1, DEC_BATCH, WINDOW, KVH, HD),
    )
```

```python
from contextlib import ExitStack

import numpy as np

import concourse.bass as bass
from concourse import mybir

F32 = mybir.dt.float32
F32R = mybir.dt.float32r
ACT = mybir.ActivationFunctionType
ALU = mybir.AluOpType
AX = mybir.AxisListType

P = 128
D_MODEL = 1024
D_FF = 2816
KT = D_MODEL // P
FT = D_FF // P
SEQ = 1024
DEC_BATCH, DEC_SEQ = 8, 8
DEC = DEC_BATCH * DEC_SEQ
TOK = SEQ + DEC
HEADS, HD = 8, 64
PAIRS = HEADS // 2
KVH = 2
GROUP = HEADS // KVH
WINDOW = 128
BLOCKS = SEQ // P
EPS = 1e-5
ALPHA = 2.0 ** 0.25
QSCALE = HD ** -0.5
MASKED = -1e30

CHUNKS = [(0, 362), (362, 726), (726, TOK)]
CW = max(b - a for a, b in CHUNKS)

RET, SWA = 0, 1


class Core:

    def __init__(self, nc, semaphore, banks):
        self.nc, self.semaphore, self.banks = nc, semaphore, banks


class Stage:

    def __init__(self, sync=None, scalar=None, gpsimd=None, tensor=None, vector=None, sync_early=None, sync_x=None, sync_small=None,
                 scalar_early=None, gpsimd_early=None, x_ready=None, acc_ready=None,
                 products_done=None, end=None):
        self.sync, self.scalar, self.gpsimd, self.tensor, self.vector = sync, scalar, gpsimd, tensor, vector
        self.sync_x, self.sync_small = sync_x, sync_small
        self.sync_early, self.scalar_early, self.gpsimd_early = sync_early, scalar_early, gpsimd_early
        self.x_ready, self.acc_ready, self.products_done, self.end = x_ready, acc_ready, products_done, end


class Layout:

    def __init__(self, nc, at):
        self.nc, self.at = nc, at

    def put(self, name, shape, dtype=F32):
        t = self.nc.alloc_sbuf_tensor_at(name, shape, dtype, offset=self.at)
        self.at += -(-int(np.prod(shape[1:])) * 4 // 32) * 32
        return t


def three_passes(pe, out, weights, moving, first, last):
    (wh, wl), (xh, xl) = weights, moving
    pe.matmul(out, wh, xh, start=first, stop=False)
    pe.matmul(out, wh, xl, start=False, stop=False)
    return pe.matmul(out, wl, xh, start=False, stop=last)


def load_stage(core, x_in, small_in, small, ones_mean, ones_head, eps, acc, xh, xl):
    sem = lambda n: core.semaphore("load_" + n)
    x_loaded = [sem(f"x_loaded{c}") for c in range(len(CHUNKS))]
    small_loaded, hi_done, lo_done, scaled, filled = map(
        sem, ("small_loaded", "hi_done", "lo_done", "scaled", "filled"))

    def sync_x(sp, c):
        a, b = CHUNKS[c]
        sp.dma_start(acc[:, :, a:b], x_in[:, :, a:b]).then_inc(x_loaded[c], 16)

    def sync_small(sp):
        sp.dma_start(small[:, :], small_in).then_inc(small_loaded, 16)
        sp.wait_ge(small_loaded, 16)

    def gpsimd(pool):
        pool.memset(ones_mean[:, :], 1.0 / D_MODEL).then_inc(filled, 1)
        pool.memset(ones_head[:, :], 0.0).then_inc(filled, 1)
        pool.memset(eps[:, :], EPS).then_inc(filled, 1)
        pool.wait_ge(filled, 3)
        for h in range(2):
            d = slice(HD * h, HD * h + HD)
            pool.memset(ones_head[d, d], 1.0 / HD).then_inc(filled, 1)
        pool.wait_ge(filled, 5)

    def scalar(act, c):
        a, b = CHUNKS[c]
        act.wait_ge(x_loaded[c], 16)
        act.activation(xh[:, :, a:b], acc[:, :, a:b], ACT.Copy).then_inc(hi_done, 1)

    def vector(dve):
        for c, (a, b) in enumerate(CHUNKS):
            dve.wait_ge(hi_done, c + 1)
            dve.tensor_tensor(xl[:, :, a:b], acc[:, :, a:b], xh[:, :, a:b].bitcast(F32),
                              ALU.subtract).then_inc(lo_done, 1)
            dve.wait_ge(lo_done, c + 1)
            dve.tensor_scalar(acc[:, :, a:b], acc[:, :, a:b], 2 * ALPHA, None, ALU.mult).then_inc(scaled, 1)

    return Stage(sync_x=sync_x, sync_small=sync_small, gpsimd=gpsimd, scalar=scalar, vector=vector,
                 x_ready=lo_done, acc_ready=(scaled, len(CHUNKS)))


def ffn_stage(core, tag, at, w_in, acc, xh, xl, x_ready, acc_ready, room=None):
    m = Layout(core.nc, at)
    stage = m.put(tag + "stage", [P, 3, D_MODEL])
    w_hi = [[m.put(f"{tag}w_hi{s}{j}", [P, KT, P], F32R) for j in range(3)] for s in range(2)]
    w_lo = [[m.put(f"{tag}w_lo{s}{j}", [P, KT, P], F32R) for j in range(3)] for s in range(2)]
    h_hi = [m.put(f"{tag}h_hi{s}", [P, TOK], F32R) for s in range(2)]
    h_lo = [m.put(f"{tag}h_lo{s}", [P, TOK], F32R) for s in range(2)]
    silu = m.put(tag + "silu", [P, 3, CW])
    h_full = m.put(tag + "h_full", [P, 3, CW])
    GATE, UP, DOWN = range(3)
    NC_ = len(CHUNKS)
    DOWNS = KT * NC_
    sem = lambda n: core.semaphore(tag + n)
    gate_ps, up_ps, down_ps = core.banks[0:2], core.banks[2:4], core.banks[4:8]
    staged = [sem(f"staged{j}") for j in range(3)]
    hi_done = sem("hi_done")
    gu_split = sem("gu_split")
    down_split = sem("down_split")
    gate_done, up_done = sem("gate_done"), sem("up_done")
    silu_done = sem("silu_done")
    pair_free = sem("pair_free")
    h_hi_done, h_lo_done = sem("h_hi_done"), sem("h_lo_done")
    down_done = sem("down_done")
    down_free = sem("down_free")

    def tiles(eng, step):
        with eng.Fori(0, (FT - 2) // 2) as i:
            step(2 * i + 1, 1)
            step(2 * i + 2, 0)
        step(FT - 1, 1)

    def pair_of(s, c):
        return (3 * s + c) % 2

    def sync_early(sp):
        if room:
            sp.wait_ge(*room)
        for j in range(3):
            sp.dma_start(stage[:, j, :], w_in[0, :, j, :]).then_inc(staged[j], 16)

    def sync(sp):
        with sp.Fori(1, FT) as f:
            for j in (GATE, UP):
                sp.wait_ge(gu_split, 2 * f - 1 + j)
                sp.dma_start(stage[:, j, :], w_in[bass.ds(f, 1), :, j, :].rearrange("a p n -> (a p) n")).then_inc(staged[j], 16)
            sp.wait_ge(down_split, f)
            sp.dma_start(stage[:, DOWN, :], w_in[bass.ds(f, 1), :, DOWN, :].rearrange("a p n -> (a p) n")).then_inc(staged[DOWN], 16)

    def round_part(act, f, s, j):
        act.wait_ge(staged[j], 16 * f + 16)
        act.activation(w_hi[s][j][:, :, :].rearrange("p k n -> p (k n)"), stage[:, j, :],
                       ACT.Copy).then_inc(hi_done, 1)

    def scalar_early(act):
        for j in range(3):
            round_part(act, 0, 0, j)

    def scalar(act):
        def silu_chunk(f, s, c):
            a, b = CHUNKS[c]
            act.wait_ge(gate_done, 3 * f + c + 1)
            act.activation(silu[:, c, 0:b - a], gate_ps[pair_of(s, c)][:, 0:b - a],
                           ACT.Silu).then_inc(silu_done, 1)

        def round_h(f, s, c):
            a, b = CHUNKS[c]
            act.wait_ge(pair_free, 2 + 3 * f + c + 1)
            act.activation(h_hi[s][:, a:b], h_full[:, c, 0:b - a], ACT.Copy).then_inc(h_hi_done, 1)

        def step(f, s, more=True):
            if more:
                if not (isinstance(f, int) and f == 0):
                    act.wait_ge(up_done, 3 * f)
                round_part(act, f + 1, 1 - s, GATE)
                round_part(act, f + 1, 1 - s, UP)
            silu_chunk(f, s, 0)
            silu_chunk(f, s, 1)
            round_h(f, s, 0)
            silu_chunk(f, s, 2)
            round_h(f, s, 1)
            round_h(f, s, 2)
            if more:
                if not (isinstance(f, int) and f == 0):
                    act.wait_ge(down_done, DOWNS * f)
                round_part(act, f + 1, 1 - s, DOWN)

        step(0, 0)
        with act.Fori(0, (FT - 2) // 2) as i:
            step(2 * i + 1, 1)
            step(2 * i + 2, 0)
        step(FT - 1, 1, more=False)

    def split(pool, f, s):
        for j, done in ((GATE, gu_split), (UP, gu_split), (DOWN, down_split)):
            pool.wait_ge(hi_done, 3 * f + j + 1)
            pool.tensor_tensor(w_lo[s][j][:, :, :].rearrange("p k n -> p (k n)"), stage[:, j, :],
                               w_hi[s][j][:, :, :].rearrange("p k n -> p (k n)").bitcast(F32),
                               ALU.subtract).then_inc(done, 1)

    def gpsimd_early(pool):
        split(pool, 0, 0)

    def gpsimd(pool):
        with pool.Fori(0, (FT - 2) // 2) as i:
            split(pool, 2 * i + 1, 1)
            split(pool, 2 * i + 2, 0)
        split(pool, FT - 1, 1)

    def tensor(pe):
        def gate_up(f, s):
            for c, (a, b) in enumerate(CHUNKS):
                pair = pair_of(s, c)
                if isinstance(f, int) and f == 0:
                    pe.wait_ge(x_ready, c + 1)
                pe.wait_ge(pair_free, 3 * f + c + 1)
                for j, ps, done in ((GATE, gate_ps, gate_done), (UP, up_ps, up_done)):
                    if c == 0:
                        pe.wait_ge(gu_split, 2 * f + j + 1)
                    for k in range(KT):
                        mm = three_passes(pe, ps[pair][:, 0:b - a],
                                          (w_hi[s][j][:, k, :], w_lo[s][j][:, k, :]),
                                          (xh[:, k, a:b], xl[:, k, a:b]), k == 0, k == KT - 1)
                    mm.then_inc(done, 1)

        def down(f, s):
            pe.wait_ge(down_split, f + 1)
            n = 0
            for d in range(KT):
                for c, (a, b) in enumerate(CHUNKS):
                    if d == 0:
                        pe.wait_ge(h_lo_done, 3 * f + c + 1)
                    pe.wait_ge(down_free, DOWNS * f + n + 1 + DOWNS - 4)
                    three_passes(pe, down_ps[n % 4][:, 0:b - a],
                                 (w_hi[s][DOWN][:, d, :], w_lo[s][DOWN][:, d, :]),
                                 (h_hi[s][:, a:b], h_lo[s][:, a:b]), True, True).then_inc(down_done, 1)
                    n += 1

        def step(f, s):
            gate_up(f, s)
            down(f - 1, 1 - s)

        gate_up(0, 0)
        tiles(pe, step)
        down(FT - 1, 1)

    def vector(dve):
        dve.sem_inc(pair_free, 2)

        def h_chunk(f, s, c):
            a, b = CHUNKS[c]
            if not (isinstance(f, int) and f == 0):
                dve.wait_ge(h_lo_done, 3 * f + c - 2)
            dve.wait_ge(silu_done, 3 * f + c + 1)
            dve.wait_ge(up_done, 3 * f + c + 1)
            dve.tensor_tensor(h_full[:, c, 0:b - a], up_ps[pair_of(s, c)][:, 0:b - a],
                              silu[:, c, 0:b - a], ALU.mult).then_inc(pair_free, 1)

        def split_h(f, s, c):
            a, b = CHUNKS[c]
            dve.wait_ge(h_hi_done, 3 * f + c + 1)
            dve.tensor_tensor(h_lo[s][:, a:b], h_full[:, c, 0:b - a],
                              h_hi[s][:, a:b].bitcast(F32), ALU.subtract).then_inc(h_lo_done, 1)

        def h_tile(f, s):
            h_chunk(f, s, 0)
            h_chunk(f, s, 1)
            split_h(f, s, 0)
            h_chunk(f, s, 2)
            split_h(f, s, 1)
            split_h(f, s, 2)

        def add_down(f):
            n = 0
            for d in range(KT):
                for a, b in CHUNKS:
                    dve.wait_ge(down_free, DOWNS * f + n + 1)
                    dve.wait_ge(down_done, DOWNS * f + n + 1)
                    dve.tensor_tensor(acc[:, d, a:b], down_ps[n % 4][:, 0:b - a], acc[:, d, a:b],
                                      ALU.add).then_inc(down_free, 1)
                    n += 1

        def step(f, s):
            h_tile(f, s)
            add_down(f - 1)

        h_tile(0, 0)
        dve.wait_ge(*acc_ready)
        dve.sem_inc(down_free, DOWNS)
        tiles(dve, step)
        add_down(FT - 1)

    return Stage(sync_early=sync_early, scalar_early=scalar_early, gpsimd_early=gpsimd_early,
                 sync=sync, scalar=scalar, gpsimd=gpsimd, tensor=tensor, vector=vector,
                 products_done=(down_done, DOWNS * FT), acc_ready=(down_free, DOWNS * (FT + 1)), end=m.at)


def norm_stage(core, tag, at, scale, acc, gain, bias, ones_mean, eps, xh=None, xl=None, rescale=None,
               y_out=None, acc_ready=None):
    m = Layout(core.nc, at)
    squares = m.put(tag + "squares", [P, KT, CW])
    rstd = [m.put(f"{tag}rstd{i}", [P, CW]) for i in range(2)]
    sem = lambda n: core.semaphore(tag + n)
    mean_ps, var_ps = core.banks[4:6], core.banks[6:8]
    mean_done, centred, squared, var_done, std_done, rstd_done, scaled, affine, hi_done, \
        lo_done, rescaled, stored = map(sem, ("mean_done", "centred", "squared", "var_done",
                                              "std_done", "rstd_done", "scaled", "affine",
                                              "hi_done", "lo_done", "rescaled", "stored"))
    N = len(CHUNKS)
    def tensor(pe):
        def mean(c):
            a, b = CHUNKS[c]
            if c >= 2:
                pe.wait_ge(centred, c - 1)
            for k in range(KT):
                mm = pe.matmul(mean_ps[c % 2][:, 0:b - a], ones_mean[:, :], acc[:, k, a:b],
                               start=k == 0, stop=k == KT - 1)
            mm.then_inc(mean_done, 1)

        def variance(c):
            a, b = CHUNKS[c]
            pe.wait_ge(squared, c + 1)
            if c >= 2:
                pe.wait_ge(std_done, c - 1)
            for k in range(KT):
                mm = pe.matmul(var_ps[c % 2][:, 0:b - a], ones_mean[:, :], squares[:, k, 0:b - a],
                               start=k == 0, stop=k == KT - 1)
            mm.then_inc(var_done, 1)

        pe.wait_ge(*acc_ready)
        mean(0)
        mean(1)
        variance(0)
        mean(2)
        variance(1)
        variance(2)

    def vector(dve):
        def centre(c):
            a, b = CHUNKS[c]
            dve.wait_ge(mean_done, c + 1)
            for k in range(KT):
                i = dve.tensor_tensor(acc[:, k, a:b], acc[:, k, a:b], mean_ps[c % 2][:, 0:b - a],
                                      ALU.subtract)
            i.then_inc(centred, 1)

        def normalise(c):
            a, b = CHUNKS[c]
            dve.wait_ge(std_done, c + 1)
            dve.reciprocal(rstd[c % 2][:, 0:b - a], rstd[c % 2][:, 0:b - a]).then_inc(rstd_done, 1)
            dve.wait_ge(rstd_done, c + 1)
            dve.wait_ge(centred, c + 1)
            for k in range(KT):
                i = dve.scalar_tensor_tensor(acc[:, k, a:b], acc[:, k, a:b], scale,
                                             rstd[c % 2][:, 0:b - a], ALU.mult, ALU.mult)
            i.then_inc(scaled, 1)

        def finish(c):
            if rescale is None:
                return
            a, b = CHUNKS[c]
            dve.wait_ge(lo_done, c + 1)
            dve.tensor_scalar(acc[:, :, a:b], acc[:, :, a:b], rescale, None, ALU.mult).then_inc(rescaled, 1)

        centre(0)
        centre(1)
        normalise(0)
        centre(2)
        normalise(1)
        finish(0)
        normalise(2)
        finish(1)
        finish(2)

    def scalar(act):
        def square(c):
            a, b = CHUNKS[c]
            act.wait_ge(centred, c + 1)
            if c:
                act.wait_ge(var_done, c)
            act.activation(squares[:, :, 0:b - a], acc[:, :, a:b], ACT.Square,
                           scale=scale).then_inc(squared, 1)

        def deviation(c):
            a, b = CHUNKS[c]
            act.wait_ge(var_done, c + 1)
            if c >= 2:
                act.wait_ge(scaled, c - 1)
            act.activation(rstd[c % 2][:, 0:b - a], var_ps[c % 2][:, 0:b - a], ACT.Sqrt,
                           bias=eps[:, 0:1]).then_inc(std_done, 1)

        def affine_and_round(c):
            a, b = CHUNKS[c]
            act.wait_ge(scaled, c + 1)
            for k in range(KT):
                i = act.activation(acc[:, k, a:b], acc[:, k, a:b], ACT.Identity,
                                   scale=gain[:, k:k + 1], bias=bias[:, k:k + 1])
            i.then_inc(affine, 1)
            if xh is not None:
                act.wait_ge(affine, c + 1)
                act.activation(xh[:, :, a:b], acc[:, :, a:b], ACT.Copy).then_inc(hi_done, 1)

        square(0)
        square(1)
        deviation(0)
        square(2)
        deviation(1)
        affine_and_round(0)
        deviation(2)
        affine_and_round(1)
        affine_and_round(2)

    def gpsimd(pool):
        for c, (a, b) in enumerate(CHUNKS):
            if xl is not None:
                pool.wait_ge(hi_done, c + 1)
                pool.tensor_tensor(xl[:, :, a:b], acc[:, :, a:b], xh[:, :, a:b].bitcast(F32),
                                   ALU.subtract).then_inc(lo_done, 1)

    def sync(sp):
        if y_out is not None:
            for c, (a, b) in enumerate(CHUNKS):
                sp.wait_ge(affine, c + 1)
                sp.dma_start(y_out[:, :, a:b], acc[:, :, a:b]).then_inc(stored, 16)
            sp.wait_ge(stored, 16 * N)

    return Stage(tensor=tensor, vector=vector, scalar=scalar, gpsimd=gpsimd, sync=sync,
                 x_ready=lo_done, acc_ready=(rescaled, N))


def weight_buffers(m, tag):
    stage = m.put(tag + "stage", [P, 2, D_MODEL])
    w_hi = [m.put(f"{tag}w_hi{s}", [P, D_MODEL], F32R) for s in range(2)]
    w_lo = [m.put(f"{tag}w_lo{s}", [P, D_MODEL], F32R) for s in range(2)]
    return stage, w_hi, w_lo


def project_tile(pe, out, w_hi, w_lo, xh, xl, a, b):
    for k in range(KT):
        d = slice(P * k, P * k + P)
        mm = three_passes(pe, out[:, 0:b - a], (w_hi[:, d], w_lo[:, d]), (xh[:, k, a:b], xl[:, k, a:b]),
                          k == 0, k == KT - 1)
    return mm


TOKEN_TILES = BLOCKS + 1
TURN_BATCHES = [(0, 3), (3, 6), (6, 9)]


def tile_tokens(n):
    return (P * n, P * n + P) if n < BLOCKS else (SEQ, TOK)


def retention_projection_stage(core, at, w_in, w_small, xh, xl, ident, q_t, k_t, gate_t, k_tok, v_tok,
                               x_ready, room):
    k_decay, k_decay_dec = w_small
    tag = "rp_"
    m = Layout(core.nc, at)
    stage, w_hi, w_lo = weight_buffers(m, tag)
    k_turn = m.put(tag + "k_turn", [P, TOK])
    v_turn = m.put(tag + "v_turn", [P, TOK])
    Q, K, V, GATE = range(4)
    TILES = 4 * PAIRS
    sem = lambda n: core.semaphore(tag + n)
    proj_ps, turn_ps = core.banks[0:4], core.banks[4:7]
    staged = [sem(f"staged{s}") for s in range(2)]
    hi_done, lo_done = sem("hi_done"), sem("lo_done")
    proj_done = sem("proj_done")
    proj_free = sem("proj_free")
    turned = sem("turned")
    turn_free = sem("turn_free")
    k_copied = sem("k_copied")
    zeroed = sem("zeroed")
    def sync_early(sp):
        sp.wait_ge(*room)
        for s in range(2):
            sp.dma_start(stage[:, s, :], w_in[s]).then_inc(staged[s], 16)

    def sync(sp):
        with sp.Fori(1, TILES // 2) as i:
            for s in range(2):
                sp.wait_ge(lo_done, 2 * i + s - 1)
                sp.dma_start(stage[:, s, :], w_in[bass.ds(2 * i + s, 1), :, :].rearrange("a p n -> (a p) n")).then_inc(staged[s], 16)

    def round_tile(act, t, j):
        act.wait_ge(staged[j % 2], 32 * t + 16 * (j // 2) + 16)
        act.activation(w_hi[j % 2][:, :], stage[:, j % 2, :], ACT.Copy).then_inc(hi_done, 1)

    def scalar_early(act):
        act.sem_inc(proj_free, 4)
        round_tile(act, 0, 0)

    def scalar(act):
        def evacuate(t, j):
            if j == K:
                act.wait_ge(turned, 6 * t + 3)
                act.wait_ge(k_copied, 3 + 3 * t)
            if j == V:
                act.wait_ge(turned, 6 * t + 6)
            for c, (a, b) in enumerate(CHUNKS):
                act.wait_ge(proj_done, 3 + 12 * t + 3 * j + c + 1)
                ps = proj_ps[(3 * j + c) % 4][:, 0:b - a]
                if j == Q:
                    out, func = q_t[:, bass.ds(t, 1), a:b].rearrange("p o n -> p (o n)"), ACT.Copy
                elif j == K:
                    out, func = k_turn[:, a:b], ACT.Copy
                elif j == V:
                    out, func = v_turn[:, a:b], ACT.Copy
                else:
                    out, func = gate_t[:, bass.ds(t, 1), a:b].rearrange("p o n -> p (o n)"), ACT.Silu
                act.activation(out, ps, func).then_inc(proj_free, 1)

        def step(t, last):
            for j in range(4):
                if not (last and j == GATE):
                    act.wait_ge(proj_done, 3 + 12 * t + 3 * j)
                    round_tile(act, t + (j + 1) // 4, (j + 1) % 4)
                evacuate(t, j)

        with act.Fori(0, PAIRS - 1) as t:
            step(t, False)
        step(PAIRS - 1, True)

    def split(pool, t, j):
        pool.wait_ge(hi_done, 4 * t + j + 1)
        pool.tensor_tensor(w_lo[j % 2][:, :], stage[:, j % 2, :], w_hi[j % 2][:, :].bitcast(F32),
                           ALU.subtract).then_inc(lo_done, 1)

    def gpsimd_early(pool):
        pool.sem_inc(k_copied, 3)
        split(pool, 0, 0)
        pool.memset(k_tok[:, BLOCKS, :], 0.0).then_inc(zeroed, 1)
        pool.memset(v_tok[:, BLOCKS, :], 0.0).then_inc(zeroed, 1)

    def gpsimd(pool):
        def step(t, last):
            for j in range(4):
                if not (last and j == GATE):
                    split(pool, t + (j + 1) // 4, (j + 1) % 4)
                if j == K:
                    for c, (a, b) in enumerate(CHUNKS):
                        pool.wait_ge(proj_free, 4 + 12 * t + 3 * K + c + 1)
                        pool.tensor_copy(k_t[:, bass.ds(t, 1), a:b].rearrange("p o n -> p (o n)"),
                                         k_turn[:, a:b]).then_inc(k_copied, 1)

        with pool.Fori(0, PAIRS - 1) as t:
            step(t, False)
        step(PAIRS - 1, True)

    def tensor(pe):
        pe.sem_inc(turned, 6)
        pe.sem_inc(proj_done, 3)
        pe.wait_ge(x_ready, len(CHUNKS))

        def project(t, j):
            pe.wait_ge(lo_done, 4 * t + j + 1)
            for c, (a, b) in enumerate(CHUNKS):
                pe.wait_ge(proj_free, 12 * t + 3 * j + c + 1)
                project_tile(pe, proj_ps[(3 * j + c) % 4], w_hi[j % 2], w_lo[j % 2], xh, xl, a, b)\
                    .then_inc(proj_done, 1)

        def turn(t, src, j):
            pe.wait_ge(proj_free, 4 + 12 * t + 3 * j + 3)
            for n, (u0, u1) in enumerate(TURN_BATCHES):
                pe.wait_ge(turn_free, 6 * t + 3 * (j - K) + n + 1)
                for u in range(u0, u1):
                    a, b = tile_tokens(u)
                    mm = pe.transpose(turn_ps[n][0:b - a, P * (u - u0):P * (u - u0) + P],
                                      src[:, a:b], ident[:, :])
                mm.then_inc(turned, 1)

        def step(t):
            project(t, Q)
            project(t, K)
            project(t, V)
            turn(t, k_turn, K)
            project(t, GATE)
            turn(t, v_turn, V)

        with pe.Fori(0, PAIRS) as t:
            step(t)

    def vector(dve):
        dve.sem_inc(turn_free, 3)
        dve.wait_ge(zeroed, 2)

        def step(t):
            for j in (K, V):
                for n, (u0, u1) in enumerate(TURN_BATCHES):
                    dve.wait_ge(turned, 6 + 6 * t + 3 * (j - K) + n + 1)
                    heads = bass.ds(t * P, P)
                    for u in range(u0, u1):
                        rows = P if u < BLOCKS else DEC
                        ps = turn_ps[n][0:rows, P * (u - u0):P * (u - u0) + P]
                        if j == V:
                            i = dve.tensor_copy(v_tok[0:rows, u, heads], ps)
                        else:
                            decay = (k_decay if u < BLOCKS else k_decay_dec)[0:rows, bass.ds(2 * t, 2)]
                            i = dve.tensor_tensor(
                                k_tok[0:rows, u, heads].rearrange("p (h n) -> p h n", h=2),
                                ps.rearrange("p (h n) -> p h n", h=2),
                                decay.unsqueeze(2).to_broadcast([rows, 2, HD]), ALU.mult)
                    i.then_inc(turn_free, 1)

        with dve.Fori(0, PAIRS) as t:
            step(t)

    return Stage(sync_early=sync_early, scalar_early=scalar_early, gpsimd_early=gpsimd_early,
                 sync=sync, scalar=scalar, gpsimd=gpsimd, tensor=tensor, vector=vector)


def retention_stage(core, at, tables, g_chunk, g_dec, state_in, q_t, k_t, k_tok, v_tok, state_out,
                    state_dec_out):
    tag = "rt_"
    m = Layout(core.nc, at)
    mask = m.put(tag + "mask", [P, 2, PAIRS, P])
    q_decay = m.put(tag + "q_decay", [P, PAIRS, P])
    mask_dec = m.put(tag + "mask_dec", [P, 2, PAIRS, DEC])
    q_decay_dec = m.put(tag + "q_decay_dec", [P, PAIRS, DEC])
    own = m.put(tag + "own", [P, DEC_BATCH])
    state_dec = m.put(tag + "state_dec", [P, PAIRS, DEC_BATCH, HD])
    v_own = m.put(tag + "v_own", [DEC, HEADS, DEC_BATCH, HD])
    q_dec = [m.put(f"{tag}q_dec{i}", [P, PAIRS, P]) for i in range(2)]
    probs = [m.put(f"{tag}probs{i}", [P, 2, PAIRS * P]) for i in range(2)]
    state = [m.put(f"{tag}state{i}", [P, PAIRS, HD]) for i in range(2)]
    LAST = BLOCKS
    sem = lambda n: core.semaphore(tag + n)
    score_ps, out_ps, kv_ps = [core.banks[0:2], core.banks[2:4]], core.banks[4:6], core.banks[6:8]
    tables_in, dec_in = sem("tables_in"), sem("dec_in")
    scored, masked, q_ready, kv_done, state_done, out_done, out_read, owned, stored, dec_state_done, \
        zeroed = map(sem, ("scored", "masked", "q_ready", "kv_done", "state_done", "out_done",
                           "out_read", "owned", "stored", "dec_state_done", "zeroed"))

    def tokens(n):
        a, b = tile_tokens(n)
        return a, b, b - a

    def head(t, h):
        return slice(HD * (2 * t + h), HD * (2 * t + h) + HD)

    def sync(sp):
        for buf, src in ((mask, tables["mask"]), (q_decay, tables["q_decay"]),
                         (mask_dec, tables["mask_dec"]), (q_decay_dec, tables["q_decay_dec"]),
                         (own, tables["own"])):
            sp.dma_start(buf[tuple(slice(None) for _ in buf.shape)], src).then_inc(tables_in, 16)
        sp.dma_start(state_dec[:, :, :, :], state_in).then_inc(dec_in, 16)
        sp.wait_ge(state_done, PAIRS * BLOCKS)
        sp.dma_start(state_out, state[(BLOCKS - 1) % 2][:, :, :]).then_inc(stored, 16)
        sp.wait_ge(dec_state_done, PAIRS)
        sp.dma_start(state_dec_out, state_dec[:, :, :, :]).then_inc(stored, 16)
        sp.wait_ge(stored, 32)

    def gpsimd(pool):
        pool.wait_ge(tables_in, 80)
        for n in range(LAST + 1):
            a, b, w = tokens(n)
            if n >= 2:
                pool.wait_ge(out_done, n - 1)
            decay = q_decay if n < LAST else q_decay_dec
            pool.tensor_tensor(q_dec[n % 2][:, :, 0:w], q_t[:, :, a:b], decay[:, :, :],
                               ALU.mult).then_inc(q_ready, 1)
            if n == 0:
                for hd in range(HEADS):
                    pool.tensor_tensor(
                        v_own[:, hd, :, :],
                        v_tok[0:DEC, LAST, HD * hd:HD * hd + HD].unsqueeze(1).to_broadcast([DEC, DEC_BATCH, HD]),
                        own[0:DEC, :].unsqueeze(2).to_broadcast([DEC, DEC_BATCH, HD]),
                        ALU.mult).then_inc(owned, 1)

    def tensor(pe):
        def scores(n):
            a, b, w = tokens(n)
            if n >= 2:
                pe.wait_ge(masked, 2 * (n - 1))
            for h in range(2):
                d = slice(HD * h, HD * h + HD)
                for t in range(PAIRS):
                    mm = pe.matmul(score_ps[n % 2][h][0:w, w * t:w * t + w], k_t[d, t, a:b], q_t[d, t, a:b],
                                   start=True, stop=True)
                mm.then_inc(scored, 1)

        def key_values(n):
            if n >= 2:
                pe.wait_ge(state_done, PAIRS * (n - 1))
            for t in range(PAIRS):
                for h in range(2):
                    mm = pe.matmul(kv_ps[n % 2][HD * h:HD * h + HD, HD * t:HD * t + HD],
                                   k_tok[:, n, head(t, h)], v_tok[:, n, head(t, h)], start=True, stop=True)
            mm.then_inc(kv_done, 1)

        def output(n):
            a, b, w = tokens(n)
            pe.wait_ge(masked, 2 * n + 2)
            if n == LAST:
                pe.wait_ge(zeroed, 1)
            if n >= 1:
                pe.wait_ge(out_read, 2 * n)
            if 1 <= n < LAST:
                pe.wait_ge(state_done, PAIRS * n)
            pe.wait_ge(q_ready, n + 1)
            if n == LAST:
                pe.wait_ge(dec_in, 16)
            for h in range(2):
                d = slice(HD * h, HD * h + HD)
                for t in range(PAIRS):
                    mm = pe.matmul(out_ps[h][d, w * t:w * t + w], v_tok[:, n, head(t, h)],
                                   probs[n % 2][:, h, w * t:w * t + w], start=True, stop=n == 0)
                    if n == LAST:
                        for s in range(DEC_BATCH):
                            i = slice(DEC_SEQ * s, DEC_SEQ * s + DEC_SEQ)
                            mm = pe.matmul(out_ps[h][d, w * t + i.start:w * t + i.stop],
                                           state_dec[d, t, s, :], q_dec[n % 2][d, t, i],
                                           start=False, stop=s == DEC_BATCH - 1)
                    elif n >= 1:
                        mm = pe.matmul(out_ps[h][d, w * t:w * t + w], state[(n - 1) % 2][d, t, :],
                                       q_dec[n % 2][d, t, 0:w], start=False, stop=True)
            mm.then_inc(out_done, 1)

        pe.wait_ge(tables_in, 80)
        scores(0)
        for n in range(LAST + 1):
            if n < LAST:
                scores(n + 1)
                key_values(n)
            output(n)
        for t in range(PAIRS):
            if t < 2:
                pe.wait_ge(state_done, PAIRS * BLOCKS)
            else:
                pe.wait_ge(dec_state_done, t - 1)
            pe.wait_ge(owned, 2 * t + 2)
            for h in range(2):
                mm = pe.matmul(kv_ps[t % 2][HD * h:HD * h + HD, :], k_tok[0:DEC, LAST, head(t, h)],
                               v_own[:, 2 * t + h, :, :].rearrange("p b e -> p (b e)"), start=True, stop=True)
            mm.then_inc(kv_done, 1)

    def vector(dve):
        dve.wait_ge(tables_in, 80)
        for n in range(LAST + 1):
            a, b, w = tokens(n)
            if n == LAST:
                dve.wait_ge(out_done, n - 1)
                dve.memset(probs[n % 2][DEC:P, :, :], 0.0).then_inc(zeroed, 1)
            for h in range(2):
                dve.wait_ge(scored, 2 * n + h + 1)
                if n >= 2:
                    dve.wait_ge(out_done, n - 1)
                table = (mask if n < LAST else mask_dec)[0:w, h, :, :].rearrange("p t i -> p (t i)")
                dve.tensor_tensor(probs[n % 2][0:w, h, 0:w * PAIRS], score_ps[n % 2][h][0:w, 0:w * PAIRS],
                                  table, ALU.mult).then_inc(masked, 1)
            if n == LAST:
                break
            dve.wait_ge(kv_done, n + 1)
            if n >= 2:
                dve.wait_ge(out_done, n)
            for t in range(PAIRS):
                kv = kv_ps[n % 2][:, HD * t:HD * t + HD]
                if n == 0:
                    dve.tensor_copy(state[0][:, t, :], kv).then_inc(state_done, 1)
                else:
                    dve.wait_ge(state_done, PAIRS * (n - 1) + t + 1)
                    dve.scalar_tensor_tensor(state[n % 2][:, t, :], state[(n - 1) % 2][:, t, :],
                                             g_chunk[:, t:t + 1], kv, ALU.mult, ALU.add).then_inc(state_done, 1)
        dve.wait_ge(out_done, LAST + 1)
        for t in range(PAIRS):
            dve.wait_ge(kv_done, BLOCKS + t + 1)
            s = state_dec[:, t, :, :].rearrange("p b e -> p (b e)")
            dve.scalar_tensor_tensor(s, s, g_dec[:, t:t + 1], kv_ps[t % 2][:, :], ALU.mult, ALU.add)\
               .then_inc(dec_state_done, 1)

    def scalar(act):
        for n in range(LAST + 1):
            a, b, w = tokens(n)
            act.wait_ge(out_done, n + 1)
            act.wait_ge(q_ready, n + 1)
            for h in range(2):
                d = slice(HD * h, HD * h + HD)
                act.activation(q_t[d, :, a:b], out_ps[h][d, 0:w * PAIRS].rearrange("p (t i) -> p t i", i=w),
                               ACT.Copy).then_inc(out_read, 1)

    return Stage(sync=sync, gpsimd=gpsimd, tensor=tensor, vector=vector, scalar=scalar)


def group_norm_stage(core, at, gn_sum, gn_spread, ones_head, eps, gn_w, o_t, gate_t, mix_hi, mix_lo):
    tag = "gn_"
    m = Layout(core.nc, at)
    sum_w = m.put(tag + "sum_w", [P, PAIRS, HEADS])
    spread_w = m.put(tag + "spread_w", [HEADS, PAIRS, P])
    squares = [m.put(f"{tag}squares{i}", [P, PAIRS, CW]) for i in range(2)]
    rstd = [m.put(f"{tag}rstd{i}", [HEADS, CW]) for i in range(2)]
    sem = lambda n: core.semaphore(tag + n)
    mean_ps, var_ps, spread_ps = core.banks[0:2], core.banks[2:4], core.banks[4:8]
    tables_in, mean_done, centred, squared, var_done, std_done, rstd_done, spread_done, scaled, \
        gated, hi_done, lo_done = map(sem, (
            "tables_in", "mean_done", "centred", "squared", "var_done", "std_done", "rstd_done",
            "spread_done", "scaled", "gated", "hi_done", "lo_done"))
    N = len(CHUNKS)
    def sync(sp):
        sp.dma_start(sum_w[:, :, :], gn_sum).then_inc(tables_in, 16)
        sp.dma_start(spread_w[:, :, :], gn_spread).then_inc(tables_in, 16)
        sp.wait_ge(tables_in, 32)

    def tensor(pe):
        def means(c):
            a, b = CHUNKS[c]
            for t in range(PAIRS):
                u = PAIRS * c + t
                if u >= 2:
                    pe.wait_ge(centred, u - 1)
                pe.matmul(mean_ps[u % 2][:, 0:b - a], ones_head[:, :], o_t[:, t, a:b],
                          start=True, stop=True).then_inc(mean_done, 1)

        def variance(c):
            a, b = CHUNKS[c]
            pe.wait_ge(squared, c + 1)
            if c >= 2:
                pe.wait_ge(std_done, c - 1)
            for t in range(PAIRS):
                mm = pe.matmul(var_ps[c % 2][0:HEADS, 0:b - a], sum_w[:, t, :], squares[c % 2][:, t, 0:b - a],
                               start=t == 0, stop=t == PAIRS - 1)
            mm.then_inc(var_done, 1)

        def spread(c):
            a, b = CHUNKS[c]
            pe.wait_ge(rstd_done, c + 1)
            for t in range(PAIRS):
                if c:
                    pe.wait_ge(scaled, PAIRS * (c - 1) + t + 1)
                pe.matmul(spread_ps[t][:, 0:b - a], spread_w[:, t, :], rstd[c % 2][:, 0:b - a],
                          start=True, stop=True).then_inc(spread_done, 1)

        pe.wait_ge(tables_in, 32)
        means(0)
        for c in range(N):
            if c + 1 < N:
                means(c + 1)
            variance(c)
            spread(c)

    def vector(dve):
        def centre(c):
            a, b = CHUNKS[c]
            for t in range(PAIRS):
                dve.wait_ge(mean_done, PAIRS * c + t + 1)
                dve.tensor_tensor(o_t[:, t, a:b], o_t[:, t, a:b], mean_ps[(PAIRS * c + t) % 2][:, 0:b - a],
                                  ALU.subtract).then_inc(centred, 1)

        def invert(c):
            a, b = CHUNKS[c]
            dve.wait_ge(std_done, c + 1)
            r = rstd[c % 2][:, 0:b - a]
            dve.reciprocal(r, r).then_inc(rstd_done, 1)

        def gate(c):
            a, b = CHUNKS[c]
            for t in range(PAIRS):
                dve.wait_ge(spread_done, PAIRS * c + t + 1)
                dve.wait_ge(centred, PAIRS * c + t + 1)
                dve.wait_ge(squared, c + 1)
                dve.scalar_tensor_tensor(o_t[:, t, a:b], o_t[:, t, a:b], gn_w[:, t:t + 1],
                                         spread_ps[t][:, 0:b - a], ALU.mult, ALU.mult).then_inc(scaled, 1)
            for t in range(PAIRS):
                dve.wait_ge(scaled, PAIRS * c + t + 1)
                dve.tensor_tensor(o_t[:, t, a:b], o_t[:, t, a:b], gate_t[:, t, a:b],
                                  ALU.mult).then_inc(gated, 1)

        centre(0)
        for c in range(N):
            if c + 1 < N:
                centre(c + 1)
            invert(c)
            gate(c)

    def scalar(act):
        def square(c):
            a, b = CHUNKS[c]
            act.wait_ge(centred, PAIRS * c + PAIRS)
            if c >= 2:
                act.wait_ge(var_done, c - 1)
            act.activation(squares[c % 2][:, :, 0:b - a], o_t[:, :, a:b], ACT.Square).then_inc(squared, 1)

        def deviation(c):
            a, b = CHUNKS[c]
            act.wait_ge(var_done, c + 1)
            if c >= 2:
                act.wait_ge(spread_done, PAIRS * (c - 1))
            act.activation(rstd[c % 2][:, 0:b - a], var_ps[c % 2][0:HEADS, 0:b - a], ACT.Sqrt,
                           bias=eps[0:HEADS, 0:1]).then_inc(std_done, 1)

        def round_mix(c):
            a, b = CHUNKS[c]
            act.wait_ge(gated, PAIRS * c + PAIRS)
            act.activation(mix_hi[:, 0:PAIRS, a:b], o_t[:, :, a:b], ACT.Copy).then_inc(hi_done, 1)

        square(0)
        for c in range(N):
            deviation(c)
            if c + 1 < N:
                square(c + 1)
            round_mix(c)

    def gpsimd(pool):
        for c, (a, b) in enumerate(CHUNKS):
            pool.wait_ge(hi_done, c + 1)
            pool.tensor_tensor(mix_lo[:, 0:PAIRS, a:b], o_t[:, :, a:b], mix_hi[:, 0:PAIRS, a:b].bitcast(F32),
                               ALU.subtract).then_inc(lo_done, 1)

    return Stage(sync=sync, tensor=tensor, vector=vector, scalar=scalar, gpsimd=gpsimd)


def attention_projection_stage(core, at, w_in, xh, xl, ident, q_t, k_t, v_tok):
    tag = "ap_"
    m = Layout(core.nc, at)
    stage, w_hi, w_lo = weight_buffers(m, tag)
    v_turn = m.put(tag + "v_turn", [P, TOK])
    K, V = PAIRS, PAIRS + 1
    TILES = PAIRS + 2
    sem = lambda n: core.semaphore(tag + n)
    ps, turn_ps = core.banks[0:6], core.banks[6:8]
    staged = [sem(f"staged{s}") for s in range(2)]
    hi_done, lo_done = sem("hi_done"), sem("lo_done")
    proj_done = sem("proj_done")
    proj_free = sem("proj_free")
    turned, turn_free, zeroed = sem("turned"), sem("turn_free"), sem("zeroed")
    def sync(sp):
        for s in range(2):
            sp.dma_start(stage[:, s, :], w_in[s]).then_inc(staged[s], 16)
        with sp.Fori(1, TILES // 2) as i:
            for s in range(2):
                sp.wait_ge(lo_done, 2 * i + s - 1)
                sp.dma_start(stage[:, s, :], w_in[bass.ds(2 * i + s, 1), :, :].rearrange("a p n -> (a p) n")).then_inc(staged[s], 16)

    def scalar(act):
        act.sem_inc(proj_free, 6)

        def round_tile(i, s):
            act.wait_ge(staged[s], 16 * i + 16)
            act.activation(w_hi[s][:, :], stage[:, s, :], ACT.Copy).then_inc(hi_done, 1)

        def evacuate(tile, s, out):
            for c, (a, b) in enumerate(CHUNKS):
                act.wait_ge(proj_done, 3 + 3 * tile + c + 1)
                act.activation(out(a, b), ps[3 * s + c][:, 0:b - a], ACT.Copy).then_inc(proj_free, 1)

        round_tile(0, 0)
        with act.Fori(0, PAIRS // 2) as i:
            for s in range(2):
                act.wait_ge(proj_done, 3 + 6 * i + 3 * s)
                round_tile(i + s, 1 - s)
                evacuate(2 * i + s, s,
                         lambda a, b: q_t[:, bass.ds(2 * i + s, 1), a:b].rearrange("p o n -> p (o n)"))
        act.wait_ge(proj_done, 3 + 3 * K)
        round_tile(PAIRS // 2, 1)
        evacuate(K, 0, lambda a, b: k_t[:, a:b])
        evacuate(V, 1, lambda a, b: v_turn[:, a:b])

    def gpsimd(pool):
        pool.memset(v_tok[:, BLOCKS, :], 0.0).then_inc(zeroed, 1)
        with pool.Fori(0, TILES // 2) as i:
            for s in range(2):
                pool.wait_ge(hi_done, 2 * i + s + 1)
                pool.tensor_tensor(w_lo[s][:, :], stage[:, s, :], w_hi[s][:, :].bitcast(F32),
                                   ALU.subtract).then_inc(lo_done, 1)

    def tensor(pe):
        pe.sem_inc(proj_done, 3)
        with pe.Fori(0, TILES // 2) as i:
            for s in range(2):
                pe.wait_ge(lo_done, 2 * i + s + 1)
                for c, (a, b) in enumerate(CHUNKS):
                    pe.wait_ge(proj_free, 6 * i + 3 * s + c + 1)
                    project_tile(pe, ps[3 * s + c], w_hi[s], w_lo[s], xh, xl, a, b).then_inc(proj_done, 1)
        pe.wait_ge(proj_free, 6 + 3 * TILES)
        for n, (u0, u1) in enumerate(TURN_BATCHES):
            if n == 2:
                pe.wait_ge(turn_free, 1)
            for u in range(u0, u1):
                a, b = tile_tokens(u)
                mm = pe.transpose(turn_ps[n % 2][0:b - a, P * (u - u0):P * (u - u0) + P], v_turn[:, a:b],
                                  ident[:, :])
            mm.then_inc(turned, 1)

    def vector(dve):
        dve.wait_ge(zeroed, 1)
        for n, (u0, u1) in enumerate(TURN_BATCHES):
            dve.wait_ge(turned, n + 1)
            for u in range(u0, u1):
                rows = P if u < BLOCKS else DEC
                i = dve.tensor_copy(v_tok[0:rows, u, :], turn_ps[n % 2][0:rows, P * (u - u0):P * (u - u0) + P])
            i.then_inc(turn_free, 1)

    return Stage(sync=sync, scalar=scalar, gpsimd=gpsimd, tensor=tensor, vector=vector)


def attention_stage(core, at, at_caches, tables, sinks, sinks_dec, caches, q_t, k_t, v_tok, ident,
                    mix_hi, mix_lo, outs):
    tag = "at_"
    m = Layout(core.nc, at)
    bias = m.put(tag + "bias", [P, KVH, GROUP, 2 * P])
    bias_dec = m.put(tag + "bias_dec", [P, KVH, 2, P + DEC])
    SLOTS = 3
    scores = [m.put(f"{tag}scores{i}", [P, GROUP * 2 * P]) for i in range(SLOTS)]
    turned = [m.put(f"{tag}turned{i}", [P, GROUP * P]) for i in range(2)]
    stats = [m.put(f"{tag}stats{i}", [P, 6, GROUP]) for i in range(SLOTS)]
    turned_new = m.put(tag + "turned_new", [P, 2 * P])
    q_rows = m.put(tag + "q_rows", [P, DEC_BATCH, GROUP, DEC_SEQ])
    TOP, NEG, SUM, SINK, DEN, INV = range(6)
    mc = Layout(core.nc, at_caches)
    k_cache = mc.put(tag + "k_cache", [P, DEC_BATCH, WINDOW])
    v_cache = mc.put(tag + "v_cache", [P, DEC_BATCH, P])
    ITEMS = [(n, h) for n in range(BLOCKS + 1) for h in range(KVH)]
    LAST = len(ITEMS)
    KEYS = P + DEC
    sem = lambda n: core.semaphore(tag + n)
    score_ps, turn_ps, out_ps = [core.banks[0:2], core.banks[2:4]], core.banks[4:6], core.banks[6:8]
    tables_in, dec_in, scored, biased, maxed, topped, negated, sunk, exped, sink_exped, summed, inverted, \
        normed, turn_done, turn_read, out_done, hi_done, lo_done, stored, cached, q_ordered = map(sem, (
            "tables_in", "dec_in", "scored", "biased", "maxed", "topped", "negated", "sunk",
            "exped", "sink_exped", "summed", "inverted", "normed", "turn_done", "turn_read",
            "out_done", "hi_done", "lo_done", "stored", "cached", "q_ordered"))

    def shape(i):
        n, h = ITEMS[i]
        if n == BLOCKS:
            return 2, 0, KEYS
        return GROUP, (P if n == 0 else 0), 2 * P

    def scores_of(i):
        n, h = ITEMS[i]
        groups, k0, k1 = shape(i)
        width = KEYS if n == BLOCKS else 2 * P
        return scores[i % SLOTS][:, 0:groups * width].rearrange("p (g k) -> p g k", g=groups)[:, :, k0:k1]

    def per_group(i, what):
        return stats[i % SLOTS][:, what, 0:shape(i)[0]]

    def sinks_of(i):
        n, h = ITEMS[i]
        if n == BLOCKS:
            return sinks_dec[:, h:h + 1].to_broadcast([P, 2])
        return sinks[:, GROUP * h:GROUP * h + GROUP]

    def sync(sp):
        sp.dma_start(bias[:, :, :, :], tables["bias"]).then_inc(tables_in, 16)
        sp.dma_start(bias_dec[:, :, :, :], tables["bias_dec"]).then_inc(tables_in, 16)
        sp.dma_start(k_cache[:, :, :], caches["k"]).then_inc(dec_in, 16)
        sp.dma_start(v_cache[:, :, :], caches["v"]).then_inc(dec_in, 16)
        sp.dma_start(outs["k_prompt"], k_t[:, SEQ - WINDOW:SEQ]).then_inc(stored, 16)
        sp.dma_start(outs["v_prompt"], v_tok[:, BLOCKS - 1, :]).then_inc(stored, 16)
        sp.dma_start(outs["k_dec"][:, :, WINDOW - DEC_SEQ:WINDOW],
                     k_t[:, SEQ:TOK].rearrange("p (b i) -> p b i", i=DEC_SEQ)).then_inc(stored, 16)
        for s in range(DEC_BATCH):
            sp.dma_start(outs["v_dec"][s, WINDOW - DEC_SEQ:WINDOW, :],
                         v_tok[DEC_SEQ * s:DEC_SEQ * s + DEC_SEQ, BLOCKS, :]).then_inc(stored, 16)
        sp.wait_ge(dec_in, 32)
        sp.dma_start(outs["k_dec"][:, :, 0:WINDOW - DEC_SEQ], k_cache[:, :, DEC_SEQ:WINDOW]).then_inc(stored, 16)
        sp.dma_start(outs["v_dec"][:, 0:WINDOW - DEC_SEQ, :].rearrange("b k n -> k b n"),
                     v_cache[DEC_SEQ:WINDOW, :, :]).then_inc(stored, 16)
        sp.wait_ge(stored, 16 * (5 + DEC_BATCH))

    def tensor(pe):
        def score(i):
            n, h = ITEMS[i]
            d = slice(HD * h, HD * h + HD)
            if i >= 2:
                pe.wait_ge(biased, i - 1)
            if n == BLOCKS:
                pe.wait_ge(dec_in, 32)
                pe.wait_ge(q_ordered, GROUP)
                for s in range(DEC_BATCH):
                    rows = slice(32 * (s % 4), 32 * (s % 4) + 32)
                    half = KEYS * (s // 4)
                    q = q_rows[d, s, :, :].rearrange("p t i -> p (t i)")
                    pe.matmul(score_ps[i % 2][0][rows, half:half + P], q, k_cache[d, s, :], start=True, stop=True)
                    mm = pe.matmul(score_ps[i % 2][0][rows, half + P:half + KEYS], q, k_t[d, SEQ:TOK],
                                   start=True, stop=True)
            else:
                k0 = P if n == 0 else 0
                for t in range(GROUP):
                    col = 2 * P * (t % 2)
                    mm = pe.matmul(score_ps[i % 2][t // 2][:, col + k0:col + 2 * P],
                                   q_t[d, t, P * n:P * n + P], k_t[d, P * (n - 1) + k0:P * (n + 1)],
                                   start=True, stop=True)
            mm.then_inc(scored, 1)

        def transposes(i):
            n, h = ITEMS[i]
            pe.wait_ge(normed, i + 1)
            if i:
                pe.wait_ge(turn_read, 2 * i)
            p = scores[i % SLOTS]
            if n == BLOCKS:
                for half in range(2):
                    pe.transpose(turn_ps[0][:, P * half:P * half + P], p[:, KEYS * half:KEYS * half + P], ident[:, :])
                for half in range(2):
                    mm = pe.transpose(turn_ps[1][0:DEC, P * half:P * half + P],
                                      p[:, KEYS * half + P:KEYS * half + KEYS], ident[:, :])
            else:
                for kb in range(1 if n == 0 else 0, 2):
                    for t in range(GROUP):
                        mm = pe.transpose(turn_ps[kb][:, P * t:P * t + P],
                                          p[:, P * (2 * t + kb):P * (2 * t + kb) + P], ident[:, :])
            mm.then_inc(turn_done, 1)

        def output(i):
            n, h = ITEMS[i]
            d = slice(HD * h, HD * h + HD)
            pe.wait_ge(turn_read, 2 * i + 2)
            if i >= 2:
                pe.wait_ge(lo_done, i - 1)
            if n == BLOCKS:
                for half in range(2):
                    mm = pe.matmul(out_ps[h][d, P * half:P * half + P], v_tok[:, BLOCKS, d],
                                   turned_new[:, P * half:P * half + P], start=True, stop=False)
                    for s in range(4 * half, 4 * half + 4):
                        col = slice(32 * s, 32 * s + 32)
                        mm = pe.matmul(out_ps[h][d, col], v_cache[:, s, d], turned[0][:, col],
                                       start=False, stop=s % 4 == 3)
            else:
                first = 1 if n == 0 else 0
                for kb in range(first, 2):
                    mm = pe.matmul(out_ps[h][d, :], v_tok[:, n - 1 + kb, d], turned[kb][:, :],
                                   start=kb == first, stop=kb == 1)
            mm.then_inc(out_done, 1)

        for i in range(SLOTS):
            score(i)
        for i in range(LAST + 1):
            if i < LAST:
                transposes(i)
            if i + SLOTS < LAST:
                score(i + SLOTS)
            if i:
                output(i - 1)

    def vector(dve):
        dve.wait_ge(tables_in, 32)

        def add_bias(i):
            n, h = ITEMS[i]
            groups, k0, k1 = shape(i)
            dve.wait_ge(scored, i + 1)
            if i >= SLOTS:
                dve.wait_ge(turn_done, i - SLOTS + 1)
            out = scores_of(i)
            if n == BLOCKS:
                ps = score_ps[i % 2][0][:, 0:2 * KEYS].rearrange("p (g k) -> p g k", g=2)
                dve.scalar_tensor_tensor(out, ps, QSCALE, bias_dec[:, h, :, :], ALU.mult, ALU.add)\
                   .then_inc(biased, 1)
            else:
                for j in range(2):
                    ps = score_ps[i % 2][j][:, :].rearrange("p (g k) -> p g k", g=2)[:, :, k0:k1]
                    x = dve.scalar_tensor_tensor(out[:, 2 * j:2 * j + 2, :], ps, QSCALE,
                                                 bias[:, h, 2 * j:2 * j + 2, k0:k1], ALU.mult, ALU.add)
                x.then_inc(biased, 1)

        def top(i):
            dve.wait_ge(biased, i + 1)
            if i >= SLOTS:
                dve.wait_ge(normed, i - SLOTS + 1)
            dve.tensor_reduce(per_group(i, TOP), scores_of(i), AX.X, ALU.max).then_inc(maxed, 1)
            dve.wait_ge(maxed, i + 1)
            dve.tensor_tensor(per_group(i, TOP), per_group(i, TOP), sinks_of(i), ALU.max).then_inc(topped, 1)
            dve.wait_ge(topped, i + 1)
            dve.tensor_tensor(per_group(i, SINK), sinks_of(i), per_group(i, TOP), ALU.subtract).then_inc(sunk, 1)
            dve.tensor_scalar(per_group(i, NEG), per_group(i, TOP), -1.0, None, ALU.mult).then_inc(negated, 1)

        def denominator(i):
            dve.wait_ge(sink_exped, i + 1)
            dve.tensor_tensor(per_group(i, DEN), per_group(i, SUM), per_group(i, SINK), ALU.add).then_inc(summed, 1)
            dve.wait_ge(summed, i + 1)
            dve.reciprocal(per_group(i, INV), per_group(i, DEN)).then_inc(inverted, 1)

        def low_part(i):
            n, h = ITEMS[i]
            d = slice(HD * h, HD * h + HD)
            dve.wait_ge(hi_done, i + 1)
            if n == BLOCKS:
                for t in range(GROUP):
                    x = dve.tensor_tensor(
                        mix_lo[d, PAIRS + t, SEQ:TOK].rearrange("p (b i) -> p b i", i=DEC_SEQ),
                        out_ps[h][d, 0:2 * P].rearrange("p (b t i) -> p b t i", t=GROUP, i=DEC_SEQ)[:, :, t, :],
                        mix_hi[d, PAIRS + t, SEQ:TOK].rearrange("p (b i) -> p b i", i=DEC_SEQ).bitcast(F32),
                        ALU.subtract)
                x.then_inc(lo_done, 1)
            else:
                dve.tensor_tensor(mix_lo[d, PAIRS:2 * PAIRS, P * n:P * n + P],
                                  out_ps[h][d, :].rearrange("p (t q) -> p t q", t=GROUP),
                                  mix_hi[d, PAIRS:2 * PAIRS, P * n:P * n + P].bitcast(F32),
                                  ALU.subtract).then_inc(lo_done, 1)

        for i in range(-SLOTS, LAST + 1):
            if 0 <= i + SLOTS - 1 < LAST:
                denominator(i + SLOTS - 1)
            if i + SLOTS < LAST:
                add_bias(i + SLOTS)
                top(i + SLOTS)
            if i >= 1:
                low_part(i - 1)

    def scalar(act):
        def exponentials(i):
            n, h = ITEMS[i]
            act.wait_ge(negated, i + 1)
            s = scores_of(i)
            for g in range(shape(i)[0]):
                act.activation(s[:, g, :], s[:, g, :], ACT.Exp, bias=stats[i % SLOTS][:, NEG, g:g + 1],
                               accum_out=stats[i % SLOTS][:, SUM, g:g + 1]).then_inc(exped, 1)
            act.activation(per_group(i, SINK), per_group(i, SINK), ACT.Exp).then_inc(sink_exped, 1)

        def read_turned(i):
            n, h = ITEMS[i]
            act.wait_ge(turn_done, i + 1)
            if i:
                act.wait_ge(out_done, i)
            for kb in range(2):
                if n == 0 and kb == 0:
                    act.sem_inc(turn_read, 1)
                    continue
                rows = DEC if n == BLOCKS and kb == 1 else P
                cols = 2 * P if n == BLOCKS else GROUP * P
                if rows < P and h == 0:
                    act.wait_ge(cached, 1)
                to = turned_new if n == BLOCKS and kb == 1 else turned[kb]
                act.activation(to[0:rows, 0:cols], turn_ps[kb][0:rows, 0:cols], ACT.Copy)\
                   .then_inc(turn_read, 1)

        def high_part(i):
            n, h = ITEMS[i]
            d = slice(HD * h, HD * h + HD)
            act.wait_ge(out_done, i + 1)
            if n == BLOCKS:
                for t in range(GROUP):
                    x = act.activation(
                        mix_hi[d, PAIRS + t, SEQ:TOK].rearrange("p (b i) -> p b i", i=DEC_SEQ),
                        out_ps[h][d, 0:2 * P].rearrange("p (b t i) -> p b t i", t=GROUP, i=DEC_SEQ)[:, :, t, :],
                        ACT.Copy)
                x.then_inc(hi_done, 1)
            else:
                act.activation(mix_hi[d, PAIRS:2 * PAIRS, P * n:P * n + P],
                               out_ps[h][d, :].rearrange("p (t q) -> p t q", t=GROUP), ACT.Copy).then_inc(hi_done, 1)

        for i in range(SLOTS):
            exponentials(i)
        for i in range(LAST + 1):
            if i < LAST:
                read_turned(i)
            if i + SLOTS < LAST:
                exponentials(i + SLOTS)
            if i:
                high_part(i - 1)

    def gpsimd(pool):
        for t in range(GROUP):
            pool.tensor_copy(q_rows[:, :, t, :], q_t[:, t, SEQ:TOK].rearrange("p (b i) -> p b i", i=DEC_SEQ))\
                .then_inc(q_ordered, 1)
        pool.memset(turned_new[:, :], 0.0).then_inc(cached, 1)
        for i in range(LAST):
            n, h = ITEMS[i]
            groups, k0, k1 = shape(i)
            pool.wait_ge(inverted, i + 1)
            s = scores_of(i)
            pool.tensor_tensor(s, s, per_group(i, INV).unsqueeze(2).to_broadcast([P, groups, k1 - k0]),
                               ALU.mult).then_inc(normed, 1)

    return Stage(sync=sync, tensor=tensor, vector=vector, scalar=scalar, gpsimd=gpsimd)


def output_projection_stage(core, at, w_out, mix_hi, mix_lo, xh, xl, acc):
    tag = "op_"
    m = Layout(core.nc, at)
    stage, w_hi, w_lo = weight_buffers(m, tag)
    sem = lambda n: core.semaphore(tag + n)
    ps = core.banks[0:6]
    staged = [sem(f"staged{s}") for s in range(2)]
    hi_done, lo_done = sem("hi_done"), sem("lo_done")
    proj_done = sem("proj_done")
    proj_free = sem("proj_free")
    summed = sem("summed")
    def sync(sp):
        for s in range(2):
            sp.dma_start(stage[:, s, :], w_out[s]).then_inc(staged[s], 16)
        with sp.Fori(1, KT // 2) as i:
            for s in range(2):
                sp.wait_ge(lo_done, 2 * i + s - 1)
                sp.dma_start(stage[:, s, :], w_out[bass.ds(2 * i + s, 1), :, :].rearrange("a p n -> (a p) n")).then_inc(staged[s], 16)

    def scalar(act):
        act.wait_ge(staged[0], 16)
        act.activation(w_hi[0][:, :], stage[:, 0, :], ACT.Copy).then_inc(hi_done, 1)
        act.wait_ge(staged[1], 16)
        act.activation(w_hi[1][:, :], stage[:, 1, :], ACT.Copy).then_inc(hi_done, 1)
        with act.Fori(1, KT // 2) as i:
            for s in range(2):
                act.wait_ge(staged[s], 16 * i + 16)
                act.wait_ge(proj_done, 6 * i + 3 * s - 3)
                act.activation(w_hi[s][:, :], stage[:, s, :], ACT.Copy).then_inc(hi_done, 1)

    def gpsimd(pool):
        with pool.Fori(0, KT // 2) as i:
            for s in range(2):
                pool.wait_ge(hi_done, 2 * i + s + 1)
                pool.tensor_tensor(w_lo[s][:, :], stage[:, s, :], w_hi[s][:, :].bitcast(F32),
                                   ALU.subtract).then_inc(lo_done, 1)

    def tensor(pe):
        with pe.Fori(0, KT // 2) as i:
            for s in range(2):
                pe.wait_ge(lo_done, 2 * i + s + 1)
                for c, (a, b) in enumerate(CHUNKS):
                    pe.wait_ge(proj_free, 6 * i + 3 * s + c + 1)
                    project_tile(pe, ps[3 * s + c], w_hi[s], w_lo[s], mix_hi, mix_lo, a, b).then_inc(proj_done, 1)

    def vector(dve):
        dve.sem_inc(proj_free, 6)
        with dve.Fori(0, KT // 2) as i:
            for s in range(2):
                for c, (a, b) in enumerate(CHUNKS):
                    u = 6 * i + 3 * s + c
                    one = lambda t: t[:, bass.ds(2 * i + s, 1), a:b].rearrange("p o n -> p (o n)")
                    dve.wait_ge(proj_done, u + 1)
                    dve.scalar_tensor_tensor(one(acc), one(xh).bitcast(F32), ALPHA, ps[3 * s + c][:, 0:b - a],
                                             ALU.mult, ALU.add).then_inc(proj_free, 1)
                    dve.wait_ge(proj_free, 6 + u + 1)
                    dve.scalar_tensor_tensor(one(acc), one(xl).bitcast(F32), ALPHA, one(acc),
                                             ALU.mult, ALU.add).then_inc(summed, 1)

    return Stage(sync=sync, scalar=scalar, gpsimd=gpsimd, tensor=tensor, vector=vector,
                 products_done=(proj_done, len(CHUNKS) * KT), acc_ready=(summed, len(CHUNKS) * KT))


SMALL = {}
for _name, _width in (("ln_gain", 3 * KT), ("ln_bias", 3 * KT), ("gn_w", PAIRS), ("g_chunk", PAIRS),
                      ("g_dec", PAIRS), ("sinks", HEADS), ("sinks_dec", KVH), ("k_decay", HEADS),
                      ("k_decay_dec", HEADS), ("ident", P)):
    _at = sum(s.stop - s.start for s in SMALL.values())
    SMALL[_name] = slice(_at, _at + _width)
SMALL_W = SMALL["ident"].stop


def decoder_layer_kernel(nc, i, o):
    with ExitStack() as ctx:
        core = Core(
            nc=nc, semaphore=lambda name: ctx.enter_context(nc.semaphore(name)),
            banks=[ctx.enter_context(nc.psum_tensor(f"bank{n}", [P, 512], F32)) for n in range(8)])
        decoder_layer(core, i, o)


def one_stage_block(nc, stage):
    with nc.Block() as block:
        block.sync(stage.sync)
        block.tensor(stage.tensor)
        block.vector(stage.vector)
        block.scalar(stage.scalar)
        block.gpsimd(stage.gpsimd)


def decoder_layer(core, i, o):
    nc = core.nc
    base = Layout(nc, -(-nc.sbuf_base // 32) * 32)
    xh = base.put("x_hi", [P, KT, TOK], F32R)
    xl = base.put("x_lo", [P, KT, TOK], F32R)
    small = base.put("small", [P, SMALL_W])
    ones_mean = base.put("ones_mean", [P, P])
    ones_head = base.put("ones_head", [P, P])
    eps = base.put("eps", [P, 1])
    part = lambda name: small[:, SMALL[name]]
    ident = part("ident")
    mixer_at = base.at
    acc = base.put("acc", [P, KT, TOK])
    free = base.at

    gain = lambda n: small[:, SMALL["ln_gain"].start + KT * n:SMALL["ln_gain"].start + KT * n + KT]
    shift = lambda n: small[:, SMALL["ln_bias"].start + KT * n:SMALL["ln_bias"].start + KT * n + KT]

    m = Layout(nc, mixer_at)
    ret_q = m.put("ret_q", [P, PAIRS, TOK])
    ret_gate = m.put("ret_gate", [P, PAIRS, TOK])
    m = Layout(nc, free)
    ret_k = m.put("ret_k", [P, PAIRS, TOK])
    ret_k_tok = m.put("ret_k_tok", [P, TOKEN_TILES, HEADS * HD])
    ret_v_tok = m.put("ret_v_tok", [P, TOKEN_TILES, HEADS * HD])
    ret_at = m.at
    m = Layout(nc, free)
    mix_hi = m.put("mix_hi", [P, KT, TOK], F32R)
    mix_lo = m.put("mix_lo", [P, KT, TOK], F32R)
    mix_end = m.at
    m = Layout(nc, mixer_at)
    att_q = m.put("att_q", [P, PAIRS, TOK])
    att_k = m.put("att_k", [P, TOK])
    att_v_tok = m.put("att_v_tok", [P, TOKEN_TILES, P])
    caches_at = m.at

    load = load_stage(core, i["x"], i["small"], small, ones_mean, ones_head, eps, acc, xh, xl)
    ffn1 = ffn_stage(core, "f1_", free, i["ffn1"], acc, xh, xl, load.x_ready, load.acc_ready)
    norm1 = norm_stage(core, "n1_", ffn1.end, 0.5, acc, gain(0), shift(0), ones_mean, eps, xh, xl,
                       acc_ready=ffn1.acc_ready)
    ret_proj = retention_projection_stage(core, ret_at, i["w_ret"], (part("k_decay"), part("k_decay_dec")), xh, xl,
                                          ident, ret_q, ret_k, ret_gate, ret_k_tok, ret_v_tok,
                                          norm1.x_ready, ffn1.products_done)
    with nc.Block() as block:

        @block.sync
        def _(sp):
            load.sync_x(sp, 0)
            ffn1.sync_early(sp)
            load.sync_x(sp, 1)
            load.sync_x(sp, 2)
            load.sync_small(sp)
            ffn1.sync(sp)
            ret_proj.sync_early(sp)
            ret_proj.sync(sp)

        @block.gpsimd
        def _(pool):
            load.gpsimd(pool)
            ffn1.gpsimd_early(pool)
            ffn1.gpsimd(pool)
            ret_proj.gpsimd_early(pool)
            norm1.gpsimd(pool)
            ret_proj.gpsimd(pool)

        @block.scalar
        def _(act):
            load.scalar(act, 0)
            ffn1.scalar_early(act)
            load.scalar(act, 1)
            load.scalar(act, 2)
            ffn1.scalar(act)
            ret_proj.scalar_early(act)
            norm1.scalar(act)
            ret_proj.scalar(act)

        @block.vector
        def _(dve):
            load.vector(dve)
            ffn1.vector(dve)
            norm1.vector(dve)
            ret_proj.vector(dve)

        @block.tensor
        def _(pe):
            ffn1.tensor(pe)
            norm1.tensor(pe)
            ret_proj.tensor(pe)

    one_stage_block(nc, retention_stage(core, ret_at, i, part("g_chunk"), part("g_dec"), i["state"], ret_q, ret_k,
                                        ret_k_tok, ret_v_tok, o["state_prompt"], o["state_dec"]))
    one_stage_block(nc, group_norm_stage(core, mix_end, i["gn_sum"], i["gn_spread"], ones_head, eps, part("gn_w"),
                                         ret_q, ret_gate, mix_hi, mix_lo))
    one_stage_block(nc, attention_projection_stage(core, mix_end, i["w_att"], xh, xl, ident, att_q, att_k, att_v_tok))
    one_stage_block(nc, attention_stage(core, mix_end, caches_at, i, part("sinks"), part("sinks_dec"),
                                        {"k": i["k_cache"], "v": i["v_cache"]}, att_q, att_k, att_v_tok, ident,
                                        mix_hi, mix_lo, o))

    out_proj = output_projection_stage(core, mix_end, i["w_out"], mix_hi, mix_lo, xh, xl, acc)
    norm2 = norm_stage(core, "n2_", ffn1.end, 1.0, acc, gain(1), shift(1), ones_mean, eps, xh, xl,
                       rescale=2 * ALPHA, acc_ready=out_proj.acc_ready)
    ffn2 = ffn_stage(core, "f2_", free, i["ffn2"], acc, xh, xl, norm2.x_ready, norm2.acc_ready,
                     room=out_proj.products_done)
    norm3 = norm_stage(core, "n3_", ffn1.end, 0.5, acc, gain(2), shift(2), ones_mean, eps, y_out=o["y"],
                       acc_ready=ffn2.acc_ready)
    with nc.Block() as block:

        @block.sync
        def _(sp):
            out_proj.sync(sp)
            ffn2.sync_early(sp)
            ffn2.sync(sp)
            norm3.sync(sp)

        @block.gpsimd
        def _(pool):
            out_proj.gpsimd(pool)
            ffn2.gpsimd_early(pool)
            norm2.gpsimd(pool)
            ffn2.gpsimd(pool)

        @block.scalar
        def _(act):
            out_proj.scalar(act)
            ffn2.scalar_early(act)
            norm2.scalar(act)
            ffn2.scalar(act)
            norm3.scalar(act)

        @block.vector
        def _(dve):
            out_proj.vector(dve)
            norm2.vector(dve)
            ffn2.vector(dve)
            norm3.vector(dve)

        @block.tensor
        def _(pe):
            out_proj.tensor(pe)
            norm2.tensor(pe)
            ffn2.tensor(pe)
            norm3.tensor(pe)


def shape_constants():
    head = np.arange(HEADS, dtype=np.float64)
    log_g = np.log1p(-np.exp2(-5.0 - head))
    halves = lambda t: np.repeat(t.reshape(PAIRS, 2).T, HD, axis=0)
    idx = np.arange(P)
    tok = np.arange(DEC)
    seq, pos = tok // DEC_SEQ, tok % DEC_SEQ

    def decay_mask(dist, valid):
        e = np.where(valid[None], np.exp(np.where(valid, dist, 0)[None] * log_g[:, None, None]), 0.0) * QSCALE
        return e.reshape(PAIRS, 2, *dist.shape).transpose(2, 1, 0, 3)

    def rows(a):
        out = np.zeros((P, *a.shape[1:]))
        out[:a.shape[0]] = a
        return out

    dist = idx[None, :] - idx[:, None]
    dist_dec = pos[None, :] - pos[:, None]
    same = seq[None, :] == seq[:, None]
    slopes = np.exp2(-8.0 / HEADS * np.arange(1, HEADS + 1))
    back = idx[:, None] + P - np.arange(2 * P)[None, :]
    bias = np.where((back >= 0) & (back <= WINDOW), -slopes.reshape(KVH, GROUP, 1, 1) * back, MASKED)
    s4, t4, i8 = (v.reshape(-1) for v in np.meshgrid(np.arange(4), np.arange(GROUP), np.arange(DEC_SEQ), indexing="ij"))
    cached = i8[:, None] + WINDOW - np.arange(WINDOW)[None, :]
    bias_dec = np.empty((P, KVH, 2, P + DEC))
    for h in range(KVH):
        for half in range(2):
            sl = slopes[GROUP * h + t4][:, None]
            new = i8[:, None] - pos[None, :]
            mine = (4 * half + s4)[:, None] == seq[None, :]
            bias_dec[:, h, half, :WINDOW] = np.where(cached <= WINDOW, -sl * cached, MASKED)
            bias_dec[:, h, half, WINDOW:] = np.where(mine & (new >= 0), -sl * new, MASKED)
    gn_sum = np.zeros((P, PAIRS, HEADS))
    gn_spread = np.zeros((HEADS, PAIRS, P))
    for t in range(PAIRS):
        for h in range(2):
            gn_sum[HD * h:HD * h + HD, t, 2 * t + h] = 1.0 / HD
            gn_spread[2 * t + h, t, HD * h:HD * h + HD] = 1.0
    small = {
        "g_chunk": halves(np.exp(P * log_g)),
        "g_dec": halves(np.exp(DEC_SEQ * log_g)),
        "k_decay": np.exp((P - 1.0 - idx)[:, None] * log_g) * QSCALE,
        "k_decay_dec": rows(np.exp((DEC_SEQ - 1.0 - pos)[:, None] * log_g) * QSCALE),
        "ident": np.eye(P),
    }
    q_exp = lambda p: np.exp((p + 1.0)[None, :] * log_g[:, None])
    q_tab = lambda p: np.repeat(q_exp(p).reshape(PAIRS, 2, -1).transpose(1, 0, 2), HD, axis=0)
    tables = {
        "mask": decay_mask(dist, dist >= 0),
        "mask_dec": rows(decay_mask(dist_dec, same & (dist_dec >= 0))),
        "q_decay": q_tab(idx),
        "q_decay_dec": q_tab(pos),
        "own": rows((seq[:, None] == np.arange(DEC_BATCH)[None, :]).astype(np.float64)),
        "bias": bias.transpose(2, 0, 1, 3),
        "bias_dec": bias_dec,
        "gn_sum": gn_sum,
        "gn_spread": gn_spread,
    }
    f = lambda d: {k: np.ascontiguousarray(v, dtype=np.float32) for k, v in d.items()}
    return f(small), f(tables)


def kernel(x_prompt, x_sample, state_ret, cache_swa_k, cache_swa_v, ln_gain, ln_bias, w_in, ret_gn_w,
           swa_sinks, w_out, ffn1_gate, ffn1_up, ffn1_down, ffn2_gate, ffn2_up, ffn2_down):
    import concourse.bacc as bacc
    from concourse.bass_utils import run_bass_kernel_spmd

    arr = np.asarray
    small_c, tables = shape_constants()

    def by_feature(v):
        return arr(v).reshape(-1, P).T

    def lhs_tiles(w):
        w = arr(w)
        return w.reshape(KT, P, -1, P).transpose(2, 1, 0, 3).reshape(-1, P, D_MODEL)

    def ffn(gate, up, down):
        return np.stack([lhs_tiles(gate[0]), lhs_tiles(up[0]), arr(down[0]).reshape(FT, P, D_MODEL)], axis=2)

    x = np.concatenate([arr(x_prompt)[0], arr(x_sample).reshape(DEC, D_MODEL)], axis=0)
    w = arr(w_in)[0]
    R = HEADS * HD
    ret = lhs_tiles(w[:, :4 * R]).reshape(4, PAIRS, P, D_MODEL).transpose(1, 0, 2, 3).reshape(4 * PAIRS, P, D_MODEL)
    att_q = w[:, 4 * R:5 * R].reshape(D_MODEL, KVH, GROUP, HD).transpose(0, 2, 1, 3).reshape(D_MODEL, R)
    att = np.concatenate([lhs_tiles(att_q), lhs_tiles(w[:, 5 * R:])], axis=0)
    wo = arr(w_out)[0]
    wo_att = wo[R:].reshape(KVH, GROUP, HD, D_MODEL).transpose(1, 0, 2, 3).reshape(R, D_MODEL)
    sinks = arr(swa_sinks)[0]
    sinks_dec = np.broadcast_to(sinks.reshape(KVH, 1, GROUP, 1), (KVH, 4, GROUP, DEC_SEQ)).reshape(KVH, P).T
    small = {
        **small_c,
        "ln_gain": by_feature(arr(ln_gain)[0]), "ln_bias": by_feature(arr(ln_bias)[0]),
        "gn_w": by_feature(arr(ret_gn_w)[0]),
        "sinks": np.broadcast_to(sinks, (P, HEADS)), "sinks_dec": sinks_dec,
    }
    ins = {
        "x": x.T.reshape(KT, P, TOK).transpose(1, 0, 2),
        "small": np.concatenate([small[n] for n in SMALL], axis=1),
        "ffn1": ffn(ffn1_gate, ffn1_up, ffn1_down),
        "ffn2": ffn(ffn2_gate, ffn2_up, ffn2_down),
        "w_ret": ret,
        "w_att": att,
        "w_out": lhs_tiles(np.concatenate([wo[:R], wo_att], axis=0)),
        "state": arr(state_ret)[0].reshape(DEC_BATCH, PAIRS, 2, HD, HD).transpose(2, 3, 1, 0, 4)
                 .reshape(P, PAIRS, DEC_BATCH, HD),
        "k_cache": arr(cache_swa_k)[0].transpose(2, 3, 0, 1).reshape(P, DEC_BATCH, WINDOW),
        "v_cache": arr(cache_swa_v)[0].transpose(1, 0, 2, 3).reshape(WINDOW, DEC_BATCH, P),
        **tables,
    }
    outs = {
        "y": (P, KT, TOK),
        "state_prompt": (P, PAIRS, HD),
        "state_dec": (P, PAIRS, DEC_BATCH, HD),
        "k_prompt": (P, WINDOW), "v_prompt": (WINDOW, P),
        "k_dec": (P, DEC_BATCH, WINDOW), "v_dec": (DEC_BATCH, WINDOW, P),
    }
    nc = bacc.Bacc("TRN2", target_bir_lowering=False, num_devices=1)
    i = {n: nc.dram_tensor(n + "_in", a.shape, F32, kind="ExternalInput").ap() for n, a in ins.items()}
    o = {n: nc.dram_tensor(n + "_out", s, F32, kind="ExternalOutput").ap() for n, s in outs.items()}
    decoder_layer_kernel(nc, i, o)
    got = run_bass_kernel_spmd(nc, [{n + "_in": np.ascontiguousarray(a) for n, a in ins.items()}],
                               core_ids=[0]).results[0]
    got = {n: got[n + "_out"] for n in outs}

    y = got["y"].transpose(2, 1, 0).reshape(TOK, D_MODEL)
    state_p = got["state_prompt"].reshape(2, HD, PAIRS, HD).transpose(2, 0, 1, 3)
    state_d = got["state_dec"].reshape(2, HD, PAIRS, DEC_BATCH, HD).transpose(3, 2, 0, 1, 4)
    k_p = got["k_prompt"].reshape(KVH, HD, WINDOW).transpose(2, 0, 1)
    k_d = got["k_dec"].reshape(KVH, HD, DEC_BATCH, WINDOW).transpose(2, 3, 0, 1)
    return (
        y[:SEQ].reshape(1, SEQ, D_MODEL), y[SEQ:].reshape(DEC_BATCH, DEC_SEQ, D_MODEL),
        state_p.reshape(1, 1, HEADS, HD, HD), k_p.reshape(1, 1, WINDOW, KVH, HD),
        got["v_prompt"].reshape(1, 1, WINDOW, KVH, HD),
        state_d.reshape(1, DEC_BATCH, HEADS, HD, HD), k_d.reshape(1, DEC_BATCH, WINDOW, KVH, HD),
        got["v_dec"].reshape(1, DEC_BATCH, WINDOW, KVH, HD),
    )
```

```python
from contextlib import ExitStack

import numpy as np

import concourse.bass as bass
from concourse import mybir

F32 = mybir.dt.float32
F32R = mybir.dt.float32r
ACT = mybir.ActivationFunctionType
ALU = mybir.AluOpType
AX = mybir.AxisListType

P = 128
D_MODEL = 1024
D_FF = 2816
KT = D_MODEL // P
FT = D_FF // P
SEQ = 1024
DEC_BATCH, DEC_SEQ = 8, 8
DEC = DEC_BATCH * DEC_SEQ
TOK = SEQ + DEC
HEADS, HD = 8, 64
PAIRS = HEADS // 2
KVH = 2
GROUP = HEADS // KVH
WINDOW = 128
BLOCKS = SEQ // P
EPS = 1e-5
ALPHA = 2.0 ** 0.25
QSCALE = HD ** -0.5
MASKED = -1e30

CHUNKS = [(0, 362), (362, 726), (726, TOK)]
CW = max(b - a for a, b in CHUNKS)

RET, SWA = 0, 1


class Core:

    def __init__(self, nc, semaphore, banks):
        self.nc, self.semaphore, self.banks = nc, semaphore, banks


class Stage:

    def __init__(self, sync=None, scalar=None, gpsimd=None, tensor=None, vector=None, sync_early=None,
                 sync_x=None, sync_small=None, gpsimd_second=None,
                 second_ready=None, outputs_stored=None, weights_split=None,
                 ready=None,
                 scalar_early=None, gpsimd_early=None, x_ready=None, acc_ready=None,
                 products_done=None, end=None):
        self.sync, self.scalar, self.gpsimd, self.tensor, self.vector = sync, scalar, gpsimd, tensor, vector
        self.sync_x, self.sync_small = sync_x, sync_small
        self.gpsimd_second = gpsimd_second
        self.second_ready, self.outputs_stored = second_ready, outputs_stored
        self.weights_split, self.ready = weights_split, ready
        self.sync_early, self.scalar_early, self.gpsimd_early = sync_early, scalar_early, gpsimd_early
        self.x_ready, self.acc_ready, self.products_done, self.end = x_ready, acc_ready, products_done, end


class Layout:

    def __init__(self, nc, at):
        self.nc, self.at = nc, at

    def put(self, name, shape, dtype=F32):
        t = self.nc.alloc_sbuf_tensor_at(name, shape, dtype, offset=self.at)
        self.at += -(-int(np.prod(shape[1:])) * 4 // 32) * 32
        return t


def three_passes(pe, out, weights, moving, first, last):
    (wh, wl), (xh, xl) = weights, moving
    pe.matmul(out, wh, xh, start=first, stop=False)
    pe.matmul(out, wh, xl, start=False, stop=False)
    return pe.matmul(out, wl, xh, start=False, stop=last)


def load_stage(core, x_in, small_in, small, ones_mean, ones_head, eps, acc, xh, xl):
    sem = lambda n: core.semaphore("load_" + n)
    x_loaded = [sem(f"x_loaded{c}") for c in range(len(CHUNKS))]
    small_loaded, hi_done, lo_done, scaled, filled = map(
        sem, ("small_loaded", "hi_done", "lo_done", "scaled", "filled"))

    def sync_x(sp, c):
        a, b = CHUNKS[c]
        sp.dma_start(acc[:, :, a:b], x_in[:, :, a:b]).then_inc(x_loaded[c], 16)

    def sync_small(sp):
        sp.dma_start(small[:, 0:SMALL_W], small_in).then_inc(small_loaded, 16)
        sp.wait_ge(small_loaded, 16)

    def gpsimd(pool):
        pool.memset(ones_mean[:, :], 1.0 / D_MODEL).then_inc(filled, 1)
        pool.memset(ones_head[:, :], 0.0).then_inc(filled, 1)
        pool.memset(eps[:, :], EPS).then_inc(filled, 1)
        pool.wait_ge(filled, 3)
        for h in range(2):
            d = slice(HD * h, HD * h + HD)
            pool.memset(ones_head[d, d], 1.0 / HD).then_inc(filled, 1)
        pool.wait_ge(filled, 5)

    def scalar(act, c):
        a, b = CHUNKS[c]
        act.wait_ge(x_loaded[c], 16)
        act.activation(xh[:, :, a:b], acc[:, :, a:b], ACT.Copy).then_inc(hi_done, 1)

    def vector(dve):
        for c, (a, b) in enumerate(CHUNKS):
            dve.wait_ge(hi_done, c + 1)
            dve.tensor_tensor(xl[:, :, a:b], acc[:, :, a:b], xh[:, :, a:b].bitcast(F32),
                              ALU.subtract).then_inc(lo_done, 1)
            dve.wait_ge(lo_done, c + 1)
            dve.tensor_scalar(acc[:, :, a:b], acc[:, :, a:b], 2 * ALPHA, None, ALU.mult).then_inc(scaled, 1)

    return Stage(sync_x=sync_x, sync_small=sync_small, gpsimd=gpsimd, scalar=scalar, vector=vector,
                 x_ready=lo_done, acc_ready=(scaled, len(CHUNKS)))


def ffn_stage(core, tag, at, stage_at, w_in, acc, xh, xl, x_ready, x_halves, acc_ready, norm, last_norm=None,
              room=None):
    m = Layout(core.nc, at)
    w_hi = [[m.put(f"{tag}w_hi{s}{j}", [P, KT, P], F32R) for j in range(3)] for s in range(2)]
    w_lo = [[m.put(f"{tag}w_lo{s}{j}", [P, KT, P], F32R) for j in range(3)] for s in range(2)]
    h_hi = [m.put(f"{tag}h_hi{s}", [P, TOK], F32R) for s in range(2)]
    h_lo = [m.put(f"{tag}h_lo{s}", [P, TOK], F32R) for s in range(2)]
    silu = m.put(tag + "silu", [P, 3, CW])
    h_full = m.put(tag + "h_full", [P, 3, CW])
    stage = Layout(core.nc, stage_at).put(tag + "stage", [P, 3, D_MODEL])
    GATE, UP, DOWN = range(3)
    NC_ = len(CHUNKS)
    DOWNS = KT * NC_
    sem = lambda n: core.semaphore(tag + n)
    gate_ps, up_ps, down_ps = core.banks[0:2], core.banks[2:4], core.banks[4:8]
    staged = [sem(f"staged{j}") for j in range(3)]
    hi_done = sem("hi_done")
    gu_split = sem("gu_split")
    down_split = sem("down_split")
    gate_done, up_done = sem("gate_done"), sem("up_done")
    silu_done = sem("silu_done")
    pair_free = sem("pair_free")
    h_hi_done, h_lo_done = sem("h_hi_done"), sem("h_lo_done")
    down_done = sem("down_done")
    down_free = sem("down_free")

    A, B = FT - 2, FT - 1
    LAST = [(A, 0), (A, 1), (B, 0), (B, 1), (A, 2), (B, 2)]

    def number(f, c):
        return 3 * A + LAST.index((f, c)) if isinstance(f, int) and f >= A else 3 * f + c

    def tiles(eng, step):
        with eng.Fori(0, (A - 1) // 2) as i:
            step(2 * i + 1, 1)
            step(2 * i + 2, 0)
        step(A - 1, 1)

    def turn_of(f, s, c):
        return number(f, c) % 6 if isinstance(f, int) else 3 * s + c

    def pair_of(f, s, c):
        return 0 if isinstance(f, int) and (f, c) == LAST[-1] else turn_of(f, s, c) % 2

    def buffer_of(f, s, c):
        return turn_of(f, s, c) % 3

    def sync_early(sp):
        if room:
            sp.wait_ge(*room)
        for j in range(3):
            sp.dma_start(stage[:, j, :], w_in[0, :, j, :]).then_inc(staged[j], 16)

    def sync(sp):
        with sp.Fori(1, FT) as f:
            for j in (GATE, UP):
                sp.wait_ge(gu_split, 2 * f - 1 + j)
                sp.dma_start(stage[:, j, :], w_in[bass.ds(f, 1), :, j, :].rearrange("a p n -> (a p) n")).then_inc(staged[j], 16)
            sp.wait_ge(down_split, f)
            sp.dma_start(stage[:, DOWN, :], w_in[bass.ds(f, 1), :, DOWN, :].rearrange("a p n -> (a p) n")).then_inc(staged[DOWN], 16)

    def round_part(act, f, s, j):
        act.wait_ge(staged[j], 16 * f + 16)
        act.activation(w_hi[s][j][:, :, :].rearrange("p k n -> p (k n)"), stage[:, j, :],
                       ACT.Copy).then_inc(hi_done, 1)

    def scalar_early(act):
        for j in range(3):
            round_part(act, 0, 0, j)

    def scalar(act):
        def silu_chunk(f, s, c):
            a, b = CHUNKS[c]
            act.wait_ge(gate_done, number(f, c) + 1)
            act.activation(silu[:, buffer_of(f, s, c), 0:b - a], gate_ps[pair_of(f, s, c)][:, 0:b - a],
                           ACT.Silu).then_inc(silu_done, 1)

        def round_h(f, s, c):
            a, b = CHUNKS[c]
            act.wait_ge(pair_free, 2 + number(f, c) + 1)
            act.activation(h_hi[s][:, a:b], h_full[:, buffer_of(f, s, c), 0:b - a],
                           ACT.Copy).then_inc(h_hi_done, 1)

        def silu_and_round(f, s, c):
            silu_chunk(f, s, c)
            round_h(f, s, c)

        def step(f, s):
            if not (isinstance(f, int) and f == 0):
                act.wait_ge(up_done, 3 * f)
            round_part(act, f + 1, 1 - s, GATE)
            round_part(act, f + 1, 1 - s, UP)
            for c in range(NC_):
                silu_and_round(f, s, c)
            if not (isinstance(f, int) and f == 0):
                act.wait_ge(down_done, DOWNS * f)
            round_part(act, f + 1, 1 - s, DOWN)

        step(0, 0)
        tiles(act, step)
        act.wait_ge(up_done, 3 * A)
        round_part(act, B, 1, GATE)
        round_part(act, B, 1, UP)
        silu_and_round(A, 0, 0)
        act.wait_ge(down_done, DOWNS * A)
        round_part(act, B, 1, DOWN)
        silu_and_round(A, 0, 1)
        silu_and_round(B, 1, 0)
        silu_and_round(B, 1, 1)
        norm.square(act, 0)
        silu_and_round(A, 0, 2)
        norm.deviation(act, 0)
        silu_and_round(B, 1, 2)
        if norm.xh is not None:
            norm.round(act, 0)
        norm.square(act, 1)

    def split(pool, f, s):
        for j, done in ((GATE, gu_split), (UP, gu_split), (DOWN, down_split)):
            pool.wait_ge(hi_done, 3 * f + j + 1)
            pool.tensor_tensor(w_lo[s][j][:, :, :].rearrange("p k n -> p (k n)"), stage[:, j, :],
                               w_hi[s][j][:, :, :].rearrange("p k n -> p (k n)").bitcast(F32),
                               ALU.subtract).then_inc(done, 1)

    def gpsimd_early(pool):
        split(pool, 0, 0)

    def gpsimd(pool):
        with pool.Fori(0, (FT - 2) // 2) as i:
            split(pool, 2 * i + 1, 1)
            split(pool, 2 * i + 2, 0)
        split(pool, FT - 1, 1)

    def tensor(pe):
        def gate_or_up(f, s, c, j):
            a, b = CHUNKS[c]
            ps, done = ((gate_ps, gate_done), (up_ps, up_done))[j]
            if c == 0:
                pe.wait_ge(gu_split, 2 * f + j + 1)
            for k in range(KT):
                mm = three_passes(pe, ps[pair_of(f, s, c)][:, 0:b - a], (w_hi[s][j][:, k, :], w_lo[s][j][:, k, :]),
                                  (xh[:, k, a:b], xl[:, k, a:b]), k == 0, k == KT - 1)
            mm.then_inc(done, 1)

        def gate_up(f, s, c, between=lambda: None):
            if isinstance(f, int) and f == 0:
                pe.wait_ge(x_ready, x_halves * (c + 1))
            pe.wait_ge(pair_free, number(f, c) + (2 if isinstance(f, int) and (f, c) == LAST[-1] else 1))
            gate_or_up(f, s, c, GATE)
            between()
            gate_or_up(f, s, c, UP)

        def down(f, s):
            pe.wait_ge(down_split, f + 1)
            n = 0
            for d in range(KT):
                for c, (a, b) in enumerate(CHUNKS):
                    if d == 0:
                        pe.wait_ge(h_lo_done, number(f, c) + 1)
                    pe.wait_ge(down_free, DOWNS * f + n + 1 + DOWNS - 4)
                    three_passes(pe, down_ps[n % 4][:, 0:b - a],
                                 (w_hi[s][DOWN][:, d, :], w_lo[s][DOWN][:, d, :]),
                                 (h_hi[s][:, a:b], h_lo[s][:, a:b]), True, True).then_inc(down_done, 1)
                    n += 1

        def last_downs(c):
            a, b = CHUNKS[c]
            pe.wait_ge(h_lo_done, max(number(A, c), number(B, c)) + 1)
            if c == 0:
                pe.wait_ge(down_split, FT)
            for d in range(KT):
                n = KT * c + d
                pe.wait_ge(down_free, DOWNS * (A + 1) + n + 1 - 4)
                for f, s in ((A, 0), (B, 1)):
                    mm = three_passes(pe, down_ps[n % 4][:, 0:b - a],
                                      (w_hi[s][DOWN][:, d, :], w_lo[s][DOWN][:, d, :]),
                                      (h_hi[s][:, a:b], h_lo[s][:, a:b]), f == A, f == B)
                mm.then_inc(down_done, 1)

        def step(f, s):
            for c in range(NC_):
                gate_up(f, s, c)
            down(f - 1, 1 - s)

        pe.sem_inc(pair_free, 2)
        gate_up(0, 0, 0)
        gate_up(0, 0, 1)
        if last_norm:
            last_norm.variance(pe, NC_ - 1)
        gate_up(0, 0, 2)
        tiles(pe, step)
        gate_up(A, 0, 0)
        down(A - 1, 1)
        gate_up(A, 0, 1)
        gate_up(B, 1, 0)
        gate_up(B, 1, 1)
        last_downs(0)
        pe.wait_ge(pair_free, 2 + number(B, 1) + 1)
        gate_up(A, 0, 2, between=lambda: norm.mean(pe, 0))
        last_downs(1)
        norm.variance(pe, 0)
        gate_up(B, 1, 2)
        norm.mean(pe, 1)
        last_downs(2)

    def vector(dve):
        def h_chunk(f, s, c):
            a, b = CHUNKS[c]
            if not (isinstance(f, int) and f == 0):
                dve.wait_ge(h_lo_done, number(f, c) - 2)
            dve.wait_ge(silu_done, number(f, c) + 1)
            dve.wait_ge(up_done, number(f, c) + 1)
            at = buffer_of(f, s, c)
            dve.tensor_tensor(h_full[:, at, 0:b - a], up_ps[pair_of(f, s, c)][:, 0:b - a],
                              silu[:, at, 0:b - a], ALU.mult).then_inc(pair_free, 1)

        def split_h(f, s, c):
            a, b = CHUNKS[c]
            dve.wait_ge(h_hi_done, number(f, c) + 1)
            dve.tensor_tensor(h_lo[s][:, a:b], h_full[:, buffer_of(f, s, c), 0:b - a],
                              h_hi[s][:, a:b].bitcast(F32), ALU.subtract).then_inc(h_lo_done, 1)

        def h_tile(f, s):
            h_chunk(f, s, 0)
            split_h(f, s, 0)
            h_chunk(f, s, 1)
            split_h(f, s, 1)
            h_chunk(f, s, 2)

        def h_and_split(f, s, c):
            h_chunk(f, s, c)
            split_h(f, s, c)

        def add_down(f, ns=range(DOWNS)):
            for n in ns:
                d, (a, b) = n // NC_, CHUNKS[n % NC_]
                dve.wait_ge(down_free, DOWNS * f + n + 1)
                dve.wait_ge(down_done, DOWNS * f + n + 1)
                dve.tensor_tensor(acc[:, d, a:b], down_ps[n % 4][:, 0:b - a], acc[:, d, a:b],
                                  ALU.add).then_inc(down_free, 1)

        def add_last(c, ds=range(KT)):
            a, b = CHUNKS[c]
            for d in ds:
                n = KT * c + d
                dve.wait_ge(down_free, DOWNS * A + NC_ * d + c + 1)
                dve.wait_ge(down_done, DOWNS * A + n + 1)
                dve.tensor_tensor(acc[:, d, a:b], down_ps[n % 4][:, 0:b - a], acc[:, d, a:b],
                                  ALU.add).then_inc(down_free, 1)

        def final(c):
            return down_free, DOWNS * (A + 1) + KT * (c + 1)

        def step(f, s):
            h_tile(f, s)
            add_down(f - 1, range(3))
            split_h(f, s, 2)
            add_down(f - 1, range(3, DOWNS))

        h_tile(0, 0)
        split_h(0, 0, 2)
        dve.wait_ge(*acc_ready)
        dve.sem_inc(down_free, DOWNS)
        tiles(dve, step)
        h_and_split(A, 0, 0)
        add_down(A - 1)
        h_and_split(A, 0, 1)
        h_and_split(B, 1, 0)
        h_and_split(B, 1, 1)
        add_last(0)
        norm.gather(dve, 0, final(0))
        norm.centre(dve, 0)
        h_and_split(A, 0, 2)
        add_last(1, range(4))
        norm.fold(dve, 0)
        add_last(1, range(4, KT))
        norm.normalise(dve, 0)
        h_and_split(B, 1, 2)
        norm.centre(dve, 1, (0,))
        add_last(2, range(2))
        norm.centre(dve, 1, (1,))
        add_last(2, range(2, KT))
        norm.fold(dve, 1)
        norm.gather(dve, 2, final(2))
        norm.normalise(dve, 1)
        norm.centre(dve, 2)
        norm.fold(dve, 2)
        norm.normalise(dve, 2)

    return Stage(sync_early=sync_early, scalar_early=scalar_early, gpsimd_early=gpsimd_early,
                 sync=sync, scalar=scalar, gpsimd=gpsimd, tensor=tensor, vector=vector,
                 products_done=(down_done, DOWNS * (A + 1)), end=m.at,
                 second_ready=(down_free, DOWNS * (A + 1) + 2 * KT), acc_ready=(down_free, DOWNS * (A + 2)))


class Norm:

    def __init__(self, core, tag, scale, acc, gain, bias, ones_mean, eps, work, rstd, banks,
                 xh=None, xl=None, rescale=None, y_out=None):
        self.scale, self.acc, self.gain, self.bias, self.ones, self.eps = scale, acc, gain, bias, ones_mean, eps
        self.work, self.rstd, self.xh, self.xl = work, rstd, xh, xl
        self.rescale, self.y_out = rescale, y_out
        self.mean_ps, self.var_ps = banks
        sem = lambda n: core.semaphore(tag + n)
        self.gathered, self.mean_done, self.centred, self.squared, self.folded, self.var_done = map(
            sem, ("gathered", "mean_done", "centred", "squared", "folded", "var_done"))
        self.std_done, self.rstd_done, self.scaled, self.affine, self.hi_done, self.lo_done = map(
            sem, ("std_done", "rstd_done", "scaled", "affine", "hi_done", "lo_done"))
        self.rescaled, self.stored = sem("rescaled"), sem("stored")
        self.x_ready = self.lo_done
        self.acc_ready = (self.rescaled, len(CHUNKS))

    def half(self, h):
        return slice(KT // 2 * h, KT // 2 * h + KT // 2)

    def mean(self, pe, c):
        a, b = CHUNKS[c]
        pe.wait_ge(self.gathered, 3 * c + 3)
        pe.matmul(self.mean_ps[:, 0:b - a], self.ones[:, :], self.work[:, 0, a:b],
                  start=True, stop=True).then_inc(self.mean_done, 1)

    def variance(self, pe, c):
        a, b = CHUNKS[c]
        pe.wait_ge(self.folded, 3 * c + 3)
        if c:
            pe.wait_ge(self.std_done, c)
        pe.matmul(self.var_ps[:, 0:b - a], self.ones[:, :], self.work[:, 0, a:b],
                  start=True, stop=True).then_inc(self.var_done, 1)

    def add_tiles(self, dve, c, src, done):
        a, b = CHUNKS[c]
        dve.tensor_tensor(self.work[:, 0:4, a:b], src[:, 0:4, a:b], src[:, 4:8, a:b], ALU.add).then_inc(done, 1)
        for i, n in enumerate((2, 1)):
            dve.wait_ge(done, 3 * c + i + 1)
            dve.tensor_tensor(self.work[:, 0:n, a:b], self.work[:, 0:n, a:b], self.work[:, n:2 * n, a:b],
                              ALU.add).then_inc(done, 1)

    def gather(self, dve, c, acc_done):
        dve.wait_ge(*acc_done)
        if c:
            dve.wait_ge(self.centred, 2 * c)
        self.add_tiles(dve, c, self.acc, self.gathered)

    def centre(self, dve, c, halves=(0, 1)):
        a, b = CHUNKS[c]
        dve.wait_ge(self.mean_done, c + 1)
        for h in halves:
            k = self.half(h)
            dve.tensor_tensor(self.acc[:, k, a:b], self.acc[:, k, a:b],
                              self.mean_ps[:, 0:b - a].unsqueeze(1).to_broadcast([P, KT // 2, b - a]),
                              ALU.subtract).then_inc(self.centred, 1)

    def fold(self, dve, c):
        dve.wait_ge(self.squared, 2 * c + 2)
        self.add_tiles(dve, c, self.work, self.folded)

    def normalise(self, dve, c):
        a, b = CHUNKS[c]
        dve.wait_ge(self.std_done, c + 1)
        dve.reciprocal(self.rstd[:, a:b], self.rstd[:, a:b]).then_inc(self.rstd_done, 1)
        dve.wait_ge(self.rstd_done, c + 1)
        dve.wait_ge(self.centred, 2 * c + 2)
        for h in range(2):
            k = self.half(h)
            dve.scalar_tensor_tensor(self.acc[:, k, a:b], self.acc[:, k, a:b], self.scale,
                                     self.rstd[:, a:b].unsqueeze(1).to_broadcast([P, KT // 2, b - a]),
                                     ALU.mult, ALU.mult).then_inc(self.scaled, 1)
        for h in range(2):
            dve.wait_ge(self.scaled, 2 * c + h + 1)
            for k in range(KT // 2 * h, KT // 2 * h + KT // 2):
                i = dve.tensor_scalar(self.acc[:, k, a:b], self.acc[:, k, a:b], self.gain[:, k:k + 1],
                                      self.bias[:, k:k + 1], ALU.mult, ALU.add)
            i.then_inc(self.affine, 1)

    def low_part(self, eng, c, halves=(0, 1)):
        a, b = CHUNKS[c]
        for h in halves:
            k = self.half(h)
            eng.wait_ge(self.hi_done, 2 * c + h + 1)
            if c or h:
                eng.wait_ge(self.lo_done, 2 * c + h)
            eng.tensor_tensor(self.xl[:, k, a:b], self.acc[:, k, a:b], self.xh[:, k, a:b].bitcast(F32),
                              ALU.subtract).then_inc(self.lo_done, 1)

    def finish(self, dve, c):
        a, b = CHUNKS[c]
        dve.wait_ge(self.lo_done, 2 * c + 2)
        dve.tensor_scalar(self.acc[:, :, a:b], self.acc[:, :, a:b], self.rescale, None,
                          ALU.mult).then_inc(self.rescaled, 1)

    def square(self, act, c):
        a, b = CHUNKS[c]
        for h in range(2):
            k = self.half(h)
            act.wait_ge(self.centred, 2 * c + h + 1)
            act.activation(self.work[:, k, a:b], self.acc[:, k, a:b], ACT.Square,
                           scale=self.scale).then_inc(self.squared, 1)

    def deviation(self, act, c):
        a, b = CHUNKS[c]
        act.wait_ge(self.var_done, c + 1)
        act.activation(self.rstd[:, a:b], self.var_ps[:, 0:b - a], ACT.Sqrt,
                       bias=self.eps[:, 0:1]).then_inc(self.std_done, 1)

    def round(self, act, c):
        a, b = CHUNKS[c]
        for h in range(2):
            act.wait_ge(self.affine, 2 * c + h + 1)
            k = self.half(h)
            act.activation(self.xh[:, k, a:b], self.acc[:, k, a:b], ACT.Copy).then_inc(self.hi_done, 1)

    def store(self, sp):
        for c, (a, b) in enumerate(CHUNKS):
            for h in range(2):
                k = self.half(h)
                sp.wait_ge(self.affine, 2 * c + h + 1)
                sp.dma_start(self.y_out[:, k, a:b], self.acc[:, k, a:b]).then_inc(self.stored, 16)
        sp.wait_ge(self.stored, 32 * len(CHUNKS))


def weight_buffers(m, tag):
    stage = m.put(tag + "stage", [P, 2, D_MODEL])
    w_hi = [m.put(f"{tag}w_hi{s}", [P, D_MODEL], F32R) for s in range(2)]
    w_lo = [m.put(f"{tag}w_lo{s}", [P, D_MODEL], F32R) for s in range(2)]
    return stage, w_hi, w_lo


def project_tile(pe, out, w_hi, w_lo, xh, xl, a, b):
    for k in range(KT):
        d = slice(P * k, P * k + P)
        mm = three_passes(pe, out[:, 0:b - a], (w_hi[:, d], w_lo[:, d]), (xh[:, k, a:b], xl[:, k, a:b]),
                          k == 0, k == KT - 1)
    return mm


TOKEN_TILES = BLOCKS + 1
TURN_BATCHES = [(0, 3), (3, 6), (6, 9)]


def tile_tokens(n):
    return (P * n, P * n + P) if n < BLOCKS else (SEQ, TOK)


def retention_projection_stage(core, at, first_at, w_in, w_small, xh, xl, ident, q_t, k_t, gate_t, k_tok, v_tok,
                               norm, room, banks_free):
    k_decay, k_decay_dec = w_small
    tag = "rp_"
    m = Layout(core.nc, at)
    k_turn = m.put(tag + "k_turn", [P, TOK])
    v_turn = m.put(tag + "v_turn", [P, TOK])
    first = Layout(core.nc, first_at)
    w_hi, w_lo = ([place.put(f"{tag}{part}{j}", [P, D_MODEL], F32R) for j, place in enumerate((first, m, m, m))]
                  for part in ("w_hi", "w_lo"))
    stage_at = first.at
    stage = first.put(tag + "stage", [P, 2, D_MODEL])
    Q, K, V, GATE = range(4)
    TILES = 4 * PAIRS
    FIRST = [(c, j) for c in range(len(CHUNKS)) for j in range(4)]
    sem = lambda n: core.semaphore(tag + n)
    proj_ps, turn_ps = core.banks[4:8], core.banks[0:3]
    staged = [sem(f"staged{s}") for s in range(2)]
    hi_done, lo_done = sem("hi_done"), sem("lo_done")
    proj_done = sem("proj_done")
    proj_free = sem("proj_free")
    turned = sem("turned")
    turn_free = sem("turn_free")
    k_copied = sem("k_copied")
    zeroed = sem("zeroed")
    def sync_early(sp):
        for s in range(2):
            sp.dma_start(stage[:, s, :], w_in[s]).then_inc(staged[s], 16)

    def sync(sp):
        with sp.Fori(1, TILES // 2) as i:
            for s in range(2):
                sp.wait_ge(lo_done, 2 * i + s - 1)
                sp.dma_start(stage[:, s, :], w_in[bass.ds(2 * i + s, 1), :, :].rearrange("a p n -> (a p) n")).then_inc(staged[s], 16)

    def round_tile(act, t, j):
        act.wait_ge(staged[j % 2], 32 * t + 16 * (j // 2) + 16)
        act.activation(w_hi[j][:, :], stage[:, j % 2, :], ACT.Copy).then_inc(hi_done, 1)

    def scalar_early(act):
        act.sem_inc(proj_free, 4)
        round_tile(act, 0, 0)

    def scalar(act):
        def evacuate_chunk(t, j, c, n):
            a, b = CHUNKS[c]
            act.wait_ge(proj_done, 3 + 12 * t + n + 1)
            ps = proj_ps[n % 4][:, 0:b - a]
            if j == Q:
                out, func = q_t[:, bass.ds(t, 1), a:b].rearrange("p o n -> p (o n)"), ACT.Copy
            elif j == K:
                out, func = k_turn[:, a:b], ACT.Copy
            elif j == V:
                out, func = v_turn[:, a:b], ACT.Copy
            else:
                out, func = gate_t[:, bass.ds(t, 1), a:b].rearrange("p o n -> p (o n)"), ACT.Silu
            act.activation(out, ps, func).then_inc(proj_free, 1)

        def evacuate(t, j):
            if j == K:
                act.wait_ge(turned, 6 * t + 3)
                act.wait_ge(k_copied, 3 + 3 * t)
            if j == V:
                act.wait_ge(turned, 6 * t + 6)
            for c in range(len(CHUNKS)):
                evacuate_chunk(t, j, c, 3 * j + c)

        def next_tile(t, j):
            t, j = t + (j + 1) // 4, (j + 1) % 4
            in_first = isinstance(t, int) and t == 1
            act.wait_ge(proj_done, 3 + len(FIRST) - 4 + j + 1 if in_first else 3 + 12 * (t - 1) + 3 * j + 3)
            round_tile(act, t, j)

        def step(t, last):
            for j in range(4):
                if not (last and j == GATE):
                    next_tile(t, j)
                evacuate(t, j)

        act.wait_ge(*room)
        round_tile(act, 0, K)
        round_tile(act, 0, V)
        norm.deviation(act, 1)
        round_tile(act, 0, GATE)
        norm.round(act, 1)
        norm.square(act, 2)
        for n, (c, j) in enumerate(FIRST):
            if n == 3:
                norm.deviation(act, 2)
            if n == 6:
                norm.round(act, 2)
            if n == len(FIRST) - 3:
                next_tile(0, GATE)
            evacuate_chunk(0, j, c, n)
        step(1, False)
        with act.Fori(2, PAIRS - 1) as t:
            step(t, False)
        step(PAIRS - 1, True)

    def split(pool, t, j):
        pool.wait_ge(hi_done, 4 * t + j + 1)
        pool.tensor_tensor(w_lo[j][:, :], stage[:, j % 2, :], w_hi[j][:, :].bitcast(F32),
                           ALU.subtract).then_inc(lo_done, 1)

    def gpsimd_early(pool):
        pool.sem_inc(k_copied, 3)
        split(pool, 0, 0)

    def gpsimd_second(pool):
        split(pool, 0, K)
        split(pool, 0, V)
        split(pool, 0, GATE)

    def gpsimd(pool):
        def copy_k(t, c, filled):
            a, b = CHUNKS[c]
            pool.wait_ge(proj_free, filled)
            pool.tensor_copy(k_t[:, bass.ds(t, 1), a:b].rearrange("p o n -> p (o n)"),
                             k_turn[:, a:b]).then_inc(k_copied, 1)

        def step(t, last):
            for j in range(4):
                if not (last and j == GATE):
                    split(pool, t + (j + 1) // 4, (j + 1) % 4)
                if j == K:
                    for c in range(len(CHUNKS)):
                        copy_k(t, c, 4 + 12 * t + 3 * K + c + 1)

        pool.memset(k_tok[:, BLOCKS, :], 0.0).then_inc(zeroed, 1)
        pool.memset(v_tok[:, BLOCKS, :], 0.0).then_inc(zeroed, 1)
        for c in range(len(CHUNKS)):
            copy_k(0, c, 4 + 4 * c + K + 1)
        split(pool, 1, Q)
        with pool.Fori(1, PAIRS - 1) as t:
            step(t, False)
        step(PAIRS - 1, True)

    def tensor(pe):
        pe.sem_inc(turned, 6)
        pe.sem_inc(proj_done, 3)

        def project_chunk(t, j, c, n):
            a, b = CHUNKS[c]
            pe.wait_ge(proj_free, 12 * t + n + 1)
            project_tile(pe, proj_ps[n % 4], w_hi[j], w_lo[j], xh, xl, a, b).then_inc(proj_done, 1)

        def project(t, j):
            pe.wait_ge(lo_done, 4 * t + j + 1)
            for c in range(len(CHUNKS)):
                project_chunk(t, j, c, 3 * j + c)

        def turn(t, src, j):
            pe.wait_ge(proj_free, 4 + (len(FIRST) if isinstance(t, int) else 12 * t + 3 * j + 3))
            for n, (u0, u1) in enumerate(TURN_BATCHES):
                pe.wait_ge(turn_free, 6 * t + 3 * (j - K) + n + 1)
                for u in range(u0, u1):
                    a, b = tile_tokens(u)
                    mm = pe.transpose(turn_ps[n][0:b - a, P * (u - u0):P * (u - u0) + P],
                                      src[:, a:b], ident[:, :])
                mm.then_inc(turned, 1)

        pe.wait_ge(*banks_free)
        for n, (c, j) in enumerate(FIRST):
            if c == 0:
                pe.wait_ge(lo_done, j + 1)
            if n == 1:
                norm.variance(pe, 1)
            if n == 2:
                norm.mean(pe, 2)
            if n == 5:
                norm.variance(pe, 2)
            pe.wait_ge(norm.x_ready, 2 * c + 2)
            project_chunk(0, j, c, n)
        turn(0, k_turn, K)
        turn(0, v_turn, V)
        with pe.Fori(1, PAIRS) as t:
            project(t, Q)
            project(t, K)
            project(t, V)
            turn(t, k_turn, K)
            project(t, GATE)
            turn(t, v_turn, V)

    def vector(dve):
        dve.sem_inc(turn_free, 3)
        dve.wait_ge(zeroed, 2)

        def step(t):
            for j in (K, V):
                for n, (u0, u1) in enumerate(TURN_BATCHES):
                    dve.wait_ge(turned, 6 + 6 * t + 3 * (j - K) + n + 1)
                    heads = bass.ds(t * P, P)
                    for u in range(u0, u1):
                        rows = P if u < BLOCKS else DEC
                        ps = turn_ps[n][0:rows, P * (u - u0):P * (u - u0) + P]
                        if j == V:
                            i = dve.tensor_copy(v_tok[0:rows, u, heads], ps)
                        else:
                            decay = (k_decay if u < BLOCKS else k_decay_dec)[0:rows, bass.ds(2 * t, 2)]
                            i = dve.tensor_tensor(
                                k_tok[0:rows, u, heads].rearrange("p (h n) -> p h n", h=2),
                                ps.rearrange("p (h n) -> p h n", h=2),
                                decay.unsqueeze(2).to_broadcast([rows, 2, HD]), ALU.mult)
                    i.then_inc(turn_free, 1)

        with dve.Fori(0, PAIRS) as t:
            step(t)

    return Stage(sync_early=sync_early, scalar_early=scalar_early, gpsimd_early=gpsimd_early,
                 gpsimd_second=gpsimd_second, weights_split=(lo_done, TILES), end=stage_at,
                 ready=[(proj_free, 4 + 3 * TILES), (k_copied, 3 + 3 * PAIRS), (turn_free, 3 + 6 * PAIRS)],
                 sync=sync, scalar=scalar, gpsimd=gpsimd, tensor=tensor, vector=vector)


def retention_stage(core, at, tables_at, tables_room, ready, tables, g_chunk, g_dec, state_in, q_t, k_t, k_tok, v_tok, state_out,
                    state_dec_out):
    tag = "rt_"
    m = Layout(core.nc, at)
    early = Layout(core.nc, tables_at)
    mask = early.put(tag + "mask", [P, 2, PAIRS, P])
    q_decay = early.put(tag + "q_decay", [P, PAIRS, P])
    mask_dec = early.put(tag + "mask_dec", [P, 2, PAIRS, DEC])
    q_decay_dec = m.put(tag + "q_decay_dec", [P, PAIRS, DEC])
    own = m.put(tag + "own", [P, DEC_BATCH])
    state_dec = m.put(tag + "state_dec", [P, PAIRS, DEC_BATCH, HD])
    v_own = m.put(tag + "v_own", [DEC, HEADS, DEC_BATCH, HD])
    q_dec = [m.put(f"{tag}q_dec{i}", [P, PAIRS, P]) for i in range(2)]
    probs = [m.put(f"{tag}probs{i}", [P, 2, PAIRS * P]) for i in range(2)]
    state = [m.put(f"{tag}state{i}", [P, PAIRS, HD]) for i in range(2)]
    LAST = BLOCKS
    sem = lambda n: core.semaphore(tag + n)
    score_ps, out_ps, kv_ps = [core.banks[4:6], core.banks[6:8]], core.banks[0:2], core.banks[2:4]
    mask_in, decay_in, tables_in, dec_in = map(sem, ("mask_in", "decay_in", "tables_in", "dec_in"))
    scored, masked, q_ready, kv_done, state_done, out_done, out_read, owned, stored, dec_state_done, \
        zeroed = map(sem, ("scored", "masked", "q_ready", "kv_done", "state_done", "out_done",
                           "out_read", "owned", "stored", "dec_state_done", "zeroed"))

    def tokens(n):
        a, b = tile_tokens(n)
        return a, b, b - a

    def head(t, h):
        return slice(HD * (2 * t + h), HD * (2 * t + h) + HD)

    def wait_ready(eng):
        for semaphore, value in ready:
            eng.wait_ge(semaphore, value)

    def sync(sp):
        sp.wait_ge(*tables_room)
        sp.dma_start(mask[:, :, :, :], tables["mask"]).then_inc(mask_in, 16)
        sp.dma_start(q_decay[:, :, :], tables["q_decay"]).then_inc(decay_in, 16)
        sp.dma_start(mask_dec[:, :, :, :], tables["mask_dec"]).then_inc(tables_in, 16)
        wait_ready(sp)
        sp.dma_start(q_decay_dec[:, :, :], tables["q_decay_dec"]).then_inc(tables_in, 16)
        sp.dma_start(own[:, :], tables["own"]).then_inc(tables_in, 16)
        sp.dma_start(state_dec[:, :, :, :], state_in).then_inc(dec_in, 16)
        sp.wait_ge(state_done, PAIRS * BLOCKS)
        sp.dma_start(state_out, state[(BLOCKS - 1) % 2][:, :, :]).then_inc(stored, 16)
        sp.wait_ge(dec_state_done, PAIRS)
        sp.dma_start(state_dec_out, state_dec[:, :, :, :]).then_inc(stored, 16)

    def gpsimd(pool):
        wait_ready(pool)
        pool.wait_ge(decay_in, 16)
        for n in range(LAST + 1):
            a, b, w = tokens(n)
            if n == 1:
                pool.wait_ge(tables_in, 48)
            if n >= 2:
                pool.wait_ge(out_done, n - 1)
            decay = q_decay if n < LAST else q_decay_dec
            pool.tensor_tensor(q_dec[n % 2][:, :, 0:w], q_t[:, :, a:b], decay[:, :, :],
                               ALU.mult).then_inc(q_ready, 1)
            if n >= 1:
                hd = n - 1
                pool.tensor_tensor(
                    v_own[:, hd, :, :],
                    v_tok[0:DEC, LAST, HD * hd:HD * hd + HD].unsqueeze(1).to_broadcast([DEC, DEC_BATCH, HD]),
                    own[0:DEC, :].unsqueeze(2).to_broadcast([DEC, DEC_BATCH, HD]),
                    ALU.mult).then_inc(owned, 1)

    def tensor(pe):
        def scores(n):
            a, b, w = tokens(n)
            if n >= 2:
                pe.wait_ge(masked, 2 * (n - 1))
            for h in range(2):
                d = slice(HD * h, HD * h + HD)
                for t in range(PAIRS):
                    mm = pe.matmul(score_ps[n % 2][h][0:w, w * t:w * t + w], k_t[d, t, a:b], q_t[d, t, a:b],
                                   start=True, stop=True)
                mm.then_inc(scored, 1)

        def key_values(n):
            if n >= 2:
                pe.wait_ge(state_done, PAIRS * (n - 1))
            for t in range(PAIRS):
                for h in range(2):
                    mm = pe.matmul(kv_ps[n % 2][HD * h:HD * h + HD, HD * t:HD * t + HD],
                                   k_tok[:, n, head(t, h)], v_tok[:, n, head(t, h)], start=True, stop=True)
            mm.then_inc(kv_done, 1)

        def output(n):
            a, b, w = tokens(n)
            pe.wait_ge(masked, 2 * n + 2)
            if n == LAST:
                pe.wait_ge(zeroed, 1)
            if n >= 1:
                pe.wait_ge(out_read, 2 * n)
            if 1 <= n < LAST:
                pe.wait_ge(state_done, PAIRS * n)
            pe.wait_ge(q_ready, n + 1)
            if n == LAST:
                pe.wait_ge(dec_in, 16)
            for h in range(2):
                d = slice(HD * h, HD * h + HD)
                for t in range(PAIRS):
                    mm = pe.matmul(out_ps[h][d, w * t:w * t + w], v_tok[:, n, head(t, h)],
                                   probs[n % 2][:, h, w * t:w * t + w], start=True, stop=n == 0)
                    if n == LAST:
                        for s in range(DEC_BATCH):
                            i = slice(DEC_SEQ * s, DEC_SEQ * s + DEC_SEQ)
                            mm = pe.matmul(out_ps[h][d, w * t + i.start:w * t + i.stop],
                                           state_dec[d, t, s, :], q_dec[n % 2][d, t, i],
                                           start=False, stop=s == DEC_BATCH - 1)
                    elif n >= 1:
                        mm = pe.matmul(out_ps[h][d, w * t:w * t + w], state[(n - 1) % 2][d, t, :],
                                       q_dec[n % 2][d, t, 0:w], start=False, stop=True)
            mm.then_inc(out_done, 1)

        for semaphore, value in ready[:2]:
            pe.wait_ge(semaphore, value)
        scores(0)
        for n in range(LAST + 1):
            if n < LAST:
                scores(n + 1)
                if n == 0:
                    wait_ready(pe)
                key_values(n)
            output(n)
        for t in range(PAIRS):
            if t < 2:
                pe.wait_ge(state_done, PAIRS * BLOCKS)
            else:
                pe.wait_ge(dec_state_done, t - 1)
            pe.wait_ge(owned, 2 * t + 2)
            for h in range(2):
                mm = pe.matmul(kv_ps[t % 2][HD * h:HD * h + HD, :], k_tok[0:DEC, LAST, head(t, h)],
                               v_own[:, 2 * t + h, :, :].rearrange("p b e -> p (b e)"), start=True, stop=True)
            mm.then_inc(kv_done, 1)

    def vector(dve):
        wait_ready(dve)
        dve.wait_ge(mask_in, 16)
        for n in range(LAST + 1):
            a, b, w = tokens(n)
            if n == LAST:
                dve.wait_ge(tables_in, 48)
                dve.wait_ge(out_done, n - 1)
                dve.memset(probs[n % 2][DEC:P, :, :], 0.0).then_inc(zeroed, 1)
            for h in range(2):
                dve.wait_ge(scored, 2 * n + h + 1)
                if n >= 2:
                    dve.wait_ge(out_done, n - 1)
                table = (mask if n < LAST else mask_dec)[0:w, h, :, :].rearrange("p t i -> p (t i)")
                dve.tensor_tensor(probs[n % 2][0:w, h, 0:w * PAIRS], score_ps[n % 2][h][0:w, 0:w * PAIRS],
                                  table, ALU.mult).then_inc(masked, 1)
            if n == LAST:
                break
            dve.wait_ge(kv_done, n + 1)
            if n >= 2:
                dve.wait_ge(out_done, n)
            for t in range(PAIRS):
                kv = kv_ps[n % 2][:, HD * t:HD * t + HD]
                if n == 0:
                    dve.tensor_copy(state[0][:, t, :], kv).then_inc(state_done, 1)
                else:
                    dve.wait_ge(state_done, PAIRS * (n - 1) + t + 1)
                    dve.scalar_tensor_tensor(state[n % 2][:, t, :], state[(n - 1) % 2][:, t, :],
                                             g_chunk[:, t:t + 1], kv, ALU.mult, ALU.add).then_inc(state_done, 1)
        dve.wait_ge(out_done, LAST + 1)
        for t in range(PAIRS):
            dve.wait_ge(kv_done, BLOCKS + t + 1)
            s = state_dec[:, t, :, :].rearrange("p b e -> p (b e)")
            dve.scalar_tensor_tensor(s, s, g_dec[:, t:t + 1], kv_ps[t % 2][:, :], ALU.mult, ALU.add)\
               .then_inc(dec_state_done, 1)

    def scalar(act):
        for n in range(LAST + 1):
            a, b, w = tokens(n)
            act.wait_ge(out_done, n + 1)
            act.wait_ge(q_ready, n + 1)
            for h in range(2):
                d = slice(HD * h, HD * h + HD)
                act.activation(q_t[d, :, a:b], out_ps[h][d, 0:w * PAIRS].rearrange("p (t i) -> p t i", i=w),
                               ACT.Copy).then_inc(out_read, 1)

    return Stage(sync=sync, gpsimd=gpsimd, tensor=tensor, vector=vector, scalar=scalar, outputs_stored=(stored, 32))


def group_norm_and_projection_stage(core, at, at_small, gn_sum, gn_spread, ones_head, eps, gn_w, o_t, gate_t,
                                    mix_hi, mix_lo, w_in, xh, xl, ident, q_t, k_t, v_tok, room):
    tag = "gp_"
    K, V = PAIRS, PAIRS + 1
    TILES = PAIRS + 2
    N = len(CHUNKS)
    small = Layout(core.nc, at_small)
    stage = small.put(tag + "stage", [P, 2, D_MODEL])
    v_turn = small.put(tag + "v_turn", [P, TOK])
    w_lo1 = small.put(tag + "w_lo1", [P, D_MODEL], F32R)
    m = Layout(core.nc, at)
    w_hi = [m.put(f"{tag}w_hi{s}", [P, D_MODEL], F32R) for s in range(2)]
    w_lo = [m.put(tag + "w_lo0", [P, D_MODEL], F32R), w_lo1]
    sum_w = m.put(tag + "sum_w", [P, PAIRS, HEADS])
    spread_w = m.put(tag + "spread_w", [HEADS, PAIRS, P])
    squares = [m.put(f"{tag}squares{i}", [P, PAIRS, CW]) for i in range(2)]
    rstd = m.put(tag + "rstd", [HEADS, CW])
    sem = lambda n: core.semaphore(tag + n)
    mean_ps, var_ps, spread_ps, ps = core.banks[0:2], core.banks[2], core.banks[3:5], core.banks[5:8]
    turn_ps = core.banks[0:2]
    tables_in, mean_done, centred, squared, var_done, std_done, rstd_done, spread_done, scaled, \
        gated, mix_hi_done, mix_lo_done = map(sem, (
            "tables_in", "mean_done", "centred", "squared", "var_done", "std_done", "rstd_done",
            "spread_done", "scaled", "gated", "mix_hi_done", "mix_lo_done"))
    staged = [sem(f"staged{s}") for s in range(2)]
    hi_done, lo_done = sem("hi_done"), sem("lo_done")
    proj_done, proj_free = sem("proj_done"), sem("proj_free")
    turned, turn_free, zeroed = sem("turned"), sem("turn_free"), sem("zeroed")

    def sync(sp):
        sp.wait_ge(*room)
        sp.dma_start(stage[:, 0, :], w_in[0]).then_inc(staged[0], 16)
        sp.dma_start(sum_w[:, :, :], gn_sum).then_inc(tables_in, 16)
        sp.dma_start(spread_w[:, :, :], gn_spread).then_inc(tables_in, 16)
        for n in range(1, TILES):
            if n >= 2:
                sp.wait_ge(lo_done, n - 1)
            sp.dma_start(stage[:, n % 2, :], w_in[n]).then_inc(staged[n % 2], 16)

    def tensor(pe):
        def means(c):
            a, b = CHUNKS[c]
            for t in range(PAIRS):
                u = PAIRS * c + t
                if u >= 2:
                    pe.wait_ge(centred, u - 1)
                pe.matmul(mean_ps[u % 2][:, 0:b - a], ones_head[:, :], o_t[:, t, a:b],
                          start=True, stop=True).then_inc(mean_done, 1)

        def variance(c):
            a, b = CHUNKS[c]
            pe.wait_ge(squared, c + 1)
            if c:
                pe.wait_ge(std_done, c)
            for t in range(PAIRS):
                mm = pe.matmul(var_ps[0:HEADS, 0:b - a], sum_w[:, t, :], squares[c % 2][:, t, 0:b - a],
                               start=t == 0, stop=t == PAIRS - 1)
            mm.then_inc(var_done, 1)

        def spread(c):
            a, b = CHUNKS[c]
            pe.wait_ge(rstd_done, c + 1)
            for t in range(PAIRS):
                u = PAIRS * c + t
                if u >= 2:
                    pe.wait_ge(scaled, u - 1)
                pe.matmul(spread_ps[u % 2][:, 0:b - a], spread_w[:, t, :], rstd[:, 0:b - a],
                          start=True, stop=True).then_inc(spread_done, 1)

        def project(n):
            pe.wait_ge(lo_done, n + 1)
            for c, (a, b) in enumerate(CHUNKS):
                if n:
                    pe.wait_ge(proj_free, N * (n - 1) + c + 1)
                project_tile(pe, ps[c], w_hi[n % 2], w_lo[n % 2], xh, xl, a, b).then_inc(proj_done, 1)

        means(0)
        project(0)
        means(1)
        pe.wait_ge(tables_in, 32)
        variance(0)
        project(1)
        spread(0)
        means(2)
        variance(1)
        project(2)
        spread(1)
        variance(2)
        project(3)
        spread(2)
        project(K)
        project(V)
        pe.wait_ge(centred, PAIRS * N)
        pe.wait_ge(proj_free, N * TILES)
        for n, (u0, u1) in enumerate(TURN_BATCHES):
            if n == 2:
                pe.wait_ge(turn_free, 1)
            for u in range(u0, u1):
                a, b = tile_tokens(u)
                mm = pe.transpose(turn_ps[n % 2][0:b - a, P * (u - u0):P * (u - u0) + P], v_turn[:, a:b],
                                  ident[:, :])
            mm.then_inc(turned, 1)

    def vector(dve):
        def centre(c):
            a, b = CHUNKS[c]
            for t in range(PAIRS):
                dve.wait_ge(mean_done, PAIRS * c + t + 1)
                dve.tensor_tensor(o_t[:, t, a:b], o_t[:, t, a:b], mean_ps[(PAIRS * c + t) % 2][:, 0:b - a],
                                  ALU.subtract).then_inc(centred, 1)

        def invert(c):
            a, b = CHUNKS[c]
            dve.wait_ge(std_done, c + 1)
            dve.reciprocal(rstd[:, 0:b - a], rstd[:, 0:b - a]).then_inc(rstd_done, 1)

        def gate(c):
            a, b = CHUNKS[c]
            for t in range(PAIRS):
                u = PAIRS * c + t
                dve.wait_ge(spread_done, u + 1)
                dve.wait_ge(centred, u + 1)
                dve.wait_ge(squared, c + 1)
                dve.scalar_tensor_tensor(o_t[:, t, a:b], o_t[:, t, a:b], gn_w[:, t:t + 1],
                                         spread_ps[u % 2][:, 0:b - a], ALU.mult, ALU.mult).then_inc(scaled, 1)
            for t in range(PAIRS):
                dve.wait_ge(scaled, PAIRS * c + t + 1)
                dve.tensor_tensor(o_t[:, t, a:b], o_t[:, t, a:b], gate_t[:, t, a:b],
                                  ALU.mult).then_inc(gated, 1)

        centre(0)
        centre(1)
        invert(0)
        gate(0)
        centre(2)
        invert(1)
        gate(1)
        invert(2)
        gate(2)
        dve.wait_ge(zeroed, 1)
        for n, (u0, u1) in enumerate(TURN_BATCHES):
            dve.wait_ge(turned, n + 1)
            for u in range(u0, u1):
                rows = P if u < BLOCKS else DEC
                i = dve.tensor_copy(v_tok[0:rows, u, :], turn_ps[n % 2][0:rows, P * (u - u0):P * (u - u0) + P])
            i.then_inc(turn_free, 1)

    def scalar(act):
        def square(c):
            a, b = CHUNKS[c]
            act.wait_ge(centred, PAIRS * c + PAIRS)
            if c >= 2:
                act.wait_ge(var_done, c - 1)
            act.activation(squares[c % 2][:, :, 0:b - a], o_t[:, :, a:b], ACT.Square).then_inc(squared, 1)

        def deviation(c):
            a, b = CHUNKS[c]
            act.wait_ge(var_done, c + 1)
            if c:
                act.wait_ge(spread_done, PAIRS * c)
            act.activation(rstd[:, 0:b - a], var_ps[0:HEADS, 0:b - a], ACT.Sqrt,
                           bias=eps[0:HEADS, 0:1]).then_inc(std_done, 1)

        def round_mix(c):
            a, b = CHUNKS[c]
            act.wait_ge(gated, PAIRS * c + PAIRS)
            act.activation(mix_hi[:, 0:PAIRS, a:b], o_t[:, :, a:b], ACT.Copy).then_inc(mix_hi_done, 1)

        def round_tile(n):
            act.wait_ge(staged[n % 2], 16 * (n // 2) + 16)
            if n >= 2:
                act.wait_ge(proj_done, N * (n - 1))
            act.activation(w_hi[n % 2][:, :], stage[:, n % 2, :], ACT.Copy).then_inc(hi_done, 1)

        def evacuate(n):
            for c, (a, b) in enumerate(CHUNKS):
                act.wait_ge(proj_done, N * n + c + 1)
                out = q_t[:, n, a:b] if n < PAIRS else k_t[:, a:b] if n == K else v_turn[:, a:b]
                act.activation(out, ps[c][:, 0:b - a], ACT.Copy).then_inc(proj_free, 1)

        round_tile(0)
        round_tile(1)
        square(0)
        evacuate(0)
        round_tile(2)
        square(1)
        deviation(0)
        evacuate(1)
        round_tile(3)
        deviation(1)
        round_mix(0)
        square(2)
        evacuate(2)
        round_tile(K)
        deviation(2)
        round_mix(1)
        evacuate(3)
        round_tile(V)
        round_mix(2)
        evacuate(K)
        evacuate(V)

    def gpsimd(pool):
        def split_tile(n):
            pool.wait_ge(hi_done, n + 1)
            pool.tensor_tensor(w_lo[n % 2][:, :], stage[:, n % 2, :], w_hi[n % 2][:, :].bitcast(F32),
                               ALU.subtract).then_inc(lo_done, 1)

        def split_mix(c):
            a, b = CHUNKS[c]
            pool.wait_ge(mix_hi_done, c + 1)
            pool.tensor_tensor(mix_lo[:, 0:PAIRS, a:b], o_t[:, :, a:b], mix_hi[:, 0:PAIRS, a:b].bitcast(F32),
                               ALU.subtract).then_inc(mix_lo_done, 1)

        pool.memset(v_tok[:, BLOCKS, :], 0.0).then_inc(zeroed, 1)
        split_tile(0)
        split_tile(1)
        split_tile(2)
        split_tile(3)
        split_mix(0)
        split_tile(K)
        split_mix(1)
        split_tile(V)
        split_mix(2)

    return Stage(sync=sync, tensor=tensor, vector=vector, scalar=scalar, gpsimd=gpsimd)


def attention_stage(core, at, at_caches, tables, sinks, sinks_dec, caches, q_t, k_t, v_tok, ident,
                    mix_hi, mix_lo, outs):
    tag = "at_"
    m = Layout(core.nc, at)
    SLOTS = 4
    scores = [m.put(f"{tag}scores{i}", [P, GROUP * 2 * P]) for i in range(SLOTS)]
    turned = [[m.put(f"{tag}turned{i}{kb}", [P, GROUP * P]) for kb in range(2)] for i in range(2)]
    stats = [m.put(f"{tag}stats{i}", [P, 6, GROUP]) for i in range(SLOTS)]
    turned_new = m.put(tag + "turned_new", [P, 2 * P])
    q_rows = m.put(tag + "q_rows", [P, DEC_BATCH, GROUP, DEC_SEQ])
    TOP, NEG, SUM, SINK, DEN, INV = range(6)
    mc = Layout(core.nc, at_caches)
    bias = mc.put(tag + "bias", [P, KVH, GROUP, 2 * P])
    bias_dec = mc.put(tag + "bias_dec", [P, KVH, 2, P + DEC])
    k_cache = mc.put(tag + "k_cache", [P, DEC_BATCH, WINDOW])
    v_cache = mc.put(tag + "v_cache", [P, DEC_BATCH, P])
    ITEMS = [(n, h) for n in range(BLOCKS + 1) for h in range(KVH)]
    LAST = len(ITEMS)
    KEYS = P + DEC
    sem = lambda n: core.semaphore(tag + n)
    score_ps, turn_ps, out_ps = [core.banks[0:2], core.banks[2:4]], core.banks[4:6], core.banks[6:8]
    bias_in = [sem(f"bias_in{h}") for h in range(KVH)]
    tables_in, dec_in, scored, biased, maxed, topped, negated, sunk, exped, sink_exped, summed, inverted, \
        normed, turn_done, turn_read, out_done, hi_done, lo_done, stored, cached, q_ordered = map(sem, (
            "tables_in", "dec_in", "scored", "biased", "maxed", "topped", "negated", "sunk",
            "exped", "sink_exped", "summed", "inverted", "normed", "turn_done", "turn_read",
            "out_done", "hi_done", "lo_done", "stored", "cached", "q_ordered"))

    def shape(i):
        n, h = ITEMS[i]
        if n == BLOCKS:
            return 2, 0, KEYS
        return GROUP, (P if n == 0 else 0), 2 * P

    def scores_of(i):
        n, h = ITEMS[i]
        groups, k0, k1 = shape(i)
        width = KEYS if n == BLOCKS else 2 * P
        return scores[i % SLOTS][:, 0:groups * width].rearrange("p (g k) -> p g k", g=groups)[:, :, k0:k1]

    def per_group(i, what):
        return stats[i % SLOTS][:, what, 0:shape(i)[0]]

    def sinks_of(i):
        n, h = ITEMS[i]
        if n == BLOCKS:
            return sinks_dec[:, h:h + 1].to_broadcast([P, 2])
        return sinks[:, GROUP * h:GROUP * h + GROUP]

    def sync(sp):
        for h in range(KVH):
            sp.dma_start(bias[:, h, :, :], tables["bias"][:, h, :, :]).then_inc(bias_in[h], 16)
        sp.dma_start(bias_dec[:, :, :, :], tables["bias_dec"]).then_inc(tables_in, 16)
        sp.dma_start(k_cache[:, :, :], caches["k"]).then_inc(dec_in, 16)
        sp.dma_start(v_cache[:, :, :], caches["v"]).then_inc(dec_in, 16)
        sp.dma_start(outs["k_prompt"], k_t[:, SEQ - WINDOW:SEQ]).then_inc(stored, 16)
        sp.dma_start(outs["v_prompt"], v_tok[:, BLOCKS - 1, :]).then_inc(stored, 16)
        sp.dma_start(outs["k_dec"][:, :, WINDOW - DEC_SEQ:WINDOW],
                     k_t[:, SEQ:TOK].rearrange("p (b i) -> p b i", i=DEC_SEQ)).then_inc(stored, 16)
        for s in range(DEC_BATCH):
            sp.dma_start(outs["v_dec"][s, WINDOW - DEC_SEQ:WINDOW, :],
                         v_tok[DEC_SEQ * s:DEC_SEQ * s + DEC_SEQ, BLOCKS, :]).then_inc(stored, 16)
        sp.wait_ge(dec_in, 32)
        sp.dma_start(outs["k_dec"][:, :, 0:WINDOW - DEC_SEQ], k_cache[:, :, DEC_SEQ:WINDOW]).then_inc(stored, 16)
        sp.dma_start(outs["v_dec"][:, 0:WINDOW - DEC_SEQ, :].rearrange("b k n -> k b n"),
                     v_cache[DEC_SEQ:WINDOW, :, :]).then_inc(stored, 16)
        sp.wait_ge(stored, 16 * (5 + DEC_BATCH))

    def tensor(pe):
        def score(i):
            n, h = ITEMS[i]
            d = slice(HD * h, HD * h + HD)
            if i >= 2:
                pe.wait_ge(biased, i - 1)
            if n == BLOCKS:
                pe.wait_ge(dec_in, 32)
                pe.wait_ge(q_ordered, GROUP)
                for s in range(DEC_BATCH):
                    rows = slice(32 * (s % 4), 32 * (s % 4) + 32)
                    half = KEYS * (s // 4)
                    q = q_rows[d, s, :, :].rearrange("p t i -> p (t i)")
                    pe.matmul(score_ps[i % 2][0][rows, half:half + P], q, k_cache[d, s, :], start=True, stop=True)
                    mm = pe.matmul(score_ps[i % 2][0][rows, half + P:half + KEYS], q, k_t[d, SEQ:TOK],
                                   start=True, stop=True)
            else:
                k0 = P if n == 0 else 0
                for t in range(GROUP):
                    col = 2 * P * (t % 2)
                    mm = pe.matmul(score_ps[i % 2][t // 2][:, col + k0:col + 2 * P],
                                   q_t[d, t, P * n:P * n + P], k_t[d, P * (n - 1) + k0:P * (n + 1)],
                                   start=True, stop=True)
            mm.then_inc(scored, 1)

        def transposes(i):
            n, h = ITEMS[i]
            pe.wait_ge(normed, i + 1)
            if i:
                pe.wait_ge(turn_read, 2 * i)
            p = scores[i % SLOTS]
            if n == BLOCKS:
                for half in range(2):
                    pe.transpose(turn_ps[0][:, P * half:P * half + P], p[:, KEYS * half:KEYS * half + P], ident[:, :])
                for half in range(2):
                    mm = pe.transpose(turn_ps[1][0:DEC, P * half:P * half + P],
                                      p[:, KEYS * half + P:KEYS * half + KEYS], ident[:, :])
            else:
                for kb in range(1 if n == 0 else 0, 2):
                    for t in range(GROUP):
                        mm = pe.transpose(turn_ps[kb][:, P * t:P * t + P],
                                          p[:, P * (2 * t + kb):P * (2 * t + kb) + P], ident[:, :])
            mm.then_inc(turn_done, 1)

        def output(i):
            n, h = ITEMS[i]
            d = slice(HD * h, HD * h + HD)
            pe.wait_ge(turn_read, 2 * i + 2)
            if i >= 2:
                pe.wait_ge(lo_done, i - 1)
            if n == BLOCKS:
                for half in range(2):
                    mm = pe.matmul(out_ps[h][d, P * half:P * half + P], v_tok[:, BLOCKS, d],
                                   turned_new[:, P * half:P * half + P], start=True, stop=False)
                    for s in range(4 * half, 4 * half + 4):
                        col = slice(32 * s, 32 * s + 32)
                        mm = pe.matmul(out_ps[h][d, col], v_cache[:, s, d], turned[i % 2][0][:, col],
                                       start=False, stop=s % 4 == 3)
            else:
                first = 1 if n == 0 else 0
                for kb in range(first, 2):
                    mm = pe.matmul(out_ps[h][d, :], v_tok[:, n - 1 + kb, d], turned[i % 2][kb][:, :],
                                   start=kb == first, stop=kb == 1)
            mm.then_inc(out_done, 1)

        for i in range(SLOTS):
            score(i)
        for i in range(LAST + 1):
            if i < LAST:
                transposes(i)
            if i + SLOTS < LAST:
                score(i + SLOTS)
            if i:
                output(i - 1)

    def vector(dve):
        def add_bias(i):
            n, h = ITEMS[i]
            groups, k0, k1 = shape(i)
            dve.wait_ge(tables_in if n == BLOCKS else bias_in[h], 16)
            dve.wait_ge(scored, i + 1)
            if i >= SLOTS:
                dve.wait_ge(turn_done, i - SLOTS + 1)
            out = scores_of(i)
            if n == BLOCKS:
                ps = score_ps[i % 2][0][:, 0:2 * KEYS].rearrange("p (g k) -> p g k", g=2)
                dve.scalar_tensor_tensor(out, ps, QSCALE, bias_dec[:, h, :, :], ALU.mult, ALU.add)\
                   .then_inc(biased, 1)
            else:
                for j in range(2):
                    ps = score_ps[i % 2][j][:, :].rearrange("p (g k) -> p g k", g=2)[:, :, k0:k1]
                    x = dve.scalar_tensor_tensor(out[:, 2 * j:2 * j + 2, :], ps, QSCALE,
                                                 bias[:, h, 2 * j:2 * j + 2, k0:k1], ALU.mult, ALU.add)
                x.then_inc(biased, 1)

        def top(i):
            dve.wait_ge(biased, i + 1)
            if i >= SLOTS:
                dve.wait_ge(normed, i - SLOTS + 1)
            dve.tensor_reduce(per_group(i, TOP), scores_of(i), AX.X, ALU.max).then_inc(maxed, 1)
            dve.wait_ge(maxed, i + 1)
            dve.tensor_tensor(per_group(i, TOP), per_group(i, TOP), sinks_of(i), ALU.max).then_inc(topped, 1)
            dve.wait_ge(topped, i + 1)
            dve.tensor_tensor(per_group(i, SINK), sinks_of(i), per_group(i, TOP), ALU.subtract).then_inc(sunk, 1)
            dve.tensor_scalar(per_group(i, NEG), per_group(i, TOP), -1.0, None, ALU.mult).then_inc(negated, 1)

        def denominator(i):
            dve.wait_ge(sink_exped, i + 1)
            dve.tensor_tensor(per_group(i, DEN), per_group(i, SUM), per_group(i, SINK), ALU.add).then_inc(summed, 1)
            dve.wait_ge(summed, i + 1)
            dve.reciprocal(per_group(i, INV), per_group(i, DEN)).then_inc(inverted, 1)

        def low_part(i):
            n, h = ITEMS[i]
            d = slice(HD * h, HD * h + HD)
            dve.wait_ge(hi_done, i + 1)
            if n == BLOCKS:
                for t in range(GROUP):
                    x = dve.tensor_tensor(
                        mix_lo[d, PAIRS + t, SEQ:TOK].rearrange("p (b i) -> p b i", i=DEC_SEQ),
                        out_ps[h][d, 0:2 * P].rearrange("p (b t i) -> p b t i", t=GROUP, i=DEC_SEQ)[:, :, t, :],
                        mix_hi[d, PAIRS + t, SEQ:TOK].rearrange("p (b i) -> p b i", i=DEC_SEQ).bitcast(F32),
                        ALU.subtract)
                x.then_inc(lo_done, 1)
            else:
                dve.tensor_tensor(mix_lo[d, PAIRS:2 * PAIRS, P * n:P * n + P],
                                  out_ps[h][d, :].rearrange("p (t q) -> p t q", t=GROUP),
                                  mix_hi[d, PAIRS:2 * PAIRS, P * n:P * n + P].bitcast(F32),
                                  ALU.subtract).then_inc(lo_done, 1)

        for i in range(-SLOTS, LAST + 2):
            if i + SLOTS < LAST:
                add_bias(i + SLOTS)
                top(i + SLOTS)
            if 0 <= i + SLOTS - 1 < LAST:
                denominator(i + SLOTS - 1)
            if i >= 2:
                low_part(i - 2)

    def scalar(act):
        def exponentials(i):
            n, h = ITEMS[i]
            act.wait_ge(negated, i + 1)
            s = scores_of(i)
            for g in range(shape(i)[0]):
                act.activation(s[:, g, :], s[:, g, :], ACT.Exp, bias=stats[i % SLOTS][:, NEG, g:g + 1],
                               accum_out=stats[i % SLOTS][:, SUM, g:g + 1]).then_inc(exped, 1)
            act.activation(per_group(i, SINK), per_group(i, SINK), ACT.Exp).then_inc(sink_exped, 1)

        def read_turned(i):
            n, h = ITEMS[i]
            act.wait_ge(turn_done, i + 1)
            if i >= 2:
                act.wait_ge(out_done, i - 1)
            for kb in range(2):
                if n == 0 and kb == 0:
                    act.sem_inc(turn_read, 1)
                    continue
                rows = DEC if n == BLOCKS and kb == 1 else P
                cols = 2 * P if n == BLOCKS else GROUP * P
                if rows < P:
                    if h == 0:
                        act.wait_ge(cached, 1)
                    else:
                        act.wait_ge(out_done, i)
                to = turned_new if n == BLOCKS and kb == 1 else turned[i % 2][kb]
                act.activation(to[0:rows, 0:cols], turn_ps[kb][0:rows, 0:cols], ACT.Copy)\
                   .then_inc(turn_read, 1)

        def high_part(i):
            n, h = ITEMS[i]
            d = slice(HD * h, HD * h + HD)
            act.wait_ge(out_done, i + 1)
            if n == BLOCKS:
                for t in range(GROUP):
                    x = act.activation(
                        mix_hi[d, PAIRS + t, SEQ:TOK].rearrange("p (b i) -> p b i", i=DEC_SEQ),
                        out_ps[h][d, 0:2 * P].rearrange("p (b t i) -> p b t i", t=GROUP, i=DEC_SEQ)[:, :, t, :],
                        ACT.Copy)
                x.then_inc(hi_done, 1)
            else:
                act.activation(mix_hi[d, PAIRS:2 * PAIRS, P * n:P * n + P],
                               out_ps[h][d, :].rearrange("p (t q) -> p t q", t=GROUP), ACT.Copy).then_inc(hi_done, 1)

        for i in range(SLOTS):
            exponentials(i)
        for i in range(LAST + 1):
            if i < LAST:
                read_turned(i)
            if i + SLOTS < LAST:
                exponentials(i + SLOTS)
            if i:
                high_part(i - 1)

    def gpsimd(pool):
        for t in range(GROUP):
            pool.tensor_copy(q_rows[:, :, t, :], q_t[:, t, SEQ:TOK].rearrange("p (b i) -> p b i", i=DEC_SEQ))\
                .then_inc(q_ordered, 1)
        pool.memset(turned_new[:, :], 0.0).then_inc(cached, 1)
        for i in range(LAST):
            n, h = ITEMS[i]
            groups, k0, k1 = shape(i)
            pool.wait_ge(inverted, i + 1)
            s = scores_of(i)
            pool.tensor_tensor(s, s, per_group(i, INV).unsqueeze(2).to_broadcast([P, groups, k1 - k0]),
                               ALU.mult).then_inc(normed, 1)

    return Stage(sync=sync, tensor=tensor, vector=vector, scalar=scalar, gpsimd=gpsimd)


def output_projection_stage(core, at, w_out, mix_hi, mix_lo, xh, xl, acc, norm):
    tag = "op_"
    m = Layout(core.nc, at)
    SLOTS = 3
    stage = m.put(tag + "stage", [P, 2, D_MODEL])
    w_hi = [m.put(f"{tag}w_hi{s}", [P, D_MODEL], F32R) for s in range(SLOTS)]
    w_lo = [m.put(f"{tag}w_lo{s}", [P, D_MODEL], F32R) for s in range(SLOTS)]
    sem = lambda n: core.semaphore(tag + n)
    BANKS = 6
    ps = core.banks[0:BANKS]
    staged = [sem(f"staged{s}") for s in range(2)]
    hi_done, lo_done = sem("hi_done"), sem("lo_done")
    proj_done = sem("proj_done")
    proj_free = sem("proj_free")
    summed = sem("summed")
    N = len(CHUNKS)

    def sync(sp):
        for s in range(2):
            sp.dma_start(stage[:, s, :], w_out[s]).then_inc(staged[s], 16)
        for n in range(2, N * KT):
            sp.wait_ge(lo_done, n - 1)
            sp.dma_start(stage[:, n % 2, :], w_out[n % KT]).then_inc(staged[n % 2], 16)

    def scalar(act):
        def round_tiles(n0, n1):
            for n in range(n0, n1):
                act.wait_ge(staged[n % 2], 16 * (n // 2) + 16)
                if n >= SLOTS:
                    act.wait_ge(proj_done, n - SLOTS + 1)
                act.activation(w_hi[n % SLOTS][:, :], stage[:, n % 2, :], ACT.Copy).then_inc(hi_done, 1)

        round_tiles(0, KT + 2)
        for c in range(1, N):
            n = KT * c
            round_tiles(n + 2, n + 5)
            norm.square(act, c - 1)
            round_tiles(n + 5, n + 7)
            norm.deviation(act, c - 1)
            round_tiles(n + 7, min(n + 10, KT * N))
            norm.round(act, c - 1)

    def gpsimd(pool):
        for n in range(N * KT):
            pool.wait_ge(hi_done, n + 1)
            pool.tensor_tensor(w_lo[n % SLOTS][:, :], stage[:, n % 2, :], w_hi[n % SLOTS][:, :].bitcast(F32),
                               ALU.subtract).then_inc(lo_done, 1)

    def tensor(pe):
        def items(c, ds):
            a, b = CHUNKS[c]
            for d in ds:
                n = KT * c + d
                pe.wait_ge(lo_done, n + 1)
                pe.wait_ge(proj_free, n + 1)
                project_tile(pe, ps[n % BANKS], w_hi[n % SLOTS], w_lo[n % SLOTS], mix_hi, mix_lo, a, b).then_inc(proj_done, 1)

        items(0, range(KT))
        for c in range(1, N):
            items(c, range(0, 2))
            norm.mean(pe, c - 1)
            items(c, range(2, 5))
            norm.variance(pe, c - 1)
            items(c, range(5, KT))

    def vector(dve):
        dve.sem_inc(proj_free, BANKS)

        def sums(c, ds):
            a, b = CHUNKS[c]
            for d in ds:
                n = KT * c + d
                dve.wait_ge(proj_done, n + 1)
                dve.scalar_tensor_tensor(acc[:, d, a:b], xh[:, d, a:b].bitcast(F32), ALPHA, ps[n % BANKS][:, 0:b - a],
                                         ALU.mult, ALU.add).then_inc(proj_free, 1)
                dve.wait_ge(proj_free, BANKS + n + 1)
                dve.scalar_tensor_tensor(acc[:, d, a:b], xl[:, d, a:b].bitcast(F32), ALPHA, acc[:, d, a:b],
                                         ALU.mult, ALU.add).then_inc(summed, 1)

        sums(0, range(KT))
        for c in range(1, N):
            norm.gather(dve, c - 1, (summed, KT * c))
            sums(c, range(0, 2))
            norm.centre(dve, c - 1)
            sums(c, range(2, 4))
            norm.fold(dve, c - 1)
            if c >= 2:
                norm.low_part(dve, c - 2)
                norm.finish(dve, c - 2)
            sums(c, range(4, 6))
            norm.normalise(dve, c - 1)
            sums(c, range(6, KT))
        norm.gather(dve, N - 1, (summed, KT * N))
        norm.centre(dve, N - 1)
        norm.low_part(dve, N - 2)
        norm.fold(dve, N - 1)
        norm.finish(dve, N - 2)
        norm.normalise(dve, N - 1)
        norm.low_part(dve, N - 1)
        norm.finish(dve, N - 1)

    return Stage(sync=sync, scalar=scalar, gpsimd=gpsimd, tensor=tensor, vector=vector,
                 products_done=(proj_done, KT * N))


SMALL = {}
for _name, _width in (("ln_gain", 3 * KT), ("ln_bias", 3 * KT), ("gn_w", PAIRS), ("g_chunk", PAIRS),
                      ("g_dec", PAIRS), ("sinks", HEADS), ("sinks_dec", KVH), ("k_decay", HEADS),
                      ("k_decay_dec", HEADS), ("ident", P)):
    _at = sum(s.stop - s.start for s in SMALL.values())
    SMALL[_name] = slice(_at, _at + _width)
SMALL_W = SMALL["ident"].stop


def decoder_layer_kernel(nc, i, o):
    with ExitStack() as ctx:
        core = Core(
            nc=nc, semaphore=lambda name: ctx.enter_context(nc.semaphore(name)),
            banks=[ctx.enter_context(nc.psum_tensor(f"bank{n}", [P, 512], F32)) for n in range(8)])
        decoder_layer(core, i, o)


def one_stage_block(nc, stage):
    with nc.Block() as block:
        block.sync(stage.sync)
        block.tensor(stage.tensor)
        block.vector(stage.vector)
        block.scalar(stage.scalar)
        block.gpsimd(stage.gpsimd)


def decoder_layer(core, i, o):
    nc = core.nc
    base = Layout(nc, -(-nc.sbuf_base // 32) * 32)
    x_at = base.at
    xh = base.put("x_hi", [P, KT, TOK], F32R)
    xl = base.put("x_lo", [P, KT, TOK], F32R)
    small = base.put("small", [P, SMALL_W + 1])
    ones_mean = base.put("ones_mean", [P, P])
    ones_head = base.put("ones_head", [P, P])
    eps = small[:, SMALL_W:SMALL_W + 1]
    part = lambda name: small[:, SMALL[name]]
    ident = part("ident")
    mixer_at = base.at
    acc = base.put("acc", [P, KT, TOK])
    free = base.at

    gain = lambda n: small[:, SMALL["ln_gain"].start + KT * n:SMALL["ln_gain"].start + KT * n + KT]
    shift = lambda n: small[:, SMALL["ln_bias"].start + KT * n:SMALL["ln_bias"].start + KT * n + KT]

    m = Layout(nc, mixer_at)
    ret_q = m.put("ret_q", [P, PAIRS, TOK])
    ret_gate = m.put("ret_gate", [P, PAIRS, TOK])
    m = Layout(nc, free)
    ret_k = m.put("ret_k", [P, PAIRS, TOK])
    ret_k_tok = m.put("ret_k_tok", [P, TOKEN_TILES, HEADS * HD])
    ret_v_tok = m.put("ret_v_tok", [P, TOKEN_TILES, HEADS * HD])
    ret_at = m.at
    m = Layout(nc, free)
    mix_hi = m.put("mix_hi", [P, KT, TOK], F32R)
    mix_lo = m.put("mix_lo", [P, KT, TOK], F32R)
    mix_end = m.at
    att_q = Layout(nc, free + 4 * PAIRS * TOK).put("att_q", [P, PAIRS, TOK])
    mix_lo_att_at = free + 3 * 4 * PAIRS * TOK
    m = Layout(nc, mix_end)
    att_k = m.put("att_k", [P, TOK])
    att_v_tok = m.put("att_v_tok", [P, TOKEN_TILES, P])
    att_end = m.at
    norm_work = Layout(nc, x_at).put("norm_work", [P, 2 * KT, TOK])
    norm_rstd, norm_work = norm_work[:, KT - 1, :], norm_work[:, KT:2 * KT, :]
    padded = lambda n: -(-4 * n // 32) * 32
    stage_at = free + 12 * padded(D_MODEL) + 4 * padded(TOK) + 2 * padded(3 * CW)
    first_at = stage_at + padded(3 * D_MODEL)

    load = load_stage(core, i["x"], i["small"], small, ones_mean, ones_head, eps, acc, xh, xl)
    norm1 = Norm(core, "n1_", 0.5, acc, gain(0), shift(0), ones_mean, eps, norm_work, norm_rstd,
                 (core.banks[1], core.banks[3]), xh, xl)
    ffn1 = ffn_stage(core, "f1_", free, stage_at, i["ffn1"], acc, xh, xl, load.x_ready, 1, load.acc_ready, norm1)
    ret_proj = retention_projection_stage(core, ret_at, first_at, i["w_ret"],
                                          (part("k_decay"), part("k_decay_dec")), xh, xl, ident, ret_q, ret_k,
                                          ret_gate, ret_k_tok, ret_v_tok, norm1, ffn1.products_done,
                                          ffn1.acc_ready)
    retention = retention_stage(core, ret_at, ret_proj.end, ret_proj.weights_split, ret_proj.ready, i, part("g_chunk"),
                                part("g_dec"), i["state"], ret_q, ret_k, ret_k_tok, ret_v_tok,
                                o["state_prompt"], o["state_dec"])
    with nc.Block() as block:

        @block.sync
        def _(sp):
            load.sync_x(sp, 0)
            ffn1.sync_early(sp)
            load.sync_x(sp, 1)
            load.sync_x(sp, 2)
            load.sync_small(sp)
            ret_proj.sync_early(sp)
            ffn1.sync(sp)
            ret_proj.sync(sp)
            retention.sync(sp)

        @block.gpsimd
        def _(pool):
            load.gpsimd(pool)
            ffn1.gpsimd_early(pool)
            ret_proj.gpsimd_early(pool)
            ffn1.gpsimd(pool)
            norm1.gather(pool, 1, ffn1.second_ready)
            norm1.low_part(pool, 0)
            ret_proj.gpsimd_second(pool)
            norm1.low_part(pool, 1)
            ret_proj.gpsimd(pool)
            retention.gpsimd(pool)

        @block.scalar
        def _(act):
            load.scalar(act, 0)
            ffn1.scalar_early(act)
            load.scalar(act, 1)
            load.scalar(act, 2)
            ret_proj.scalar_early(act)
            ffn1.scalar(act)
            ret_proj.scalar(act)
            retention.scalar(act)

        @block.vector
        def _(dve):
            load.vector(dve)
            ffn1.vector(dve)
            norm1.low_part(dve, 2)
            ret_proj.vector(dve)
            retention.vector(dve)

        @block.tensor
        def _(pe):
            ffn1.tensor(pe)
            ret_proj.tensor(pe)
            retention.tensor(pe)

    one_stage_block(nc, group_norm_and_projection_stage(
        core, att_end, mix_lo_att_at, i["gn_sum"], i["gn_spread"], ones_head, eps, part("gn_w"), ret_q, ret_gate,
        mix_hi, mix_lo, i["w_att"], xh, xl, ident, att_q, att_k, att_v_tok, retention.outputs_stored))
    one_stage_block(nc, attention_stage(core, att_end, mixer_at, i, part("sinks"), part("sinks_dec"),
                                        {"k": i["k_cache"], "v": i["v_cache"]}, att_q, att_k, att_v_tok, ident,
                                        mix_hi, mix_lo, o))

    norm2 = Norm(core, "n2_", 1.0, acc, gain(1), shift(1), ones_mean, eps, norm_work, norm_rstd,
                 core.banks[6:8], xh, xl, rescale=2 * ALPHA)
    out_proj = output_projection_stage(core, mix_end, i["w_out"], mix_hi, mix_lo, xh, xl, acc, norm2)
    norm3 = Norm(core, "n3_", 0.5, acc, gain(2), shift(2), ones_mean, eps, norm_work, norm_rstd,
                 (core.banks[1], core.banks[3]), y_out=o["y"])
    ffn2 = ffn_stage(core, "f2_", free, stage_at, i["ffn2"], acc, xh, xl, norm2.x_ready, 2, norm2.acc_ready,
                     norm3, norm2, room=out_proj.products_done)
    with nc.Block() as block:

        @block.sync
        def _(sp):
            out_proj.sync(sp)
            ffn2.sync_early(sp)
            ffn2.sync(sp)
            norm3.store(sp)

        @block.gpsimd
        def _(pool):
            out_proj.gpsimd(pool)
            ffn2.gpsimd_early(pool)
            ffn2.gpsimd(pool)
            norm3.gather(pool, 1, ffn2.second_ready)

        @block.scalar
        def _(act):
            out_proj.scalar(act)
            ffn2.scalar_early(act)
            norm2.square(act, 2)
            norm2.deviation(act, 2)
            norm2.round(act, 2)
            ffn2.scalar(act)
            norm3.deviation(act, 1)
            norm3.square(act, 2)
            norm3.deviation(act, 2)

        @block.vector
        def _(dve):
            out_proj.vector(dve)
            ffn2.vector(dve)

        @block.tensor
        def _(pe):
            out_proj.tensor(pe)
            norm2.mean(pe, 2)
            ffn2.tensor(pe)
            norm3.variance(pe, 1)
            norm3.mean(pe, 2)
            norm3.variance(pe, 2)


def shape_constants():
    head = np.arange(HEADS, dtype=np.float64)
    log_g = np.log1p(-np.exp2(-5.0 - head))
    halves = lambda t: np.repeat(t.reshape(PAIRS, 2).T, HD, axis=0)
    idx = np.arange(P)
    tok = np.arange(DEC)
    seq, pos = tok // DEC_SEQ, tok % DEC_SEQ

    def decay_mask(dist, valid):
        e = np.where(valid[None], np.exp(np.where(valid, dist, 0)[None] * log_g[:, None, None]), 0.0) * QSCALE
        return e.reshape(PAIRS, 2, *dist.shape).transpose(2, 1, 0, 3)

    def rows(a):
        out = np.zeros((P, *a.shape[1:]))
        out[:a.shape[0]] = a
        return out

    dist = idx[None, :] - idx[:, None]
    dist_dec = pos[None, :] - pos[:, None]
    same = seq[None, :] == seq[:, None]
    slopes = np.exp2(-8.0 / HEADS * np.arange(1, HEADS + 1))
    back = idx[:, None] + P - np.arange(2 * P)[None, :]
    bias = np.where((back >= 0) & (back <= WINDOW), -slopes.reshape(KVH, GROUP, 1, 1) * back, MASKED)
    s4, t4, i8 = (v.reshape(-1) for v in np.meshgrid(np.arange(4), np.arange(GROUP), np.arange(DEC_SEQ), indexing="ij"))
    cached = i8[:, None] + WINDOW - np.arange(WINDOW)[None, :]
    bias_dec = np.empty((P, KVH, 2, P + DEC))
    for h in range(KVH):
        for half in range(2):
            sl = slopes[GROUP * h + t4][:, None]
            new = i8[:, None] - pos[None, :]
            mine = (4 * half + s4)[:, None] == seq[None, :]
            bias_dec[:, h, half, :WINDOW] = np.where(cached <= WINDOW, -sl * cached, MASKED)
            bias_dec[:, h, half, WINDOW:] = np.where(mine & (new >= 0), -sl * new, MASKED)
    gn_sum = np.zeros((P, PAIRS, HEADS))
    gn_spread = np.zeros((HEADS, PAIRS, P))
    for t in range(PAIRS):
        for h in range(2):
            gn_sum[HD * h:HD * h + HD, t, 2 * t + h] = 1.0 / HD
            gn_spread[2 * t + h, t, HD * h:HD * h + HD] = 1.0
    small = {
        "g_chunk": halves(np.exp(P * log_g)),
        "g_dec": halves(np.exp(DEC_SEQ * log_g)),
        "k_decay": np.exp((P - 1.0 - idx)[:, None] * log_g) * QSCALE,
        "k_decay_dec": rows(np.exp((DEC_SEQ - 1.0 - pos)[:, None] * log_g) * QSCALE),
        "ident": np.eye(P),
    }
    q_exp = lambda p: np.exp((p + 1.0)[None, :] * log_g[:, None])
    q_tab = lambda p: np.repeat(q_exp(p).reshape(PAIRS, 2, -1).transpose(1, 0, 2), HD, axis=0)
    tables = {
        "mask": decay_mask(dist, dist >= 0),
        "mask_dec": rows(decay_mask(dist_dec, same & (dist_dec >= 0))),
        "q_decay": q_tab(idx),
        "q_decay_dec": q_tab(pos),
        "own": rows((seq[:, None] == np.arange(DEC_BATCH)[None, :]).astype(np.float64)),
        "bias": bias.transpose(2, 0, 1, 3),
        "bias_dec": bias_dec,
        "gn_sum": gn_sum,
        "gn_spread": gn_spread,
    }
    f = lambda d: {k: np.ascontiguousarray(v, dtype=np.float32) for k, v in d.items()}
    return f(small), f(tables)


def kernel(x_prompt, x_sample, state_ret, cache_swa_k, cache_swa_v, ln_gain, ln_bias, w_in, ret_gn_w,
           swa_sinks, w_out, ffn1_gate, ffn1_up, ffn1_down, ffn2_gate, ffn2_up, ffn2_down):
    import concourse.bacc as bacc
    from concourse.bass_utils import run_bass_kernel_spmd

    arr = np.asarray
    small_c, tables = shape_constants()

    def by_feature(v):
        return arr(v).reshape(-1, P).T

    def lhs_tiles(w):
        w = arr(w)
        return w.reshape(KT, P, -1, P).transpose(2, 1, 0, 3).reshape(-1, P, D_MODEL)

    def ffn(gate, up, down):
        return np.stack([lhs_tiles(gate[0]), lhs_tiles(up[0]), arr(down[0]).reshape(FT, P, D_MODEL)], axis=2)

    x = np.concatenate([arr(x_prompt)[0], arr(x_sample).reshape(DEC, D_MODEL)], axis=0)
    w = arr(w_in)[0]
    R = HEADS * HD
    ret = lhs_tiles(w[:, :4 * R]).reshape(4, PAIRS, P, D_MODEL).transpose(1, 0, 2, 3).reshape(4 * PAIRS, P, D_MODEL)
    att_q = w[:, 4 * R:5 * R].reshape(D_MODEL, KVH, GROUP, HD).transpose(0, 2, 1, 3).reshape(D_MODEL, R)
    att = np.concatenate([lhs_tiles(att_q), lhs_tiles(w[:, 5 * R:])], axis=0)
    wo = arr(w_out)[0]
    wo_att = wo[R:].reshape(KVH, GROUP, HD, D_MODEL).transpose(1, 0, 2, 3).reshape(R, D_MODEL)
    sinks = arr(swa_sinks)[0]
    sinks_dec = np.broadcast_to(sinks.reshape(KVH, 1, GROUP, 1), (KVH, 4, GROUP, DEC_SEQ)).reshape(KVH, P).T
    small = {
        **small_c,
        "ln_gain": by_feature(arr(ln_gain)[0]), "ln_bias": by_feature(arr(ln_bias)[0]),
        "gn_w": by_feature(arr(ret_gn_w)[0]),
        "sinks": np.broadcast_to(sinks, (P, HEADS)), "sinks_dec": sinks_dec,
    }
    ins = {
        "x": x.T.reshape(KT, P, TOK).transpose(1, 0, 2),
        "small": np.concatenate([small[n] for n in SMALL], axis=1),
        "ffn1": ffn(ffn1_gate, ffn1_up, ffn1_down),
        "ffn2": ffn(ffn2_gate, ffn2_up, ffn2_down),
        "w_ret": ret,
        "w_att": att,
        "w_out": lhs_tiles(np.concatenate([wo[:R], wo_att], axis=0)),
        "state": arr(state_ret)[0].reshape(DEC_BATCH, PAIRS, 2, HD, HD).transpose(2, 3, 1, 0, 4)
                 .reshape(P, PAIRS, DEC_BATCH, HD),
        "k_cache": arr(cache_swa_k)[0].transpose(2, 3, 0, 1).reshape(P, DEC_BATCH, WINDOW),
        "v_cache": arr(cache_swa_v)[0].transpose(1, 0, 2, 3).reshape(WINDOW, DEC_BATCH, P),
        **tables,
    }
    outs = {
        "y": (P, KT, TOK),
        "state_prompt": (P, PAIRS, HD),
        "state_dec": (P, PAIRS, DEC_BATCH, HD),
        "k_prompt": (P, WINDOW), "v_prompt": (WINDOW, P),
        "k_dec": (P, DEC_BATCH, WINDOW), "v_dec": (DEC_BATCH, WINDOW, P),
    }
    nc = bacc.Bacc("TRN2", target_bir_lowering=False, num_devices=1)
    i = {n: nc.dram_tensor(n + "_in", a.shape, F32, kind="ExternalInput").ap() for n, a in ins.items()}
    o = {n: nc.dram_tensor(n + "_out", s, F32, kind="ExternalOutput").ap() for n, s in outs.items()}
    decoder_layer_kernel(nc, i, o)
    got = run_bass_kernel_spmd(nc, [{n + "_in": np.ascontiguousarray(a) for n, a in ins.items()}],
                               core_ids=[0]).results[0]
    got = {n: got[n + "_out"] for n in outs}

    y = got["y"].transpose(2, 1, 0).reshape(TOK, D_MODEL)
    state_p = got["state_prompt"].reshape(2, HD, PAIRS, HD).transpose(2, 0, 1, 3)
    state_d = got["state_dec"].reshape(2, HD, PAIRS, DEC_BATCH, HD).transpose(3, 2, 0, 1, 4)
    k_p = got["k_prompt"].reshape(KVH, HD, WINDOW).transpose(2, 0, 1)
    k_d = got["k_dec"].reshape(KVH, HD, DEC_BATCH, WINDOW).transpose(2, 3, 0, 1)
    return (
        y[:SEQ].reshape(1, SEQ, D_MODEL), y[SEQ:].reshape(DEC_BATCH, DEC_SEQ, D_MODEL),
        state_p.reshape(1, 1, HEADS, HD, HD), k_p.reshape(1, 1, WINDOW, KVH, HD),
        got["v_prompt"].reshape(1, 1, WINDOW, KVH, HD),
        state_d.reshape(1, DEC_BATCH, HEADS, HD, HD), k_d.reshape(1, DEC_BATCH, WINDOW, KVH, HD),
        got["v_dec"].reshape(1, DEC_BATCH, WINDOW, KVH, HD),
    )
```
